# Optimizing a Trainium2 kernel written in Bass

```python
import jax, jax.numpy as jnp
from jax import lax
import numpy as np

D_MODEL = 1024
BATCH = 1
SEQ = 512
DEPTH = 2
DEC_BATCH = 8
DEC_SEQ = 1
PAST_LEN = 256
PAGE_SIZE = 128

HEAD_DIM = 64
A_WIDTH = D_MODEL // 2
A_HEADS = A_WIDTH // HEAD_DIM
A_KV_HEADS = A_HEADS // 4
KV_WIDTH = A_KV_HEADS * HEAD_DIM
CMP_BLOCK = 32
CMP_STRIDE = CMP_BLOCK // 2
SEL_BLOCK = 64
SEL_TOP = 16
WINDOW = 512
FORCE_SCORE = 1.0e4
ROT_DIM = HEAD_DIM // 4
ROPE_THETA = 500000.0
B_WIDTH = D_MODEL // 4
CONV_W = 31
C_WIDTH = D_MODEL // 4
C_HEADS = C_WIDTH // HEAD_DIM
LORA_W = 32
LORA_A = 32
LORA_G = 64
RW_SPLITS = (C_WIDTH, C_WIDTH, C_WIDTH, LORA_W, LORA_A, LORA_G)
RW_COLS = sum(RW_SPLITS)
IN_SPLITS = (A_WIDTH,) + (KV_WIDTH,) * 6 + (3 * A_HEADS, B_WIDTH, B_WIDTH, RW_COLS)
IN_COLS = sum(IN_SPLITS)
D_FF = 11 * D_MODEL // 4
RMS_EPS = 1e-6
LN_EPS = 1e-5
GN_EPS = 64e-5

kernel_name = 'nsa_conv_rwkv7_hybrid_step'

def split_cols(x, sizes):
    cuts = [int(c) for c in np.cumsum(sizes)[:-1]]
    return jnp.split(x, cuts, axis=-1)

def rms_norm(x, g):
    xf = x.astype(jnp.float32)
    y = xf * lax.rsqrt(jnp.mean(xf * xf, axis=-1, keepdims=True) + RMS_EPS)
    return (y * g.astype(jnp.float32)).astype(x.dtype)

def layer_norm(x, g, b, eps):
    xf = x.astype(jnp.float32)
    mu = jnp.mean(xf, axis=-1, keepdims=True)
    var = jnp.mean(jnp.square(xf - mu), axis=-1, keepdims=True)
    return (xf - mu) * lax.rsqrt(var + eps) * g.astype(jnp.float32) + b.astype(jnp.float32)

def swiglu(x, wg, wu, wd):
    return (jax.nn.silu(x @ wg) * (x @ wu)) @ wd

def masked_softmax(s, mask):
    s = jnp.where(mask, s.astype(jnp.float32), -1e30)
    m = jnp.max(s, axis=-1, keepdims=True)
    e = jnp.where(mask, jnp.exp(s - m), 0.0)
    d = jnp.sum(e, axis=-1, keepdims=True)
    return e / jnp.maximum(d, 1e-30)

def rope_partial(x, pos):
    half = ROT_DIM // 2
    inv = ROPE_THETA ** (-jnp.arange(half, dtype=jnp.float32) * 2.0 / ROT_DIM)
    ang = pos.astype(jnp.float32)[:, None] * inv[None, :]
    cos = jnp.cos(ang)[None, :, None, :]
    sin = jnp.sin(ang)[None, :, None, :]
    x1 = x[..., :half].astype(jnp.float32)
    x2 = x[..., half:ROT_DIM].astype(jnp.float32)
    out = jnp.concatenate([x1 * cos - x2 * sin, x2 * cos + x1 * sin, x[..., ROT_DIM:].astype(jnp.float32)], axis=-1)
    return out.astype(x.dtype)

def compress(x, pe, w):
    B, L, G, Dh = x.shape
    n_cmp = (L - CMP_BLOCK) // CMP_STRIDE + 1
    c = x[:, :(n_cmp + 1) * CMP_STRIDE].reshape(B, n_cmp + 1, CMP_STRIDE, G, Dh)
    blk = jnp.concatenate([c[:, :-1], c[:, 1:]], axis=2) + pe[:, None, :]
    return jnp.einsum('bnlgd,lde->bnge', blk, w.reshape(CMP_BLOCK, Dh, Dh))

def sel_blocks(x):
    B, L, G, Dh = x.shape
    n_sel = -(-L // SEL_BLOCK)
    x = jnp.pad(x, ((0, 0), (0, n_sel * SEL_BLOCK - L), (0, 0), (0, 0)))
    return x.reshape(B, n_sel, SEL_BLOCK, G, Dh).transpose(0, 3, 1, 2, 4).reshape(B, G, n_sel, SEL_BLOCK * Dh)

def nsa_attention(q, q_rot, k_cmp, v_cmp, k_sel, v_sel, k_win, v_win, gates, pos0, win_pos0, cmp_pe, cmp_w):
    B, T, H, Dh = q.shape
    L, G = k_cmp.shape[1], k_cmp.shape[2]
    HPG = H // G
    scale = Dh ** -0.5
    q_c5 = q.reshape(B, T, G, HPG, Dh)
    q_r5 = q_rot.reshape(B, T, G, HPG, Dh)
    kc = compress(k_cmp, cmp_pe[0], cmp_w[0])
    vc = compress(v_cmp, cmp_pe[1], cmp_w[1])
    n_cmp = kc.shape[1]
    cmp_end = jnp.arange(n_cmp) * CMP_STRIDE + CMP_BLOCK - 1
    n_sel = -(-L // SEL_BLOCK)
    n_top = min(SEL_TOP, n_sel)
    ci = jnp.arange(n_cmp)[:, None] * CMP_STRIDE
    sj = jnp.arange(n_sel)[None, :] * SEL_BLOCK
    overlap = ((ci < sj + SEL_BLOCK) & (ci + CMP_BLOCK > sj)).astype(jnp.float32)
    ksb = sel_blocks(k_sel)
    vsb = sel_blocks(v_sel)
    kw_pad = jnp.pad(k_win, ((0, 0), (WINDOW, 0), (0, 0), (0, 0)))
    vw_pad = jnp.pad(v_win, ((0, 0), (WINDOW, 0), (0, 0), (0, 0)))
    QB = 128 if T % 128 == 0 else T
    blk_id = jnp.arange(n_sel)
    bi = jnp.arange(B)[:, None, None]
    gi = jnp.arange(G)[None, :, None]

    def block(i):
        lo = i * QB
        p0 = pos0 + lo
        t = p0 + jnp.arange(QB)
        qc = lax.dynamic_slice_in_dim(q_c5, lo, QB, 1)
        qr = lax.dynamic_slice_in_dim(q_r5, lo, QB, 1)
        g = jax.nn.sigmoid(lax.dynamic_slice_in_dim(gates, lo, QB, 1).astype(jnp.float32))
        s = jnp.einsum('bqghd,bngd->bghqn', qc, kc) * scale
        p_cmp = masked_softmax(s, cmp_end[None, :] <= t[:, None])
        o_cmp = jnp.einsum('bghqn,bngd->bqghd', p_cmp.astype(vc.dtype), vc)
        imp = jnp.einsum('bghqn,nj->bgqj', p_cmp, overlap)
        cur = t // SEL_BLOCK
        valid = blk_id[None, :] <= cur[:, None]
        forced = (blk_id[None, :] == 0) | (blk_id[None, :] == cur[:, None]) | (blk_id[None, :] == cur[:, None] - 1)
        score = jnp.where(valid, jnp.where(forced, FORCE_SCORE, imp), -1.0)
        _, idx = lax.top_k(score, n_top)
        flat = idx.reshape(B, G, QB * n_top)
        kg = ksb[bi, gi, flat].reshape(B, G, QB, n_top, SEL_BLOCK, Dh)
        vg = vsb[bi, gi, flat].reshape(B, G, QB, n_top, SEL_BLOCK, Dh)
        kpos = idx[..., None] * SEL_BLOCK + jnp.arange(SEL_BLOCK)
        m_sel = (kpos <= t[None, None, :, None, None]).reshape(B, G, 1, QB, n_top * SEL_BLOCK)
        s = jnp.einsum('bqghd,bgqkld->bghqkl', qr, kg) * scale
        p = masked_softmax(s.reshape(B, G, HPG, QB, n_top * SEL_BLOCK), m_sel).reshape(s.shape)
        o_sel = jnp.einsum('bghqkl,bgqkld->bqghd', p.astype(vg.dtype), vg)
        kwb = lax.dynamic_slice_in_dim(kw_pad, p0 - win_pos0, WINDOW + QB, 1)
        vwb = lax.dynamic_slice_in_dim(vw_pad, p0 - win_pos0, WINDOW + QB, 1)
        kp = p0 - WINDOW + jnp.arange(WINDOW + QB)
        m_win = (kp[None, :] >= win_pos0) & (kp[None, :] >= t[:, None] - WINDOW) & (kp[None, :] <= t[:, None])
        s = jnp.einsum('bqghd,bkgd->bghqk', qr, kwb) * scale
        p = masked_softmax(s, m_win)
        o_win = jnp.einsum('bghqk,bkgd->bqghd', p.astype(vwb.dtype), vwb)
        o = (g[..., 0:1] * o_cmp.reshape(B, QB, H, Dh) + g[..., 1:2] * o_sel.reshape(B, QB, H, Dh)
             + g[..., 2:3] * o_win.reshape(B, QB, H, Dh))
        return o.reshape(B, QB, H * Dh).astype(q.dtype)

    out = lax.map(block, jnp.arange(T // QB))
    return out.transpose(1, 0, 2, 3).reshape(B, T, H * Dh)

def conv_mixer(cv, cg, buf, p):
    u = cv * jax.nn.sigmoid(cg)
    u_all = jnp.concatenate([buf, u], axis=1)
    c = lax.conv_general_dilated(u_all, p['conv_w'][:, None, :], (1,), 'VALID',
                                 dimension_numbers=('NWC', 'WIO', 'NWC'),
                                 feature_group_count=B_WIDTH) + p['conv_b']
    c = jax.nn.silu(layer_norm(c, p['conv_ln_g'], p['conv_ln_b'], LN_EPS)).astype(u.dtype)
    return c @ p['conv_pw'] + p['conv_pw_b'], u_all[:, -(CONV_W - 1):]

def wkv7_step(S, inp):
    r, w, k, v, kk, a = inp
    sk = jnp.einsum('bhvk,bhk->bhv', S, -kk)
    S = S * w[:, :, None, :] + sk[..., None] * (kk * a)[:, :, None, :] + v[..., None] * k[:, :, None, :]
    return S, jnp.einsum('bhvk,bhk->bhv', S, r)

def rwkv7_mixer(rw, shift_prev, s0, p):
    B, T, _ = rw.shape
    f32 = jnp.float32
    prev = jnp.concatenate([shift_prev[:, None], rw[:, :-1]], axis=1)
    xm = rw + (prev - rw) * p['rw_mu']
    r, k, v, wd, ad, gd = split_cols(xm, RW_SPLITS)
    w_log = -jax.nn.softplus(-(p['rw_w0'] + jnp.tanh(wd) @ p['rw_w2']).astype(f32)) - 0.5
    decay = jnp.exp(-jnp.exp(w_log))
    a = jax.nn.sigmoid((p['rw_a0'] + ad @ p['rw_a2']).astype(f32))
    gate = (jax.nn.sigmoid(gd) @ p['rw_g2']).astype(f32)
    hd = lambda z: z.astype(f32).reshape(B, T, C_HEADS, HEAD_DIM)
    hv = lambda z: z.astype(f32).reshape(C_HEADS, HEAD_DIM)
    r, k, v, decay, a = hd(r), hd(k), hd(v), hd(decay), hd(a)
    kk = k * hv(p['rw_kk'])
    kk = kk / jnp.maximum(jnp.sqrt(jnp.sum(kk * kk, axis=-1, keepdims=True)), 1e-12)
    k = k * (1.0 + (a - 1.0) * hv(p['rw_ka']))
    xs = tuple(z.transpose(1, 0, 2, 3) for z in (r, decay, k, v, kk, a))
    s_fin, o = lax.scan(wkv7_step, s0.astype(f32), xs)
    o = o.transpose(1, 0, 2, 3)
    o = layer_norm(o, hv(p['rw_ln_w']), hv(p['rw_ln_b']), GN_EPS)
    o = o + jnp.sum(r * k * p['rw_rk'].astype(f32), axis=-1, keepdims=True) * v
    o = o.reshape(B, T, C_WIDTH) * gate
    return o.astype(rw.dtype), rw[:, -1], s_fin

def token_mix(xn, pos0, past, p):
    B, T, _ = xn.shape
    q, kc, vc, ks, vs, kw, vw, gt, cv, cg, rw = split_cols(xn @ p['w_in'], IN_SPLITS)
    pos = pos0 + jnp.arange(T)
    kv = lambda z: z.reshape(B, T, A_KV_HEADS, HEAD_DIM)
    q = q.reshape(B, T, A_HEADS, HEAD_DIM)
    q_rot = rope_partial(q, pos)
    kc, vc, vs, vw = kv(kc), kv(vc), kv(vs), kv(vw)
    ks, kw = rope_partial(kv(ks), pos), rope_partial(kv(kw), pos)
    if past is None:
        ctx = (kc, vc, ks, vs)
        kw_all, vw_all = kw, vw
        n_buf = min(WINDOW, T)
        conv_buf = jnp.zeros((B, CONV_W - 1, B_WIDTH), xn.dtype)
        shift_prev = jnp.zeros((B, RW_COLS), xn.dtype)
        s0 = jnp.zeros((B, C_HEADS, HEAD_DIM, HEAD_DIM), jnp.float32)
    else:
        ctx = (jnp.concatenate([past['cmp_k'], kc], axis=1), jnp.concatenate([past['cmp_v'], vc], axis=1),
               jnp.concatenate([past['sel_k'], ks], axis=1), jnp.concatenate([past['sel_v'], vs], axis=1))
        kw_all = jnp.concatenate([past['win_k'], kw], axis=1)
        vw_all = jnp.concatenate([past['win_v'], vw], axis=1)
        n_buf = past['win_k'].shape[1]
        conv_buf, shift_prev, s0 = past['conv'], past['shift'], past['wkv']
    win_pos0 = pos0 + T - kw_all.shape[1]
    o_a = nsa_attention(q, q_rot, ctx[0], ctx[1], ctx[2], ctx[3], kw_all, vw_all,
                        gt.reshape(B, T, A_HEADS, 3), pos0, win_pos0, p['cmp_pe'], p['cmp_w'])
    o_b, conv_new = conv_mixer(cv, cg, conv_buf, p)
    o_c, shift_new, s_new = rwkv7_mixer(rw, shift_prev, s0, p)
    gn = p['grp_norm']
    merged = jnp.concatenate([rms_norm(o_a, gn[:A_WIDTH]),
                              rms_norm(o_b, gn[A_WIDTH:A_WIDTH + B_WIDTH]),
                              rms_norm(o_c, gn[A_WIDTH + B_WIDTH:])], axis=-1)
    new = dict(cmp_k=kc, cmp_v=vc, sel_k=ks, sel_v=vs,
               win_k=kw_all[:, -n_buf:], win_v=vw_all[:, -n_buf:],
               conv=conv_new, shift=shift_new, wkv=s_new.astype(xn.dtype))
    return merged @ p['w_out'], new

def trunk(x, pos0, past_fn, W):
    h = x
    states = []
    for l in range(DEPTH):
        p = {n: a[l] for n, a in W.items()}
        nr = p['norms']
        h = h + 0.5 * rms_norm(swiglu(rms_norm(h, nr[0]), p['ffn_gate'][0], p['ffn_up'][0], p['ffn_down'][0]), nr[1])
        m, st = token_mix(rms_norm(h, nr[2]), pos0, None if past_fn is None else past_fn(l), p)
        h = h + rms_norm(m, nr[3])
        h = h + 0.5 * rms_norm(swiglu(rms_norm(h, nr[4]), p['ffn_gate'][1], p['ffn_up'][1], p['ffn_down'][1]), nr[5])
        states.append(st)
    stacked = {k: jnp.stack([s[k] for s in states]) for k in states[0]}
    return h, stacked

def setup_inputs(seed: int = 0) -> dict:
    key = jax.random.key(seed)
    ks = iter(jax.random.split(key, 48))
    nrm = lambda shape, s: jax.random.normal(next(ks), shape, jnp.float32) * s
    gain = lambda shape: 1.0 + nrm(shape, 0.05)
    n_pages = PAST_LEN // PAGE_SIZE
    n_used = DEC_BATCH * n_pages
    n_pool = n_used + max(1, n_used // 4)
    win_buf = min(WINDOW, PAST_LEN)
    pool = (DEPTH, n_pool, PAGE_SIZE, A_KV_HEADS, HEAD_DIM)
    page_table = jax.random.permutation(next(ks), n_pool)[:n_used].reshape(DEC_BATCH, n_pages).astype(jnp.int32)
    return {
        'x_prompt': nrm((BATCH, SEQ, D_MODEL), 1.0),
        'x_sample': nrm((DEC_BATCH, DEC_SEQ, D_MODEL), 1.0),
        'cache_cmp_k': nrm(pool, 1.0),
        'cache_cmp_v': nrm(pool, 1.0),
        'cache_sel_k': nrm(pool, 1.0),
        'cache_sel_v': nrm(pool, 1.0),
        'cache_win_k': nrm((DEPTH, DEC_BATCH, win_buf, A_KV_HEADS, HEAD_DIM), 1.0),
        'cache_win_v': nrm((DEPTH, DEC_BATCH, win_buf, A_KV_HEADS, HEAD_DIM), 1.0),
        'state_conv': nrm((DEPTH, DEC_BATCH, CONV_W - 1, B_WIDTH), 0.5),
        'state_shift': nrm((DEPTH, DEC_BATCH, RW_COLS), 1.0),
        'state_wkv': nrm((DEPTH, DEC_BATCH, C_HEADS, HEAD_DIM, HEAD_DIM), 0.1),
        'page_table': page_table,
        'w_in': nrm((DEPTH, D_MODEL, IN_COLS), D_MODEL ** -0.5),
        'w_out': nrm((DEPTH, D_MODEL, D_MODEL), D_MODEL ** -0.5),
        'norms': gain((DEPTH, 6, D_MODEL)),
        'grp_norm': gain((DEPTH, D_MODEL)),
        'ffn_gate': nrm((DEPTH, 2, D_MODEL, D_FF), D_MODEL ** -0.5),
        'ffn_up': nrm((DEPTH, 2, D_MODEL, D_FF), D_MODEL ** -0.5),
        'ffn_down': nrm((DEPTH, 2, D_FF, D_MODEL), D_FF ** -0.5),
        'cmp_pe': nrm((DEPTH, 2, CMP_BLOCK, HEAD_DIM), 0.5),
        'cmp_w': nrm((DEPTH, 2, CMP_BLOCK * HEAD_DIM, HEAD_DIM), (CMP_BLOCK * HEAD_DIM) ** -0.5),
        'conv_w': nrm((DEPTH, CONV_W, B_WIDTH), CONV_W ** -0.5),
        'conv_b': nrm((DEPTH, B_WIDTH), 0.01),
        'conv_ln_g': gain((DEPTH, B_WIDTH)),
        'conv_ln_b': nrm((DEPTH, B_WIDTH), 0.01),
        'conv_pw': nrm((DEPTH, B_WIDTH, B_WIDTH), B_WIDTH ** -0.5),
        'conv_pw_b': nrm((DEPTH, B_WIDTH), 0.01),
        'rw_mu': jax.random.uniform(next(ks), (DEPTH, RW_COLS), jnp.float32),
        'rw_w0': jax.random.uniform(next(ks), (DEPTH, C_WIDTH), jnp.float32, -2.0, 1.0),
        'rw_w2': nrm((DEPTH, LORA_W, C_WIDTH), 0.1),
        'rw_a0': nrm((DEPTH, C_WIDTH), 0.5),
        'rw_a2': nrm((DEPTH, LORA_A, C_WIDTH), 0.1),
        'rw_g2': nrm((DEPTH, LORA_G, C_WIDTH), LORA_G ** -0.5),
        'rw_kk': 0.85 + nrm((DEPTH, C_WIDTH), 0.1),
        'rw_ka': gain((DEPTH, C_WIDTH)),
        'rw_rk': nrm((DEPTH, C_HEADS, HEAD_DIM), 0.1),
        'rw_ln_w': gain((DEPTH, C_WIDTH)),
        'rw_ln_b': nrm((DEPTH, C_WIDTH), 0.01),
    }

def reference(x_prompt, x_sample, cache_cmp_k, cache_cmp_v, cache_sel_k, cache_sel_v, cache_win_k, cache_win_v,
              state_conv, state_shift, state_wkv, page_table, w_in, w_out, norms, grp_norm, ffn_gate, ffn_up,
              ffn_down, cmp_pe, cmp_w, conv_w, conv_b, conv_ln_g, conv_ln_b, conv_pw, conv_pw_b, rw_mu, rw_w0,
              rw_w2, rw_a0, rw_a2, rw_g2, rw_kk, rw_ka, rw_rk, rw_ln_w, rw_ln_b):
    W = dict(w_in=w_in, w_out=w_out, norms=norms, grp_norm=grp_norm, ffn_gate=ffn_gate, ffn_up=ffn_up,
             ffn_down=ffn_down, cmp_pe=cmp_pe, cmp_w=cmp_w, conv_w=conv_w, conv_b=conv_b, conv_ln_g=conv_ln_g,
             conv_ln_b=conv_ln_b, conv_pw=conv_pw, conv_pw_b=conv_pw_b, rw_mu=rw_mu, rw_w0=rw_w0, rw_w2=rw_w2,
             rw_a0=rw_a0, rw_a2=rw_a2, rw_g2=rw_g2, rw_kk=rw_kk, rw_ka=rw_ka, rw_rk=rw_rk, rw_ln_w=rw_ln_w,
             rw_ln_b=rw_ln_b)
    y_prompt, sp = trunk(x_prompt, 0, None, W)
    past_len = page_table.shape[1] * cache_cmp_k.shape[2]
    n_dec = x_sample.shape[0]

    def past_fn(l):
        def paged(c):
            return c[l][page_table].reshape(n_dec, past_len, A_KV_HEADS, HEAD_DIM)
        return dict(cmp_k=paged(cache_cmp_k), cmp_v=paged(cache_cmp_v),
                    sel_k=paged(cache_sel_k), sel_v=paged(cache_sel_v),
                    win_k=cache_win_k[l], win_v=cache_win_v[l],
                    conv=state_conv[l], shift=state_shift[l], wkv=state_wkv[l])

    y_sample, ss = trunk(x_sample, past_len, past_fn, W)
    return (y_prompt, y_sample,
            sp['cmp_k'], sp['cmp_v'], sp['sel_k'], sp['sel_v'], sp['win_k'], sp['win_v'],
            sp['conv'], sp['shift'], sp['wkv'],
            ss['cmp_k'], ss['cmp_v'], ss['sel_k'], ss['sel_v'], ss['win_k'], ss['win_v'],
            ss['conv'], ss['shift'], ss['wkv'])


_drawn_inputs = setup_inputs


def setup_inputs(seed=0):
    import zlib

    import numpy as np

    out = dict(_drawn_inputs(seed))
    spreads = {}
    factors = {'conv_b': 5.354, 'conv_ln_b': 8.0, 'conv_pw_b': 6.625, 'rw_ln_b': 8.0}
    for name, (base, spread) in spreads.items():
        noise = np.random.default_rng([zlib.crc32(name.encode()), seed]).standard_normal(out[name].shape)
        drawn = base * np.exp(spread * noise) if base else spread * noise
        out[name] = __import__('jax').numpy.asarray(drawn.astype(out[name].dtype))
    for name, factor in factors.items():
        out[name] = (out[name] * factor).astype(out[name].dtype)
    return out
```

```python
from contextlib import ExitStack

import concourse.bass as bass
from concourse import mybir
import numpy as np

F32 = mybir.dt.float32
I32 = mybir.dt.int32
ALU = mybir.AluOpType
ACT = mybir.ActivationFunctionType
X = mybir.AxisListType.X

P = 128
DEPTH, D, SEQ, DEC = 2, 1024, 512, 8
TOK = SEQ + DEC
HALF = TOK // 2
KC = D // P
DFF = 2816
FC = DFF // P
HD = 64
NQ, NKV = 8, 2
QT = SEQ // P
PAST, PAGE = 256, 128
NPAGE = PAST // PAGE
CTX = PAST + 1
CB, CS = 32, 16
NCMP = (SEQ - CB) // CS + 1
NCMP_D = (CTX - CB) // CS + 1
XCOLS = SEQ + DEC * PAST
NWIN = (XCOLS + CB - CB) // CS + 1
CW = 31
CH = 64
NCH = SEQ // CH
RWC = 896
COL_ROWS = 512
N_ROWS = 6 * P + 3 * NQ
COL_T = COL_ROWS + N_ROWS
NEG = -1e30
SCALE = HD ** -0.5
RMS_EPS, LN_EPS, GN_EPS = 1e-6, 1e-5, 64e-5

C_ID, C_ONES, C_BONES, C_ROT, C_CAUS, C_CMPM, C_DMASK, C_LVL, C_LT1, C_STR, C_INC, C_COS, C_SIN, C_EPS, C_END = (
    int(v) for v in np.cumsum([0, 128, 128, 128, 128, 128, QT * NCMP, DEC, 6 * 128, 128, 128, 128, 40, 40, 8]))


def constants():
    c = np.zeros((P, C_END), np.float32)
    i = np.arange(P)
    c[:, C_ID:C_ID + P] = np.eye(P)
    c[:, C_ONES:C_ONES + P] = 1
    same = i[:, None] // 64 == i[None, :] // 64
    c[:, C_BONES:C_BONES + P] = same
    rot = np.zeros((P, P), np.float32)
    for b in (0, 64):
        for e in range(8):
            rot[b + 8 + e, b + e] = -1
            rot[b + e, b + 8 + e] = 1
    c[:, C_ROT:C_ROT + P] = rot
    c[:, C_CAUS:C_CAUS + P] = np.where(i[None, :] <= i[:, None], 0, NEG)
    end = np.arange(NCMP) * CS + CB - 1
    for t in range(QT):
        c[:, C_CMPM + t * NCMP:C_CMPM + (t + 1) * NCMP] = np.where(end[None, :] <= (t * P + i)[:, None], 0, NEG)
    c[:, C_DMASK:C_DMASK + DEC] = np.where(np.arange(DEC)[None, :] == (i // NQ)[:, None], 0, NEG)
    for n in range(6):
        m = 1 << n
        c[:, C_LVL + n * P:C_LVL + (n + 1) * P] = (
            same & (i[:, None] // (2 * m) == i[None, :] // (2 * m))
            & (i[:, None] // m % 2 == 1) & (i[None, :] // m % 2 == 0))
    c[:, C_LT1:C_LT1 + P] = c[:, C_LVL:C_LVL + P].T
    c[:, C_STR:C_STR + P] = same & (i[:, None] < i[None, :])
    c[:, C_INC:C_INC + P] = same & (i[:, None] <= i[None, :])
    inv = np.float32(500000.0) ** (-np.arange(8, dtype=np.float32) * np.float32(2.0) / np.float32(16))
    pos = np.arange(5 * P, dtype=np.float32)
    pos[SEQ:] = PAST
    ang = (pos[:, None] * inv[None, :].astype(np.float32)).astype(np.float32)
    c[:, C_COS:C_COS + 40] = np.cos(ang).reshape(5, P, 8).transpose(1, 0, 2).reshape(P, 40)
    c[:, C_SIN:C_SIN + 40] = np.sin(ang).reshape(5, P, 8).transpose(1, 0, 2).reshape(P, 40)
    c[:, C_EPS:C_EPS + 3] = (RMS_EPS, LN_EPS, GN_EPS)
    rope = np.zeros((P, 2, TOK), np.float32)
    rope[:, 0] = 1
    for b in (0, 64):
        for o in (0, 8):
            rope[b + o:b + o + 8, 0] = np.cos(ang[:TOK]).T
            rope[b + o:b + o + 8, 1] = np.sin(ang[:TOK]).T
    return c, rope


V_NORM, V_GRP, V_CB, V_CLG, V_CLB, V_PWB, V_MU, V_W0, V_A0, V_KK, V_KA, V_RK, V_LW, V_LB = (
    0, 48, 56, 58, 60, 62, 64, 71, 73, 75, 77, 79, 81, 83)
V_END = 85
V_CW = 88


MILESTONES = {
    "dve_stage": ("conv_ready", "kT_ready", "gates_ready", "c_centered", "c_scaled", "ob_ready", "oacc_ready",
                  "on_ready", "oD_ready", "attn_done", "xm_ready", "lora_ready", "kk_raw", "wsig", "sd_new", "dec_o",
                  "chunks_ready", "g_centered", "bonus_in", "oc_ready", "merged_ready"),
    "act_stage": ("state_rows", "gate_exp", "c_act", "oroot", "lora_act", "w_ready"),
    "pool_stage": ("wc_zero", "qz_ready", "mats_zero"),
}


class Tally:

    def __init__(self):
        self.n = {}

    def up(self, name, k=1):
        self.n[name] = self.n.get(name, 0) + k
        return self.n[name]

    def at(self, name):
        return self.n.get(name, 0)


def trunk(nc, a, o):
    es = ExitStack()
    with es:
        def sb(name, shape, dt=F32):
            return es.enter_context(nc.sbuf_tensor(name, shape, dt))

        sems = {}

        def S(name):
            if name not in sems:
                sems[name] = es.enter_context(nc.semaphore(name))
            return sems[name]

        reached = {}

        def stage(name):
            group = next(g for g, names in MILESTONES.items() if name in names)
            return S(group), MILESTONES[group].index(name) + 1

        def reach(name):
            sem, n = stage(name)
            group = next(g for g, names in MILESTONES.items() if name in names)
            assert reached.get(group, 0) == n - 1, f"{name} is out of order"
            reached[group] = n
            return sem

        layer_end = es.enter_context(nc.semaphore("layer_end"))
        fence = es.enter_context(nc.semaphore("fence"))
        layer_go = es.enter_context(nc.semaphore("layer_go"))

        ps = es.enter_context(nc.psum_tensor("ps", [P, 8, 512], F32))
        hT = sb("hT", [P, KC, TOK])
        xnT = sb("xnT", [P, KC, TOK])
        fT = sb("fT", [P, KC * TOK])
        big = sb("big", [P, FC * TOK])
        wup = sb("wup", [P, 2, 2, KC, P])
        win = sb("win", [P, 3, KC, P])
        wdn = sb("wdn", [P, 2 * FC * P])
        mix = sb("mix", [P, 15 * TOK + 4 * TOK])
        cst = sb("cst", [P, C_END])
        vec = sb("vec", [P, 152])
        sq = sb("sq", [P, 2, TOK])
        rstd = sb("rstd", [P, TOK])
        sg = sb("sg", [P, 2, TOK])
        pages = sb("pages", [1, DEC * NPAGE], I32)

        act_v = big[:, :].rearrange("p (f t) -> p f t", t=TOK)
        wdn_v = wdn[:, :].rearrange("p (s k n) -> p s k n", s=2, k=FC)
        f_v = fT[:, :].rearrange("p (c t) -> p c t", t=TOK)
        proj = mix[:, 0:15 * TOK].rearrange("p (c t) -> p c t", t=TOK)
        qrT = mix[:, 15 * TOK:19 * TOK].rearrange("p (c t) -> p c t", t=TOK)
        rows = fT[:, 0:5 * N_ROWS].rearrange("p (i n) -> p i n", n=N_ROWS)
        wrow = big[:, 0:2 * KC * (N_ROWS // 2)].rearrange("p (h k n) -> p h k n", h=2, k=KC)
        ident = cst[:, C_ID:C_ID + P]
        ones = cst[:, C_ONES:C_ONES + P]
        bones = cst[:, C_BONES:C_BONES + P]

        def halves(v):
            return v.rearrange("p (h n) -> p h n", h=2)

        def pair(b):
            return ps[:, b:b + 2, 0:HALF]

        def chain(eng, name, tally):
            def link(ins):
                ins.then_inc(S(name), 1)
                eng.wait_ge(S(name), tally.up(name))
            return link

        block = es.enter_context(nc.Block())

        def boundary(eng, l, tally):
            eng.drain().then_inc(layer_end, 1)
            tally.n.clear()
            if eng is nc.gpsimd:
                eng.wait_ge(layer_end, l * 5 + 5)
                eng.sem_inc(fence, 1)
                for name in sorted(sems):
                    eng.sem_clear(sems[name])
                eng.sem_inc(layer_go, 1)
            else:
                eng.wait_ge(layer_go, l + 1)
                eng.sem_inc(fence, 1)

        def mm_tokens(pe, bank, w, x, first, last):
            for h in range(2):
                ins = pe.matmul(ps[:, bank + h, 0:HALF], w, x[:, h * HALF:(h + 1) * HALF], start=first, stop=last)
            return ins

        def act_prenorm(act, T, n):
            for c in range(KC):
                if n:
                    act.wait_ge(S("h_ready"), T.up("h_ready"))
                if T.up("_sq") > 2:
                    act.wait_ge(S("sq_used"), T.at("_sq") - 2)
                act.activation(sq[:, c % 2, :], hT[:, c, :], ACT.Square).then_inc(S("sq_ready"), 1)
            act_rstd(act, T, RMS_EPS, D)

        def act_rstd(act, T, eps, n, src=None, dst=None):
            col = C_EPS + (RMS_EPS, LN_EPS, GN_EPS).index(eps)
            act.wait_ge(S("sq_used"), T.at("_sq"))
            if T.up("_root") > 1:
                act.wait_ge(S("rstd_used"), T.at("_root") - 1)
            act.activation(halves(rstd[:, :]), pair(6), ACT.Sqrt, scale=1.0 / n,
                           bias=cst[:, col:col + 1]).then_inc(S("root_ready"), 1)

        def pe_sumsq(pe, T, c, last, n=KC, mat=None):
            pe.wait_ge(S("sq_ready"), T.up("sq_ready"))
            if c == 0 and T.up("_ss") > 1:
                pe.wait_ge(S("root_ready"), T.at("_ss") - 1)
            ins = mm_tokens(pe, 6, ones if mat is None else mat, sq[:, (T.at("sq_ready") - 1) % 2, :], c == 0, last)
            ins.then_inc(S("sq_used"), 1)

        def pe_prenorm(pe, T):
            for c in range(KC):
                pe_sumsq(pe, T, c, c == KC - 1)

        def dve_recip(dve, T):
            dve.wait_ge(S("root_ready"), T.up("root_ready"))
            dve.reciprocal(rstd[:, :], rstd[:, :]).then_inc(S("dve_rstd"), 1)
            dve.wait_ge(S("dve_rstd"), T.up("dve_rstd"))

        def dve_prenorm(dve, T, n):
            dve_recip(dve, T)
            for c in range(KC):
                dve.scalar_tensor_tensor(out=xnT[:, c, :], in0=hT[:, c, :],
                                         scalar=vec[:, V_NORM + n * KC + c:V_NORM + n * KC + c + 1],
                                         in1=rstd[:, :], op0=ALU.mult, op1=ALU.mult).then_inc(S("xn_ready"), 1)
            dve.wait_ge(S("xn_ready"), T.up("xn_ready", KC))
            dve.sem_inc(S("rstd_used"), 1)

        def dve_postnorm(dve, T, n):
            dve_recip(dve, T)
            for c in range(KC):
                dve.scalar_tensor_tensor(out=f_v[:, c, :], in0=f_v[:, c, :],
                                         scalar=vec[:, V_NORM + n * KC + c:V_NORM + n * KC + c + 1],
                                         in1=rstd[:, :], op0=ALU.mult, op1=ALU.mult).then_inc(S("fn_ready"), 1)
            for c in range(KC):
                dve.wait_ge(S("fn_ready"), T.up("fn_ready"))
                dve.tensor_tensor(hT[:, c, :], hT[:, c, :], f_v[:, c, :], ALU.add).then_inc(S("h_ready"), 1)
            dve.wait_ge(S("h_ready"), T.up("h_ready", KC))
            dve.sem_inc(S("rstd_used"), 1)

        def sp_ffn(sp, T, l, f):
            base = f * FC

            def load(j, s):
                for n, w in enumerate((a["ffn_gate"], a["ffn_up"])):
                    sp.dma_start(wup[:, s, n], w[bass.ds(l, 1), f, :, bass.ds((j * 2 + s) * P, P)]
                                 .rearrange("a (k p) n -> p (a k) n", p=P)).then_inc(S(f"wup_full{s}"), 16)

            for s in range(2):
                if f:
                    sp.wait_ge(S("gu_ready"), base + s - 1)
                load(0, s)
            with sp.Fori(1, FC // 2) as j:
                for s in range(2):
                    sp.wait_ge(S("gu_ready"), j * 2 + (base + s - 1))
                    sp.sem_inc(S("sp_step"), 1)
                    load(j, s)

        def sp_down(sp, T, l, f):
            for m in range(KC):
                if m >= 2:
                    sp.wait_ge(S("f_ready"), f * 2 * KC + m - 1)
                sp.dma_start(wdn_v[:, m % 2], a["ffn_down"][bass.ds(l, 1), f, :, m * P:(m + 1) * P]
                             .rearrange("a (k p) n -> p (a k) n", p=P)).then_inc(S(f"wdn_full{m % 2}"), 16)

        def pe_ffn(pe, T, f):
            base = f * FC
            pe.wait_ge(S("xn_ready"), T.up("xn_ready", KC))
            with pe.Fori(0, FC // 2) as j:
                for s in range(2):
                    pe.wait_ge(S(f"wup_full{s}"), j * 32 + (f * FC // 2 + 1) * 32)
                    pe.wait_ge(S("gu_used"), j * 2 + (base + s + 1))
                    for n in range(2):
                        for k in range(KC):
                            ins = mm_tokens(pe, 4 * s + 2 * n, wup[:, s, n, k, :], xnT[:, k, :], k == 0, k == KC - 1)
                    ins.then_inc(S("gu_ready"), 1)

        def act_ffn(act, T, f):
            base = f * FC
            with act.Fori(0, FC // 2) as j:
                for s in range(2):
                    act.wait_ge(S("gu_ready"), j * 2 + (base + s + 1))
                    act.activation(halves(sg[:, s, :]), pair(4 * s), ACT.Silu).then_inc(S("sg_ready"), 1)

        def dve_ffn(dve, T, f):
            base = f * FC
            with dve.Fori(0, FC // 2) as j:
                for s in range(2):
                    dve.wait_ge(S("sg_ready"), j * 2 + (base + s + 1))
                    dve.tensor_tensor(act_v[:, bass.ds(j * 2 + s, 1), :].rearrange("p a (h n) -> p (a h) n", h=2),
                                      halves(sg[:, s, :]), pair(4 * s + 2), ALU.mult).then_inc(S("gu_used"), 1)

        def pe_out_chunk(pe, T, m, full, val, w, x, nk):
            pe.wait_ge(full, val)
            pe.wait_ge(S("f_used"), T.up("f_used"))
            for k in range(nk):
                ins = mm_tokens(pe, 2 * (m % 2), w[:, k, :], x[:, k, :], k == 0, k == nk - 1)
            ins.then_inc(S("f_ready"), 1)

        def pe_down(pe, T, f):
            pe.wait_ge(S("gu_used"), (f + 1) * FC + 2)
            for m in range(KC):
                pe_out_chunk(pe, T, m, S(f"wdn_full{m % 2}"), 16 * (f * KC // 2 + m // 2 + 1),
                             wdn_v[:, m % 2], act_v, FC)
                if m:
                    pe_sumsq(pe, T, m - 1, False)
            pe_sumsq(pe, T, KC - 1, True)

        def act_out(act, T):
            for m in range(KC):
                act.wait_ge(S("f_ready"), T.up("f_ready"))
                if T.up("_sq") > 2:
                    act.wait_ge(S("sq_used"), T.at("_sq") - 2)
                act.activation(halves(f_v[:, m, :]), pair(2 * (m % 2)), ACT.Copy).then_inc(S("f_out"), 1)
                act.activation(halves(sq[:, m % 2, :]), pair(2 * (m % 2)), ACT.Square).then_inc(S("sq_ready"), 1)
                act.wait_ge(S("f_out"), T.up("f_out"))
                act.wait_ge(S("sq_ready"), T.at("_sq"))
                act.sem_inc(S("f_used"), 1)
            act_rstd(act, T, RMS_EPS, D)

        xin = big[:, 0:QT * D].rearrange("p (i n) -> p i n", n=D)
        xin_d = big[0:DEC, QT * D:(QT + 1) * D]
        vst = sb("vst", [P, 2, P])

        def sp_first(sp, T):
            sp.dma_start(cst[:, :], a["const"]).then_inc(S("const_in"), 16)
            sp.dma_start(xin, a["x_prompt"].rearrange("b (i p) n -> p (b i) n", p=P)).then_inc(S("x_in"), 16)
            sp.dma_start(xin_d, a["x_sample"].rearrange("b t n -> (b t) n")).then_inc(S("x_in"), 16)
            sp.dma_start(pages[:, :], a["page_table"].rearrange("(o b) n -> o (b n)", o=1)).then_inc(S("page_in"), 16)
            for name, n in (("const_in", 1), ("x_in", 2), ("page_in", 1)):
                sp.wait_ge(S(name), 16 * n)

        def pe_first(pe, T):
            pe.wait_ge(S("const_in"), 16)
            pe.wait_ge(S("x_in"), 32)
            for c in range(KC):
                b = 2 * (c % 2)
                if c >= 2:
                    pe.wait_ge(S("x_rows_out"), c - 1)
                    pe.wait_ge(S("x_dec_out"), c - 1)
                for i in range(QT):
                    pe.transpose(ps[:, b, i * P:(i + 1) * P], xin[:, i, c * P:(c + 1) * P], ident)
                pe.transpose(ps[:, b + 1, 0:DEC], xin_d[:, c * P:(c + 1) * P], ident[0:DEC, 0:DEC]).then_inc(S("x_t"), 1)

        def act_first(act, T):
            for c in range(KC):
                act.wait_ge(S("x_t"), c + 1)
                act.activation(hT[:, c, 0:SEQ], ps[:, 2 * (c % 2), :], ACT.Copy).then_inc(S("x_rows_out"), 1)

        def dve_first(dve, T):
            for c in range(KC):
                dve.wait_ge(S("x_t"), c + 1)
                dve.tensor_copy(hT[:, c, SEQ:TOK], ps[:, 2 * (c % 2) + 1, 0:DEC]).then_inc(S("x_dec_out"), 1)

        def sp_vectors(sp, T, l):
            L = bass.ds(l, 1)

            def put(row, n, src, slot=0):
                sp.dma_start(vst[row:row + n, slot, :], src).then_inc(S("vec_in"), 16)

            put(V_NORM, 6 * KC, a["norms"][L].rearrange("a n (c p) -> (a n c) p", p=P))
            for g in range(2):
                sp.dma_start(vst[V_GRP:V_GRP + 4, 0, g * HD:(g + 1) * HD],
                               a["grp_norm"][L, g * 256:(g + 1) * 256].rearrange("a (t d) -> (a t) d", d=HD))\
                    .then_inc(S("vec_in"), 16)
            put(V_GRP + 4, 4, a["grp_norm"][L, 512:1024].rearrange("a (c p) -> (a c) p", p=P))
            for row, n, name in ((V_CB, 2, "conv_b"), (V_CLG, 2, "conv_ln_g"), (V_CLB, 2, "conv_ln_b"),
                                 (V_PWB, 2, "conv_pw_b"), (V_MU, 7, "rw_mu"), (V_W0, 2, "rw_w0"), (V_A0, 2, "rw_a0"),
                                 (V_KK, 2, "rw_kk"), (V_KA, 2, "rw_ka"), (V_LW, 2, "rw_ln_w"), (V_LB, 2, "rw_ln_b")):
                put(row, n, a[name][L].rearrange("a (c p) -> (a c) p", p=P))
            put(V_RK, 2, a["rw_rk"][L].rearrange("a (c h) d -> (a c) (h d)", c=2))
            put(0, 2 * CW, a["conv_w"][L].rearrange("a j (c p) -> (a j c) p", p=P), slot=1)

        def pe_vectors(pe, T):
            pe.wait_ge(S("vec_in"), 17 * 16)
            pe.transpose(ps[:, 0, 0:V_END], vst[0:V_END, 0, :], ident[0:V_END, 0:V_END])
            pe.transpose(ps[:, 0, V_CW:V_CW + 2 * CW], vst[0:2 * CW, 1, :], ident[0:2 * CW, 0:2 * CW])\
                .then_inc(S("vec_t"), 1)

        def dve_vectors(dve, T, link):
            dve.wait_ge(S("vec_t"), 1)
            link(dve.tensor_copy(vec[:, 0:V_END], ps[:, 0, 0:V_END]))
            link(dve.tensor_copy(vec[:, V_CW:V_CW + 2 * CW], ps[:, 0, V_CW:V_CW + 2 * CW]))
            for n in (1, 5):
                link(dve.tensor_scalar(vec[:, V_NORM + n * KC:V_NORM + (n + 1) * KC],
                                       vec[:, V_NORM + n * KC:V_NORM + (n + 1) * KC], 0.5, None, ALU.mult))

        def pe_last(pe, T):
            for i in range(QT + 1):
                m = P if i < QT else DEC
                if i >= 2:
                    pe.wait_ge(S("y_out"), 2 * i - 2)
                for n in range(2):
                    for c in range(4):
                        ins = pe.transpose(ps[0:m, 2 * (i % 2) + n, c * P:(c + 1) * P],
                                           hT[:, 4 * n + c, i * P:i * P + m], ident)
                    ins.then_inc(S("y_t"), 1)

        def act_last(act, T):
            for i in range(QT + 1):
                m = P if i < QT else DEC
                for n in range(2):
                    act.wait_ge(S("y_t"), 2 * i + n + 1)
                    act.activation(big[0:m, i * D + n * 512:i * D + (n + 1) * 512], ps[0:m, 2 * (i % 2) + n, :],
                                   ACT.Copy).then_inc(S("y_out"), 1)

        def sp_last(sp, T):
            for i in range(QT):
                sp.wait_ge(S("y_out"), 2 * i + 2)
                sp.dma_start(o["y_prompt"][0, i * P:(i + 1) * P, :], big[:, i * D:(i + 1) * D]).then_inc(S("y_st"), 16)
            sp.wait_ge(S("y_out"), 2 * QT + 2)
            sp.dma_start(o["y_sample"].rearrange("b t n -> (b t) n"), big[0:DEC, QT * D:(QT + 1) * D])\
                .then_inc(S("y_st"), 16)
            sp.wait_ge(S("y_st"), 16 * (QT + 1))

        NH2 = N_ROWS // 2
        CO = 2 * KC * NH2
        uP = big[:, CO:CO + 1084].rearrange("p (t n) -> p t n", t=2)
        uD = big[:, CO + 1084:CO + 1580].rearrange("p (t b j) -> p t b j", t=2, b=DEC)
        cT = big[:, CO + 1580:CO + 2620].rearrange("p (t n) -> p t n", t=2)
        cst_in = big[0:120, CO + 2620:CO + 3132].rearrange("p (h n) -> p h n", h=2)
        dtmp = big[:, CO + 3132:CO + 3628].rearrange("p (t b j) -> p t b j", t=2, b=DEC)
        cout = big[:, CO + 3628:CO + 4140]
        srow = big[:, CO + 4140:CO + 4140 + RWC]
        rope = wdn[:, 2592:2592 + 2 * TOK].rearrange("p (s n) -> p s n", s=2)
        pw = sb("pw", [P, 2, 256])
        merged = xnT
        rtq = sq
        rtmp = vst[:, :, :].rearrange("p s (n e) -> p s n e", n=4)
        small = sb("small", [P, 904])

        def sp_win_chunk(sp, l, c):
            for n in range(2):
                if c < 4:
                    sp.dma_start(win[:, c % 3, :, n * HD:(n + 1) * HD],
                                 a["w_in"][bass.ds(l, 1), :, n * 256 + c * HD:n * 256 + (c + 1) * HD]
                                 .rearrange("a (k p) n -> p (a k) n", p=P)).then_inc(S(f"win_full{c % 3}"), 16)
                else:
                    col = COL_T + (c - 4) * P
                    sp.dma_start(win[:, c % 3, 4 * n:4 * n + 4, :],
                                 a["w_in"][bass.ds(l, 1), n * 512:(n + 1) * 512, col:col + P]
                                 .rearrange("a (k p) n -> p (a k) n", p=P)).then_inc(S(f"win_full{c % 3}"), 16)

        def sp_project(sp, T, l):
            L = bass.ds(l, 1)
            sp.wait_ge(S("f_ready"), KC)
            for n in range(2):
                sp.dma_start(cst_in[:, n, :], a["state_conv"][L, 4 * n:4 * n + 4]
                             .rearrange("a b j n -> (a b j) n")).then_inc(S("conv_in"), 16)
            for c in range(3, 6):
                sp.wait_ge(S("p_ready"), c - 2)
                sp_win_chunk(sp, l, c)
            for n in range(2):
                sp.dma_start(wrow[:, n], a["w_in"][L, :, COL_ROWS + n * NH2:COL_ROWS + (n + 1) * NH2]
                             .rearrange("a (k p) n -> p (a k) n", p=P)).then_inc(S("wrow_full"), 16)
            sp.dma_start(rope, a["rope"]).then_inc(S("rope_in"), 16)
            sp.dma_start(pw[:, :, :], a["conv_pw"][L].rearrange("a (k p) n -> p (a k) n", p=P)).then_inc(S("pw_in"), 16)
            for c in range(6, 15):
                sp.wait_ge(S("p_ready"), c - 2)
                sp_win_chunk(sp, l, c)

        def pe_project(pe, T):
            pe.wait_ge(S("xn_ready"), T.up("xn_ready", KC))
            pe.wait_ge(S("conv_in"), 32)
            for n in range(2):
                for t in range(2):
                    for_b = ps[:, 6, t * 240 + n * 120:t * 240 + n * 120 + 120]
                    ins = pe.transpose(for_b, cst_in[:, n, t * P:(t + 1) * P], ident[0:120, 0:120])
            ins.then_inc(S("conv_state_t"), 1)
            with pe.Fori(0, 5) as j:
                for s in range(3):
                    pe.wait_ge(S(f"win_full{s}"), j * 32 + 32)
                    pe.wait_ge(S("p_used"), j * 3 + (s + 1))
                    for k in range(KC):
                        ins = mm_tokens(pe, 2 * s, win[:, s, k, :], xnT[:, k, :], k == 0, k == KC - 1)
                    ins.then_inc(S("p_ready"), 1)
            pe.wait_ge(S("wrow_full"), 32)
            pe.wait_ge(S("conv_state_out"), 1)
            for i in range(QT + 1):
                m = P if i < QT else DEC
                b = 6 if i % 2 == 0 else 0
                if i == 1:
                    pe.wait_ge(S("p_used"), 3 + 13)
                if i >= 2:
                    pe.wait_ge(S("r_used"), i - 1)
                for n in range(2):
                    for k in range(KC):
                        ins = pe.matmul(ps[0:m, b + n, 0:NH2], xnT[:, k, i * P:i * P + m], wrow[:, n, k, :],
                                        start=k == 0, stop=k == KC - 1)
                ins.then_inc(S("r_ready"), 1)
            for t in range(4):
                if t == 0:
                    pe.wait_ge(S("p_used"), 3 + 15)
                if t >= 2:
                    pe.wait_ge(S("rot_used"), t - 1)
                mm_tokens(pe, 2 + 2 * (t % 2), cst[:, C_ROT:C_ROT + P], proj[:, t, :], True, True)\
                    .then_inc(S("rot_ready"), 1)

        def act_project(act, T, link):
            def evac(j):
                for s in range(3):
                    act.wait_ge(S("p_ready"), j * 3 + (s + 1))
                    act.activation(proj[:, bass.ds(j * 3 + s, 1), :].rearrange("p a (h n) -> p (a h) n", h=2),
                                   pair(2 * s), ACT.Copy).then_inc(S("p_used"), 1)
            act.sem_inc(S("p_used"), 3)
            with act.Fori(0, 3) as j:
                evac(j)
            act.wait_ge(S("p_used"), 3 + 9)
            act.activation(sg[:, :, :], proj[:, 6:8, :], ACT.Exp, scale=-1.0).then_inc(S("cg_exp"), 1)
            with act.Fori(3, 5) as j:
                evac(j)
            for i in range(QT + 1):
                m = P if i < QT else DEC
                b = 6 if i % 2 == 0 else 0
                act.wait_ge(S("r_ready"), i + 1)
                act.activation(rows[0:m, i, :].rearrange("p (h n) -> p h n", h=2), ps[0:m, b:b + 2, 0:NH2],
                               ACT.Copy).then_inc(S("r_used"), 1)

        def dve_rope(dve, T, link):
            dve.wait_ge(S("rope_in"), 16)
            for t in range(4):
                dve.wait_ge(S("rot_ready"), t + 1)
                dve.tensor_tensor(halves(qrT[:, t, :]), pair(2 + 2 * (t % 2)), halves(rope[:, 1, :]), ALU.mult)\
                    .then_inc(S("rot_used"), 1)
                dve.wait_ge(S("q_cos"), t + 1)
                dve.wait_ge(S("rot_used"), t + 1)
                dve.tensor_tensor(qrT[:, t, :], qrT[:, t, :], rtq[:, t % 2, :], ALU.add).then_inc(S("qr_ready"), 1)

        def pool_rope(pool, T, link):
            pool.wait_ge(S("rope_in"), 16)
            pool.wait_ge(S("p_used"), 3 + 9)
            for t in range(4):
                if t >= 2:
                    pool.wait_ge(S("qr_ready"), t - 1)
                pool.tensor_tensor(rtq[:, t % 2, :], proj[:, t, :], rope[:, 0, :], ALU.mult).then_inc(S("q_cos"), 1)
            for i in range(QT + 1):
                m = P if i < QT else DEC
                pool.wait_ge(S("r_used"), i + 1)
                kk = rows[0:m, i, 256:768].rearrange("p (s v g d) -> p s v g d", s=2, v=2, g=2)[:, :, 0]
                for s in range(2):
                    lo, hi = kk[:, s, :, 0:8], kk[:, s, :, 8:16]
                    cos = cst[0:m, C_COS + 8 * i:C_COS + 8 * i + 8].unsqueeze(1).broadcast_to((m, 2, 8))
                    sin = cst[0:m, C_SIN + 8 * i:C_SIN + 8 * i + 8].unsqueeze(1).broadcast_to((m, 2, 8))
                    w = [rtmp[0:m, s, n, 0:16].rearrange("p (g d) -> p g d", g=2) for n in range(4)]
                    link(pool.tensor_tensor(w[0], lo, cos, ALU.mult))
                    link(pool.tensor_tensor(w[1], hi, sin, ALU.mult))
                    link(pool.tensor_tensor(w[2], hi, cos, ALU.mult))
                    link(pool.tensor_tensor(w[3], lo, sin, ALU.mult))
                    link(pool.tensor_tensor(lo, w[0], w[1], ALU.subtract))
                    link(pool.tensor_tensor(hi, w[2], w[3], ALU.add))
                pool.sem_inc(S("rows_ready"), 1)

        def sp_rows_out(sp, T, l):
            L = bass.ds(l, 1)
            names = ("cmp_k", "cmp_v", "sel_k", "sel_v", "win_k", "win_v")
            sp.wait_ge(S("rows_ready"), QT + 1)
            for n, name in enumerate(names):
                sp.dma_start(o[f"p_{name}"][L].rearrange("a b (i p) g d -> p (a b i) (g d)", p=P),
                             rows[:, 0:QT, n * P:(n + 1) * P]).then_inc(S("rows_st"), 16)
                if n < 4:
                    dst = o[f"s_{name}"][L].rearrange("a b t g d -> (a b t) (g d)")
                else:
                    dst = o[f"s_{name}"][L, :, PAST - 1].rearrange("a b g d -> (a b) (g d)")
                    src = a[f"cache_{name}"][L, :, 1:PAST].rearrange("a b t g d -> (a b) (t g d)")
                    sp.dma_start(o[f"s_{name}"][L, :, 0:PAST - 1].rearrange("a b t g d -> (a b) (t g d)"), src)\
                        .then_inc(S("rows_st"), 16)
                sp.dma_start(dst, rows[0:DEC, QT, n * P:(n + 1) * P]).then_inc(S("rows_st"), 16)

        def dve_conv(dve, T, link):
            dve.wait_ge(S("conv_state_t"), 1)
            dve.tensor_copy(uD[:, :, :, 0:CW - 1].rearrange("p t b j -> p (t b) j"),
                            ps[:, 6, 0:480].rearrange("p (x j) -> p x j", j=CW - 1)).then_inc(S("conv_state_out"), 1)
            link(dve.memset(uP[:, :, 0:CW - 1], 0.0))
            dve.wait_ge(S("cg_exp"), 1)
            link(dve.tensor_scalar(sg[:, :, :], sg[:, :, :], 1.0, None, ALU.add))
            link(dve.reciprocal(sg[:, :, :], sg[:, :, :]))
            link(dve.tensor_tensor(uP[:, :, CW - 1:CW - 1 + SEQ], proj[:, 4:6, 0:SEQ], sg[:, :, 0:SEQ], ALU.mult))
            dve.tensor_tensor(uD[:, :, :, CW - 1], proj[:, 4:6, SEQ:TOK], sg[:, :, SEQ:TOK], ALU.mult)\
                .then_inc(S("u_ready"), 1)
            dve.wait_ge(S("u_ready"), 1)
            dve.wait_ge(S("conv_state_out"), 1)
            base = T.at("dve_step")
            n = 0
            for j in range(CW):
                for t in range(2):
                    w = vec[:, V_CW + 2 * j + t:V_CW + 2 * j + t + 1]
                    x = uP[:, t, j:j + SEQ]
                    if j == 0:
                        dve.tensor_scalar(cT[:, t, 0:SEQ], x, w, vec[:, V_CB + t:V_CB + t + 1], ALU.mult, ALU.add)\
                            .then_inc(S("dve_step"), 1)
                    else:
                        dve.wait_ge(S("dve_step"), base + n - 1)
                        dve.scalar_tensor_tensor(out=cT[:, t, 0:SEQ], in0=x, scalar=w, in1=cT[:, t, 0:SEQ],
                                                 op0=ALU.mult, op1=ALU.add).then_inc(S("dve_step"), 1)
                    n += 1
            dve.wait_ge(S("dve_step"), T.up("dve_step", n))
            taps = vec[:, V_CW:V_CW + 2 * CW].rearrange("p (j t) -> p t j", t=2).unsqueeze(2)\
                .broadcast_to((P, 2, DEC, CW))
            for t in range(2):
                link(dve.tensor_tensor(dtmp[:, t], uD[:, t], taps[:, t], ALU.mult))
                link(dve.tensor_reduce(cT[:, t, SEQ:TOK], dtmp[:, t], X, ALU.add))
                link(dve.tensor_scalar(cT[:, t, SEQ:TOK], cT[:, t, SEQ:TOK], vec[:, V_CB + t:V_CB + t + 1], None,
                                       ALU.add))
            dve.sem_inc(reach("conv_ready"), 1)

        def pe_conv_state(pe, T):
            pe.wait_ge(S("u_ready"), 1)
            pe.wait_ge(S("r_used"), QT + 1)
            for t in range(2):
                pe.transpose(ps[0:CW - 1, 6, t * P:(t + 1) * P], uP[:, t, SEQ:SEQ + CW - 1], ident)
                ins = pe.transpose(ps[0:DEC, 6, 256 + t * P:256 + (t + 1) * P], uD[:, t, :, CW - 1], ident)
            for t in range(7):
                ins = pe.transpose(ps[0:DEC + 1, 7 if t < 4 else 0, (t % 4) * P:(t % 4 + 1) * P],
                                   proj[:, 8 + t, SEQ - 1:TOK], ident)
            ins.then_inc(S("state_t"), 1)

        def act_conv_state(act, T, link):
            act.wait_ge(S("state_t"), 1)
            act.activation(cout[0:CW - 1, 0:256], ps[0:CW - 1, 6, 0:256], ACT.Copy)
            act.activation(cout[0:DEC, 256:512], ps[0:DEC, 6, 256:512], ACT.Copy)
            act.activation(srow[0:DEC + 1, 0:512], ps[0:DEC + 1, 7, :], ACT.Copy)
            link(act.activation(srow[0:DEC + 1, 512:RWC], ps[0:DEC + 1, 0, 0:RWC - 512], ACT.Copy))
            act.sem_inc(reach("state_rows"), 1)

        def sp_state_out(sp, T, l):
            L = bass.ds(l, 1)
            sp.wait_ge(*stage("state_rows"))
            for dst, src in ((o["p_conv"][L].rearrange("a b j n -> (a b j) n"), cout[0:CW - 1, 0:256]),
                             (o["s_conv"][L, :, CW - 2].rearrange("a b n -> (a b) n"), cout[0:DEC, 256:512]),
                             (o["p_shift"][L].rearrange("a b n -> (a b) n"), srow[0:1, :]),
                             (o["s_shift"][L].rearrange("a b n -> (a b) n"), srow[1:DEC + 1, :]),
                             (o["s_conv"][L, :, 0:CW - 2].rearrange("a b j n -> (a b) (j n)"),
                              a["state_conv"][L, :, 1:CW - 1].rearrange("a b j n -> (a b) (j n)"))):
                sp.dma_start(dst, src).then_inc(S("state_st"), 16)
            sp.wait_ge(S("state_st"), 5 * 16)

        def dve_conv_norm(dve, T, link):
            dve.wait_ge(S("cmean"), 1)
            for t in range(2):
                ins = dve.scalar_tensor_tensor(out=halves(cT[:, t, :]), in0=pair(2), scalar=-1 / 256,
                                               in1=halves(cT[:, t, :]), op0=ALU.mult, op1=ALU.add)
            link(ins)
            dve.sem_inc(reach("c_centered"), 1)
            dve.wait_ge(S("croot"), 1)
            link(dve.reciprocal(rtq[:, 0, :], rtq[:, 0, :]))
            for t in range(2):
                link(dve.scalar_tensor_tensor(out=cT[:, t, :], in0=cT[:, t, :],
                                              scalar=vec[:, V_CLG + t:V_CLG + t + 1], in1=rtq[:, 0, :],
                                              op0=ALU.mult, op1=ALU.mult))
            dve.sem_inc(reach("c_scaled"), 1)
            dve.wait_ge(S("pw_ready"), 1)
            for t in range(2):
                link(dve.tensor_scalar(halves(cT[:, t, :]), pair(2 + 2 * t), vec[:, V_PWB + t:V_PWB + t + 1], None,
                                       ALU.add))
            dve.sem_inc(reach("ob_ready"), 1)
            dve.wait_ge(S("croot"), 2)
            link(dve.reciprocal(rtq[:, 1, :], rtq[:, 1, :]))
            for t in range(2):
                ins = dve.scalar_tensor_tensor(out=merged[:, 4 + t, :], in0=cT[:, t, :],
                                               scalar=vec[:, V_GRP + 4 + t:V_GRP + 5 + t], in1=rtq[:, 1, :],
                                               op0=ALU.mult, op1=ALU.mult)
            link(ins)

        def act_conv_norm(act, T, link):
            act.wait_ge(*stage("c_centered"))
            link(act.activation(sg[:, :, :], cT[:, :, :], ACT.Square))
            act.sem_inc(S("csq"), 1)
            act.wait_ge(S("cvar"), 1)
            act.activation(halves(rtq[:, 0, :]), pair(4), ACT.Sqrt, scale=1 / 256,
                           bias=cst[:, C_EPS + 1:C_EPS + 2]).then_inc(S("croot"), 1)
            act.wait_ge(*stage("c_scaled"))
            for t in range(2):
                ins = act.activation(sg[:, t, :], cT[:, t, :], ACT.Silu, bias=vec[:, V_CLB + t:V_CLB + t + 1])
            link(ins)
            act.sem_inc(reach("c_act"), 1)
            act.wait_ge(*stage("ob_ready"))
            link(act.activation(sg[:, :, :], cT[:, :, :], ACT.Square))
            act.sem_inc(S("csq"), 1)
            act.wait_ge(S("cvar"), 2)
            act.activation(halves(rtq[:, 1, :]), pair(6), ACT.Sqrt, scale=1 / 256,
                           bias=cst[:, C_EPS:C_EPS + 1]).then_inc(S("croot"), 1)

        def pe_conv_norm(pe, T):
            pe.wait_ge(*stage("conv_ready"))
            pe.wait_ge(*stage("kT_ready"))
            pe.wait_ge(S("qr_ready"), 4)
            for t in range(2):
                ins = mm_tokens(pe, 2, ones, cT[:, t, :], t == 0, t == 1)
            ins.then_inc(S("cmean"), 1)
            pe.wait_ge(S("csq"), 1)
            for t in range(2):
                ins = mm_tokens(pe, 4, ones, sg[:, t, :], t == 0, t == 1)
            ins.then_inc(S("cvar"), 1)
            pe.wait_ge(S("pw_in"), 16)
            pe.wait_ge(*stage("c_act"))
            for m in range(2):
                for t in range(2):
                    ins = mm_tokens(pe, 2 + 2 * m, pw[:, t, m * P:(m + 1) * P], sg[:, t, :], t == 0, t == 1)
            ins.then_inc(S("pw_ready"), 1)
            pe.wait_ge(S("csq"), 2)
            pe.wait_ge(*stage("state_rows"))
            for t in range(2):
                ins = mm_tokens(pe, 6, ones, sg[:, t, :], t == 0, t == 1)
            ins.then_inc(S("cvar"), 1)

        xc = wdn[:, 0:XCOLS + CB]
        PT = wdn[:, 2592:4640].rearrange("p (s g n) -> p s g n", s=2, g=2)
        kcmp = wdn[:, 4640:4640 + NWIN]
        vcmp = wdn[:, 4804:4804 + NWIN]
        vcr = wdn[:, 0:P]
        vcd = wdn[:, P:9 * P].rearrange("p (b n) -> p b n", b=DEC)
        qz = [wdn[:, 1152 + 512 * n:1664 + 512 * n].rearrange("p (b m) -> p b m", b=DEC) for n in range(2)]
        wc = big[:, 0:CB * P].rearrange("p (l e) -> p l e", e=P)
        prob = big[:, 4096:6144].rearrange("p (s g n) -> p s g n", s=2, g=2)
        oacc = big[:, 0:QT * 512].rearrange("p (i n) -> p i n", n=512)
        kT = [big[:, 2048 + TOK * n:2048 + TOK * (n + 1)] for n in range(2)]
        otmp = big[:, 3100:3612]
        wup_f = wup[:, :, :, :, :].rearrange("p a b k n -> p (a b k n)")
        page = [wup_f[:, 2048 * n:2048 * (n + 1)].rearrange("p (x n) -> p x n", n=P) for n in range(2)]
        kdT = wup_f[:, 2048:4096]
        vdn = big[:, 4096:6144].rearrange("p (x n) -> p x n", n=P)
        dP = small[0:64, 0:264]
        dPT = small[:, 264:456].rearrange("p (n m) -> p n m", n=3)
        negm = small[:, 456:460]
        mx = small[:, 460:464]
        ssum = small[:, 464:560]
        coef = small[:, 560:568]
        osq = small[:, 568:572]
        gD = small[0:64, 572:575]
        dst_ = small[0:64, 576:580]
        cbias = small[:, 580:582]
        oD = small[:, 584:616].rearrange("p (t b) -> p t b", t=4)
        oD2 = small[:, 616:648].rearrange("p (t b) -> p t b", t=4)
        peN = small[0:CB, 648:904].rearrange("p (v n) -> p v n", v=2)
        gates = sb("gates", [P, QT + 1, 3 * NQ])

        def sp_pages(sp, l, names, dsts, sem_name):
            for x in range(DEC * NPAGE):
                pg = sp.value_load(pages[0:1, x:x + 1], min_val=0, max_val=a[f"cache_{names[0]}"].shape[1] - 1)
                for name, dst in zip(names, dsts):
                    sp.dma_start(dst[:, x, :], a[f"cache_{name}"][bass.ds(l, 1), bass.ds(pg, 1)]
                                 .rearrange("a b t g d -> t (a b) (g d)").squeeze(1)).then_inc(S(sem_name), 16)

        def sp_compress_in(sp, T, l):
            sp_pages(sp, l, ("cmp_k", "cmp_v"), page, "cpage_in")
            for v in range(2):
                for g in range(2):
                    sp.dma_start(peN[:, v, g * HD:(g + 1) * HD], a["cmp_pe"][bass.ds(l, 1), v]
                                 .rearrange("a j d -> (a j) d")).then_inc(S("pe_in"), 16)

        def sp_compress_w(sp, T, l, v):
            if v == 0:
                sp.wait_ge(*stage("wc_zero"))
            else:
                sp.wait_ge(S("win_ready"), 1)
            for g in range(2):
                sp.dma_start(wc[g * HD:(g + 1) * HD, :, g * HD:(g + 1) * HD], a["cmp_w"][bass.ds(l, 1), v]
                             .rearrange("a (j d) e -> d (a j) e", d=HD)).then_inc(S("wc_in"), 16)

        def pool_compress(pool, T, link):
            pool.wait_ge(S("r_ready"), QT + 1)
            link(pool.memset(big[:, 0:CB * P], 0.0))
            pool.sem_inc(reach("wc_zero"), 1)

        def pe_compress(pe, T, v):
            if v == 0:
                pe.wait_ge(S("cpage_in"), 32 * 16)
                pe.wait_ge(S("pe_in"), 64)
                pe.wait_ge(S("rows_ready"), QT + 1)
                pe.wait_ge(*stage("state_rows"))
                pe.wait_ge(S("rot_used"), 4)
            else:
                pe.wait_ge(S("xc_a"), 1)
                pe.wait_ge(S("xc_d"), 1)
            for i in range(QT):
                pe.transpose(ps[:, 0, i * P:(i + 1) * P], rows[:, i, v * P:(v + 1) * P], ident)
            for x in range(DEC * NPAGE):
                pe.transpose(ps[:, 1 + x // 4, x % 4 * P:(x % 4 + 1) * P], page[v][:, x, :], ident)
            pe.transpose(ps[:, 5, 0:CB], peN[:, v, :], ident[0:CB, 0:CB]).then_inc(S("xc_t"), 1)
            pe.wait_ge(S("wc_in"), 32 * (v + 1))
            pe.wait_ge(S("xc_a"), v + 1)
            pe.wait_ge(S("xc_d"), v + 1)
            for j in range(CB):
                ins = pe.matmul(ps[:, 6 + v, 0:NWIN], wc[:, j, :], xc[:, j:j + CS * (NWIN - 1) + 1:CS],
                                start=j == 0, stop=j == CB - 1)
            ins.then_inc(S("win_ready"), 1)

        def act_compress(act, T, link, v):
            act.wait_ge(S("xc_t"), v + 1)
            if v:
                act.wait_ge(S("win_ready"), v)
            act.activation(xc[:, 0:3 * 512].rearrange("p (x n) -> p x n", x=3), ps[:, 0:3, :], ACT.Copy)\
                .then_inc(S("xc_a"), 1)

        def dve_compress(dve, T, link, v):
            dve.wait_ge(S("xc_t"), v + 1)
            if v:
                dve.wait_ge(S("win_ready"), v)
            dve.tensor_copy(xc[:, 3 * 512:5 * 512].rearrange("p (x n) -> p x n", x=2), ps[:, 3:5, :])
            link(dve.tensor_copy(xc[:, XCOLS:XCOLS + CB], ps[:, 5, 0:CB]))
            dve.sem_inc(S("xc_d"), 1)
            dve.wait_ge(S("win_ready"), v + 1)
            link(dve.tensor_copy(cbias[:, v:v + 1], ps[:, 6 + v, NWIN - 1:NWIN]))
            link(dve.tensor_scalar((kcmp, vcmp)[v], ps[:, 6 + v, 0:NWIN], cbias[:, v:v + 1], None, ALU.add))
            dve.sem_inc(S("cmp_out"), 1)

        def pe_cmp_rows(pe, T):
            pe.wait_ge(S("cmp_out"), 2)
            pe.transpose(ps[0:NCMP, 0, 0:P], vcmp[:, 0:NCMP], ident)
            for b in range(DEC):
                o_ = P + b * P
                at = SEQ // CS + b * (PAST // CS)
                ins = pe.transpose(ps[0:NCMP_D, o_ // 512, o_ % 512:o_ % 512 + P], vcmp[:, at:at + NCMP_D], ident)
            ins.then_inc(S("vc_t"), 1)
            for n in range(2):
                for i in range(QT + 1):
                    m = P if i < QT else DEC
                    b, at = (3 + n, i * P) if i < QT else (5, n * DEC)
                    ins = pe.transpose(ps[:, b, at:at + m], rows[0:m, i, 256 * (n + 1):256 * (n + 1) + P],
                                       ident[0:m, 0:m])
            ins.then_inc(S("kT_t"), 1)

        def dve_cmp_rows(dve, T, link):
            dve.wait_ge(S("vc_t"), 1)
            dve.tensor_copy(vcr[0:NCMP, :], ps[0:NCMP, 0, 0:P])
            dve.tensor_copy(vcd[0:NCMP_D, 0:3, :], ps[0:NCMP_D, 0, P:512].rearrange("p (b n) -> p b n", b=3))
            dve.tensor_copy(vcd[0:NCMP_D, 3:7, :], ps[0:NCMP_D, 1, :].rearrange("p (b n) -> p b n", b=4))
            link(dve.tensor_copy(vcd[0:NCMP_D, 7, :], ps[0:NCMP_D, 2, 0:P]))
            dve.wait_ge(S("kT_t"), 1)
            for n in range(2):
                dve.tensor_copy(kT[n][:, 0:SEQ], ps[:, 3 + n, :])
                ins = dve.tensor_copy(kT[n][:, SEQ:TOK], ps[:, 5, n * DEC:(n + 1) * DEC])
            link(ins)
            dve.sem_inc(reach("kT_ready"), 1)
            dve.wait_ge(*stage("gate_exp"))
            for v in (gates[:, 0:QT, :], gates[0:DEC, QT, :]):
                link(dve.tensor_scalar(v, v, 1.0, None, ALU.add))
                link(dve.reciprocal(v, v))
            dve.sem_inc(reach("gates_ready"), 1)

        def act_gates(act, T, link):
            act.wait_ge(S("r_used"), QT + 1)
            act.activation(gates[:, 0:QT, :], rows[:, 0:QT, 768:792], ACT.Exp, scale=-1.0)
            link(act.activation(gates[0:DEC, QT, :], rows[0:DEC, QT, 768:792], ACT.Exp, scale=-1.0))
            act.sem_inc(reach("gate_exp"), 1)

        UNITS = [(i, br, t) for i in range(QT) for br in range(3) for t in range(4)]
        CMPB = 0

        def keys_of(i, br):
            return (NCMP, 1, NCMP) if br == CMPB else ((i + 1) * P, i + 1, P)

        def pe_scores(pe, u):
            i, br, t = UNITS[u]
            nk = keys_of(i, br)[0]
            q, k = (proj, kcmp) if br == CMPB else (qrT, kT[br - 1])
            if u >= 2:
                pe.wait_ge(S("p_exp"), 2 * (u - 1))
            for g in range(2):
                h = slice(g * HD, (g + 1) * HD)
                ins = pe.matmul(ps[:, 2 * (u % 2) + g, 0:nk], q[h, t, i * P:(i + 1) * P], k[h, 0:nk],
                                start=True, stop=True)
            ins.then_inc(S("s_ready"), 1)

        def pe_prompt(pe, T):
            pe.wait_ge(*stage("kT_ready"))
            pe.wait_ge(S("qr_ready"), 4)
            pe_scores(pe, 0)
            pe_scores(pe, 1)
            for u, (i, br, t) in enumerate(UNITS):
                nk, nt, kk = keys_of(i, br)
                pe.wait_ge(S("p_exp"), 2 * (u + 1))
                if u:
                    pe.wait_ge(S("pt_a"), u)
                    pe.wait_ge(S("pt_d"), u)
                for g in range(2):
                    for n in range(nt):
                        ins = pe.transpose(ps[0:kk, 4 + g, n * P:(n + 1) * P],
                                           prob[:, u % 2, g, n * P:n * P + kk], ident)
                ins.then_inc(S("pt_ready"), 1)
                if u + 2 < len(UNITS):
                    pe_scores(pe, u + 2)
                pe.wait_ge(S("pt_a"), u + 1)
                pe.wait_ge(S("pt_d"), u + 1)
                k = u // 4
                if t == 0 and k >= 2:
                    pe.wait_ge(S("o_used"), k - 1)
                for g in range(2):
                    h = 2 * t + g
                    for n in range(nt):
                        v = vcr[0:kk] if br == CMPB else rows[:, n, 384 if br == 1 else 640:][:, 0:P]
                        ins = pe.matmul(ps[:, 6 + k % 2, h * HD:(h + 1) * HD], PT[0:kk, u % 2, g, n * P:(n + 1) * P],
                                        v[:, g * HD:(g + 1) * HD], start=n == 0, stop=n == nt - 1)
                ins.then_inc(S("pv_ready"), 1)

        def act_exps(act, u):
            i, br, t = UNITS[u]
            nk = keys_of(i, br)[0]
            act.wait_ge(S("nm_ready"), u + 1)
            if u >= 2:
                act.wait_ge(S("pt_ready"), u - 1)
            for g in range(2):
                at = (i * 3 + br) * 8 + 2 * t + g
                act.activation(prob[:, u % 2, g, 0:nk], ps[:, 2 * (u % 2) + g, 0:nk], ACT.Exp, scale=SCALE,
                               bias=negm[:, 2 * (u % 2) + g:2 * (u % 2) + g + 1],
                               accum_out=ssum[:, at:at + 1]).then_inc(S("p_exp"), 1)

        def act_prompt(act, T, link):
            act_exps(act, 0)
            for u, (i, br, t) in enumerate(UNITS):
                nk, nt, kk = keys_of(i, br)
                if u + 1 < len(UNITS):
                    act_exps(act, u + 1)
                act.wait_ge(S("pt_ready"), u + 1)
                if u >= 2:
                    act.wait_ge(S("pv_ready"), u - 1)
                act.activation(PT[0:kk, u % 2, 0, 0:nt * P], ps[0:kk, 4, 0:nt * P], ACT.Copy).then_inc(S("pt_a"), 1)
            act.wait_ge(*stage("oacc_ready"))
            for i in range(QT):
                ins = act.activation(prob[:, 0, 0, 0:512], oacc[:, i, :], ACT.Square, accum_out=osq[:, i:i + 1])
                link(ins)
            link(act.activation(osq, osq, ACT.Sqrt, scale=1 / 512, bias=cst[:, C_EPS:C_EPS + 1]))
            act.sem_inc(reach("oroot"), 1)

        def dve_softmax(dve, T, link, u):
            i, br, t = UNITS[u]
            nk = keys_of(i, br)[0]
            b = 2 * (u % 2)
            dve.wait_ge(S("s_ready"), u + 1)
            if br == CMPB:
                s, m = ps[:, b:b + 2, 0:nk], cst[:, C_CMPM + i * NCMP:C_CMPM + (i + 1) * NCMP]
            else:
                s, m = ps[:, b:b + 2, i * P:nk], cst[:, C_CAUS:C_CAUS + P]
            link(dve.tensor_tensor(s, s, m.unsqueeze(1).broadcast_to((P, 2, m.shape[1])), ALU.add))
            link(dve.tensor_reduce(mx[:, b:b + 2], ps[:, b:b + 2, 0:nk], X, ALU.max))
            dve.tensor_scalar(negm[:, b:b + 2], mx[:, b:b + 2], 0.1 * NEG, -SCALE, ALU.max, ALU.mult)\
                .then_inc(S("nm_ready"), 1)

        def dve_combine(dve, T, link, k):
            i, br = k // 3, k % 3
            dve.wait_ge(S("pv_ready"), 4 * (k + 1))
            link(dve.tensor_scalar(coef, ssum[:, k * 8:k * 8 + 8], 1e-30, None, ALU.max))
            link(dve.reciprocal(coef, coef))
            c2 = coef.rearrange("p (t g) -> p t g", g=2)
            link(dve.tensor_tensor(c2, c2, gates[:, i, :].rearrange("p (g t r) -> p t g r", g=2, r=3)[:, :, :, br],
                                   ALU.mult))
            f = coef.unsqueeze(2).broadcast_to((P, NQ, HD))
            src = ps[:, 6 + k % 2, :].rearrange("p (h d) -> p h d", d=HD)
            dst = oacc[:, i, :] if br == 0 else otmp
            dve.tensor_tensor(dst.rearrange("p (h d) -> p h d", d=HD), src, f, ALU.mult).then_inc(S("o_used"), 1)
            dve.wait_ge(S("o_used"), k + 1)
            if br:
                link(dve.tensor_tensor(oacc[:, i, :], oacc[:, i, :], otmp, ALU.add))

        def dve_prompt(dve, T, link):
            dve_softmax(dve, T, link, 0)
            for u, (i, br, t) in enumerate(UNITS):
                nk, nt, kk = keys_of(i, br)
                if u + 1 < len(UNITS):
                    dve_softmax(dve, T, link, u + 1)
                dve.wait_ge(S("pt_ready"), u + 1)
                if u >= 2:
                    dve.wait_ge(S("pv_ready"), u - 1)
                dve.tensor_copy(PT[0:kk, u % 2, 1, 0:nt * P], ps[0:kk, 5, 0:nt * P]).then_inc(S("pt_d"), 1)
                if u % 4 == 1 and u > 4:
                    dve_combine(dve, T, link, u // 4 - 1)
            dve_combine(dve, T, link, len(UNITS) // 4 - 1)
            dve.sem_inc(reach("oacc_ready"), 1)
            dve.wait_ge(*stage("oroot"))
            link(dve.reciprocal(osq, osq))
            for i in range(QT):
                link(dve.tensor_scalar(oacc[:, i, :], oacc[:, i, :], osq[:, i:i + 1], None, ALU.mult))
            dve.sem_inc(reach("on_ready"), 1)
            for t in range(4):
                dve.wait_ge(S("ot_ready"), t + 1)
                dve.tensor_scalar(merged[:, t, 0:SEQ], ps[:, t, :], vec[:, V_GRP + t:V_GRP + t + 1], None, ALU.mult)\
                    .then_inc(S("om_ready"), 1)
            dve.wait_ge(S("om_ready"), 4)

        def pe_prompt_out(pe, T):
            pe.wait_ge(*stage("on_ready"))
            for t in range(4):
                for i in range(QT):
                    heads = oacc[:, i, t * P:(t + 1) * P]
                    ins = pe.transpose(ps[:, t, i * P:(i + 1) * P], heads, ident)
                ins.then_inc(S("ot_ready"), 1)

        def pool_qz(pool, T, link):
            pool.wait_ge(S("win_ready"), 2)
            pool.wait_ge(S("qr_ready"), 4)
            link(pool.memset(wdn[:, 1152:2176], 0.0))
            for n, q in enumerate((proj, qrT)):
                for g in range(2):
                    h = slice(g * HD, (g + 1) * HD)
                    dst = wdn[h, 1152 + 512 * n:1152 + 512 * n + 576].rearrange("p (b x) -> p b x", x=72)
                    link(pool.tensor_copy(dst[:, :, 4 * g:4 * g + 4], q[h, 0:4, SEQ:TOK].rearrange("p t b -> p b t")))
            pool.sem_inc(reach("qz_ready"), 1)

        def sp_decode_in(sp, T, l):
            def window(kind, dst):
                for n in range(2):
                    sp.dma_start(dst[:, 8 * n:8 * n + 8], a[f"cache_win_{kind}"][bass.ds(l, 1), 4 * n:4 * n + 4]
                                 .rearrange("a b (n t) g d -> t (a b n) (g d)", t=P)).then_inc(S("wwin_in"), 16)

            sp.wait_ge(*stage("gates_ready"))
            sp.dma_start(gD, gates[0:DEC, QT, :]).then_inc(S("gD_in"), 16)
            sp.wait_ge(S("xc_t"), 2)
            sp.wait_ge(S("pt_ready"), len(UNITS))
            sp.wait_ge(*stage("oroot"))
            sp_pages(sp, l, ("sel_k", "sel_v"), (page[0], vdn), "spage_in")
            sp.wait_ge(S("kd_t"), 4)
            window("k", page[0])
            sp.wait_ge(S("do_ready"), 2)
            window("v", vdn)

        def pe_decode(pe, T):
            pe.wait_ge(*stage("qz_ready"))
            pe.wait_ge(S("om_ready"), 4)
            for br in range(3):
                n = br - 1
                if br:
                    if br == 1:
                        pe.wait_ge(S("spage_in"), 32 * 16)
                    else:
                        pe.wait_ge(S("wwin_in"), 64)
                    for x in range(4):
                        if x >= 2 or br == 2:
                            pe.wait_ge(S("kd_out"), 4 * n + x - 1)
                        for y in range(4):
                            ins = pe.transpose(ps[:, x % 2, y * P:(y + 1) * P], page[0][:, 4 * x + y, :], ident)
                        ins.then_inc(S("kd_t"), 1)
                    pe.wait_ge(S("kd_out"), 4 * (n + 1))
                    for b in range(DEC):
                        pe.matmul(ps[0:64, 2, 0:PAST], qz[1][:, b, :], kdT[:, b * PAST:(b + 1) * PAST],
                                  start=b == 0, stop=b == DEC - 1, skip_group_check=True)
                    for b in range(DEC):
                        ins = pe.matmul(ps[0:64, 2, PAST:PAST + DEC], qz[1][:, b, :], kT[n][:, SEQ:TOK],
                                        start=False, stop=b == DEC - 1, skip_group_check=True)
                else:
                    for b in range(DEC):
                        at = SEQ // CS + b * (PAST // CS)
                        ins = pe.matmul(ps[0:64, 2, 0:NCMP_D], qz[0][:, b, :], kcmp[:, at:at + NCMP_D],
                                        start=b == 0, stop=b == DEC - 1)
                ins.then_inc(S("ds_ready"), 1)
                pe.wait_ge(S("dp_ready"), br + 1)
                if br:
                    for m in range(2):
                        pe.transpose(ps[:, 3, m * 64:(m + 1) * 64], dP[:, m * P:(m + 1) * P], ident[0:64, 0:64])
                    ins = pe.transpose(ps[0:DEC, 3, 128:192], dP[:, PAST:PAST + DEC], ident[0:64, 0:64])
                else:
                    ins = pe.transpose(ps[0:NCMP_D, 3, 0:64], dP[:, 0:NCMP_D], ident[0:64, 0:64])
                ins.then_inc(S("dpt_ready"), 1)
                pe.wait_ge(S("dpt_out"), br + 1)
                for b in range(DEC):
                    c = slice(b * NQ, (b + 1) * NQ)
                    for m in range(2 if br else 1):
                        v, w = (vdn[:, 2 * b + m, :], P) if br else (vcd[0:NCMP_D, b, :], NCMP_D)
                        ins = pe.matmul(ps[:, 7, c], v, dPT[0:w, m, c], start=br == 0 and b == 0,
                                        stop=False, skip_group_check=True)
                if br:
                    at = 384 if br == 1 else 640
                    ins = pe.matmul(ps[:, 7, 0:64], rows[0:DEC, QT, at:at + P], dPT[0:DEC, 2, :],
                                    start=False, stop=br == 2, skip_group_check=True)
                ins.then_inc(S("do_ready"), 1)
            pe.wait_ge(S("osq_ready"), 1)
            for t in range(4):
                ins = pe.matmul(ps[:, 6, 0:DEC], ones, oD2[:, t, :], start=t == 0, stop=t == 3)
            ins.then_inc(S("oss_ready"), 1)

        def act_decode(act, T, link):
            for br in range(3):
                if br:
                    for x in range(4):
                        act.wait_ge(S("kd_t"), 4 * (br - 1) + x + 1)
                        if x == 0 and br == 2:
                            act.wait_ge(S("ds_ready"), 2)
                        act.activation(kdT[:, x * 512:(x + 1) * 512], ps[:, x % 2, :], ACT.Copy)\
                            .then_inc(S("kd_out"), 1)
                act.wait_ge(S("dm_ready"), br + 1)
                nk = PAST + DEC if br else NCMP_D
                link(act.activation(dP[:, 0:nk], ps[0:64, 2, 0:nk], ACT.Exp, scale=SCALE, bias=dst_[:, 1:2],
                                    accum_out=dst_[:, 2:3]))
                act.sem_inc(S("de_ready"), 1)
            act.wait_ge(*stage("oD_ready"))
            act.activation(oD2, oD, ACT.Square).then_inc(S("osq_ready"), 1)
            act.wait_ge(S("oss_ready"), 1)
            act.activation(small[:, 0:DEC], ps[:, 6, 0:DEC], ACT.Sqrt, scale=1 / 512, bias=cst[:, C_EPS:C_EPS + 1])\
                .then_inc(S("odroot"), 1)

        def dve_decode(dve, T, link):
            for br in range(3):
                nk = PAST + DEC if br else NCMP_D
                dve.wait_ge(S("ds_ready"), br + 1)
                if br:
                    s = ps[0:64, 2, PAST:PAST + DEC]
                    link(dve.tensor_tensor(s, s, cst[0:64, C_DMASK:C_DMASK + DEC], ALU.add))
                link(dve.tensor_reduce(dst_[:, 0:1], ps[0:64, 2, 0:nk], X, ALU.max))
                link(dve.tensor_scalar(dst_[:, 1:2], dst_[:, 0:1], -SCALE, None, ALU.mult))
                dve.sem_inc(S("dm_ready"), 1)
                if br == 0:
                    dve.wait_ge(S("gD_in"), 16)
                dve.wait_ge(S("de_ready"), br + 1)
                link(dve.reciprocal(dst_[:, 3:4], dst_[:, 2:3]))
                link(dve.tensor_tensor(dst_[:, 3:4], dst_[:, 3:4], gD[:, br:br + 1], ALU.mult))
                link(dve.tensor_scalar(dP[:, 0:nk], dP[:, 0:nk], dst_[:, 3:4], None, ALU.mult))
                dve.sem_inc(S("dp_ready"), 1)
                dve.wait_ge(S("dpt_ready"), br + 1)
                if br:
                    dve.tensor_copy(dPT[:, 0:2, :], ps[:, 3, 0:128].rearrange("p (n m) -> p n m", n=2))
                    link(dve.tensor_copy(dPT[0:DEC, 2, :], ps[0:DEC, 3, 128:192]))
                else:
                    link(dve.tensor_copy(dPT[0:NCMP_D, 0, :], ps[0:NCMP_D, 3, 0:64]))
                dve.sem_inc(S("dpt_out"), 1)
            dve.wait_ge(S("do_ready"), 3)
            for g in range(2):
                h = slice(g * HD, (g + 1) * HD)
                ins = dve.tensor_copy(oD[h], ps[h, 7, 0:64].rearrange("p (b x) -> p x b", x=NQ)[:, 4 * g:4 * g + 4])
                link(ins)
            dve.sem_inc(reach("oD_ready"), 1)
            dve.wait_ge(S("odroot"), 1)
            link(dve.reciprocal(small[:, 0:DEC], small[:, 0:DEC]))
            for t in range(4):
                ins = dve.scalar_tensor_tensor(out=merged[:, t, SEQ:TOK], in0=oD[:, t, :],
                                               scalar=vec[:, V_GRP + t:V_GRP + t + 1], in1=small[:, 0:DEC],
                                               op0=ALU.mult, op1=ALU.mult)
                link(ins)
            dve.sem_inc(reach("attn_done"), 1)

        rw = proj[:, 8:15, :]
        xm = proj[:, 0:7, :]
        wdec, aa, gate, nkk, bb, tt = (big[:, 1040 * n:1040 * (n + 1)].rearrange("p (m t) -> p m t", m=2)
                                       for n in range(6))
        ar = big[:, 6240:8288].rearrange("p (m c s t) -> p m c s t", m=2, c=NCH, s=2)
        bt = big[:, 8288:9312].rearrange("p (m c t) -> p m c t", m=2, c=NCH)
        kt = big[:, 9312:10336].rearrange("p (m c t) -> p m c t", m=2, c=NCH)
        pp = big[:, 10336:11360].rearrange("p (m t) -> p m t", m=2)
        bh = wdn[:, 0:1024].rearrange("p (m c t) -> p m c t", m=2, c=NCH)
        kh = wdn[:, 1024:2048].rearrange("p (m c t) -> p m c t", m=2, c=NCH)
        wu = wdn[:, 2048:3072].rearrange("p (c s n) -> p c s n", c=NCH, s=2)
        gT = wdn[:, 3072:3584].rearrange("p (c n) -> p c n", c=NCH)
        hh = wdn[:, 3584:4096].rearrange("p (c n) -> p c n", c=NCH)
        rwt = wdn[:, 4096:4608].rearrange("p (c n) -> p c n", c=NCH)
        st = wdn[:, 4608:5184].rearrange("p (c n) -> p c n", c=NCH + 1)
        swk = wdn[0:64, 5184:5312]
        lora = wdn[:, 5312:5568]
        bst, kst, vst_ = (wup_f[:, 1024 * n:1024 * (n + 1)].rearrange("p (m c n) -> p m c n", m=2, c=NCH)
                          for n in range(3))
        ag = wup_f[:, 3072:4096].rearrange("p (c s n) -> p c s n", c=NCH, s=2)
        mats = fT[:, 0:4096].rearrange("p (k c n) -> p k c n", k=4, c=NCH)
        inv = proj[:, 8:15, :].rearrange("p c t -> p (c t)")
        xi, xT, yy = (inv[:, 1024 * n:1024 * (n + 1)].rearrange("p (c n) -> p c n", c=NCH) for n in range(3))
        oT = mix[:, 15 * TOK:17 * TOK].rearrange("p (m t) -> p m t", m=2)
        sd = mix[:, 17 * TOK:17 * TOK + 1024].rearrange("p (x k) -> p x k", k=HD)
        zz = fT[:, 0:1024].rearrange("p (x k) -> p x k", k=HD)
        zt = fT[:, 1024:2048].rearrange("p (x k) -> p x k", k=HD)
        shn = wdn[0:DEC, 2048:2048 + RWC]
        shT = small[:, 700:756].rearrange("p (c b) -> p c b", c=7)
        nw0 = small[:, 756:760]
        sk = small[:, 760:776]
        pend = small[:, 776:792].rearrange("p (m c) -> p m c", m=2)
        i2 = small[:, 792:856]

        def levels(n):
            return cst[:, C_LVL + n * P:C_LVL + (n + 1) * P]

        def bc4(v, n):
            return v.unsqueeze(1).broadcast_to((P, n, v.shape[1]))

        def sp_rwkv(sp, T, l):
            L = bass.ds(l, 1)
            sp.wait_ge(*stage("attn_done"))
            sp.dma_start(shn, a["state_shift"][L].rearrange("a b n -> (a b) n")).then_inc(S("rw_in"), 16)
            for n, (name, r0, r1) in enumerate((("rw_w2", 0, 32), ("rw_a2", 32, 64), ("rw_g2", 64, 128))):
                sp.dma_start(lora[r0:r1, :], a[name][L].rearrange("a r n -> (a r) n")).then_inc(S("rw_in"), 16)
            for m in range(2):
                sp.dma_start(sd[:, m * DEC:(m + 1) * DEC, :],
                             a["state_wkv"][L, :, 2 * m:2 * m + 2].rearrange("a b q v k -> (q v) (a b) k"))\
                    .then_inc(S("rw_in"), 16)
            sp.wait_ge(*stage("sd_new"))
            for m in range(2):
                sp.dma_start(o["s_wkv"][L, :, 2 * m:2 * m + 2].rearrange("a b q v k -> (q v) (a b) k"),
                             sd[:, m * DEC:(m + 1) * DEC, :]).then_inc(S("wkv_st"), 16)
            for m in range(2):
                sp.wait_ge(S("swk_ready"), m + 1)
                sp.dma_start(o["p_wkv"][L, :, 2 * m:2 * m + 2].rearrange("a b q v k -> v (a b q) k"),
                             swk.rearrange("p (q k) -> p q k", q=2)).then_inc(S("wkv_st"), 16)
                sp.wait_ge(S("wkv_st"), 32 + 16 * (m + 1))
                sp.sem_inc(S("swk_free"), 1)

        def pe_rw_in(pe, T):
            pe.wait_ge(S("rw_in"), 6 * 16)
            pe.wait_ge(*stage("attn_done"))
            for c in range(7):
                ins = pe.transpose(ps[:, 6, c * DEC:(c + 1) * DEC], shn[:, c * P:(c + 1) * P], ident[0:DEC, 0:DEC])
            ins.then_inc(S("sh_t"), 1)
            pe.wait_ge(*stage("lora_ready"))
            for m in range(2):
                if m:
                    pe.wait_ge(S("lora_out"), 1)
                for n, (r0, r1) in enumerate(((0, 32), (32, 64), (64, 128))):
                    for h in range(2):
                        ins = pe.matmul(ps[:, 2 * n + h, 0:HALF], lora[r0:r1, m * P:(m + 1) * P],
                                        xm[r0:r1, 6, h * HALF:(h + 1) * HALF], start=True, stop=True)
                ins.then_inc(S("lora_mm"), 1)
            for m in range(2):
                pe.wait_ge(S("kksq"), m + 1)
                if m:
                    pe.wait_ge(S("kkroot"), 1)
                mm_tokens(pe, 6, bones, tt[:, m, :], True, True).then_inc(S("kkss"), 1)

        def act_rw_in(act, T, link):
            act.wait_ge(*stage("xm_ready"))
            act.activation(xm[0:32, 6, :], xm[0:32, 6, :], ACT.Tanh)
            link(act.activation(xm[64:128, 6, :], xm[64:128, 6, :], ACT.Exp, scale=-1.0))
            act.sem_inc(reach("lora_act"), 1)
            for m in range(2):
                act.wait_ge(S("lora_mm"), m + 1)
                act.activation(halves(wdec[:, m, :]), pair(0), ACT.Exp, scale=-1.0, bias=nw0[:, m:m + 1])
                act.activation(halves(aa[:, m, :]), pair(2), ACT.Exp, scale=-1.0, bias=nw0[:, 2 + m:3 + m])
                link(act.activation(halves(gate[:, m, :]), pair(4), ACT.Copy))
                act.sem_inc(S("lora_out"), 1)
            act.wait_ge(*stage("wsig"))
            link(act.activation(wdec, wdec, ACT.Exp, scale=-float(np.exp(-0.5))))
            act.sem_inc(reach("w_ready"), 1)
            act.wait_ge(*stage("kk_raw"))
            for m in range(2):
                act.activation(tt[:, m, :], nkk[:, m, :], ACT.Square).then_inc(S("kksq"), 1)
            for m in range(2):
                act.wait_ge(S("kkss"), m + 1)
                act.activation(halves(tt[:, m, :]), pair(6), ACT.Sqrt).then_inc(S("kkroot"), 1)

        def dve_rw_in(dve, T, link):
            link(dve.tensor_tensor(i2, ident[:, 0:HD], ident[:, HD:P], ALU.add))
            link(dve.tensor_scalar(nw0, vec[:, V_W0:V_W0 + 4], -1.0, None, ALU.mult))
            link(dve.tensor_tensor(xm[:, :, 1:SEQ], rw[:, :, 0:SEQ - 1], rw[:, :, 1:SEQ], ALU.subtract))
            link(dve.tensor_scalar(xm[:, :, 0], rw[:, :, 0], -1.0, None, ALU.mult))
            dve.wait_ge(S("sh_t"), 1)
            link(dve.tensor_copy(shT, ps[:, 6, 0:7 * DEC].rearrange("p (c b) -> p c b", c=7)))
            link(dve.tensor_tensor(xm[:, :, SEQ:TOK], shT, rw[:, :, SEQ:TOK], ALU.subtract))
            for c in range(7):
                ins = dve.scalar_tensor_tensor(out=xm[:, c, :], in0=xm[:, c, :], scalar=vec[:, V_MU + c:V_MU + c + 1],
                                               in1=rw[:, c, :], op0=ALU.mult, op1=ALU.add)
            link(ins)
            dve.sem_inc(reach("xm_ready"), 1)
            dve.wait_ge(*stage("lora_act"))
            link(dve.tensor_scalar(xm[64:128, 6, :], xm[64:128, 6, :], 1.0, None, ALU.add))
            link(dve.reciprocal(xm[64:128, 6, :], xm[64:128, 6, :]))
            dve.sem_inc(reach("lora_ready"), 1)
            for m in range(2):
                ins = dve.tensor_scalar(nkk[:, m, :], xm[:, 2 + m, :], vec[:, V_KK + m:V_KK + m + 1], -1.0,
                                        ALU.mult, ALU.mult)
            link(ins)
            dve.sem_inc(reach("kk_raw"), 1)
            dve.wait_ge(S("lora_out"), 2)
            both = big[:, 0:2080]
            link(dve.tensor_scalar(both, both, 1.0, None, ALU.add))
            link(dve.reciprocal(both, both))
            dve.sem_inc(reach("wsig"), 1)
            for m in range(2):
                link(dve.tensor_scalar(bb[:, m, :], aa[:, m, :], -1.0, vec[:, V_KA + m:V_KA + m + 1], ALU.add,
                                       ALU.mult))
                link(dve.scalar_tensor_tensor(out=xm[:, 2 + m, :], in0=bb[:, m, :], scalar=1.0, in1=xm[:, 2 + m, :],
                                              op0=ALU.add, op1=ALU.mult))
            dve.wait_ge(S("kkroot"), 2)
            link(dve.tensor_scalar(tt, tt, 1e-12, None, ALU.max))
            link(dve.reciprocal(tt, tt))
            link(dve.tensor_tensor(nkk, nkk, tt, ALU.mult))
            link(dve.scalar_tensor_tensor(out=bb, in0=nkk, scalar=-1.0, in1=aa, op0=ALU.mult, op1=ALU.mult))
            dve.wait_ge(*stage("w_ready"))

        def pe_rw_decode(pe, T):
            for n in range(5):
                b = 2 * (n % 2)
                pe.wait_ge(S("z_ready"), n + 1)
                for h in range(2):
                    ins = pe.matmul(ps[:, b + h, :], bones, zz[:, 8 * h:8 * h + 8, :].rearrange("p x k -> p (x k)"),
                                    start=True, stop=True)
                ins.then_inc(S("zb_ready"), 1)

        def dve_rw_decode(dve, T, link):
            def x16(v):
                return v[:, :, SEQ:TOK]

            def spread(n):
                v = x16((nkk, wdec, bb, xm[:, 2:4, :], xm[:, 0:2, :])[n])
                for m in range(2):
                    ins = dve.tensor_tensor(zz[:, m * DEC:(m + 1) * DEC, :],
                                            v[:, m].unsqueeze(2).broadcast_to((P, DEC, HD)),
                                            i2.unsqueeze(1).broadcast_to((P, DEC, HD)), ALU.mult)
                link(ins)
                dve.sem_inc(S("z_ready"), 1)
                dve.wait_ge(S("zb_ready"), n + 1)
                return ps[:, 2 * (n % 2):2 * (n % 2) + 2, :].rearrange("p h (x k) -> p (h x) k", k=HD)

            def per_row(v):
                return v.unsqueeze(2).broadcast_to((P, 2 * DEC, HD))

            z = spread(0)
            link(dve.tensor_tensor(zt, sd, z, ALU.mult))
            link(dve.tensor_reduce(sk, zt, X, ALU.add))
            z = spread(1)
            link(dve.tensor_tensor(sd, sd, z, ALU.mult))
            z = spread(2)
            link(dve.tensor_tensor(zt, z, per_row(sk), ALU.mult))
            link(dve.tensor_tensor(sd, sd, zt, ALU.add))
            z = spread(3)
            for m in range(2):
                ins = dve.tensor_tensor(zt[:, m * DEC:(m + 1) * DEC], z[:, m * DEC:(m + 1) * DEC],
                                        xm[:, 4 + m, SEQ:TOK].unsqueeze(2).broadcast_to((P, DEC, HD)), ALU.mult)
            link(ins)
            link(dve.tensor_tensor(sd, sd, zt, ALU.add))
            dve.sem_inc(reach("sd_new"), 1)
            z = spread(4)
            link(dve.tensor_tensor(zt, sd, z, ALU.mult))
            for m in range(2):
                link(dve.tensor_reduce(oT[:, m, SEQ:TOK], zt[:, m * DEC:(m + 1) * DEC], X, ALU.add))

        def dve_rw_decay(dve, T, link):
            for m in range(2):
                for c in range(NCH):
                    s = slice(c * CH, (c + 1) * CH)
                    ins = dve.tensor_tensor_scan(pp[:, m, s], wdec[:, m, s], wdec[:, m, s], 1.0, ALU.mult, ALU.bypass)
            link(ins)
            pc = pp.rearrange("p m (c t) -> p m c t", t=CH)
            for m in range(2):
                def ch(v):
                    return v[:, m, 0:SEQ].rearrange("p (c t) -> p c t", t=CH)
                dve.tensor_tensor(ar[:, m, :, 1, :], ch(xm[:, 0:2, :]), pc[:, m], ALU.mult)
                dve.tensor_tensor(ar[:, m, :, 0, 1:CH], ch(nkk)[:, :, 1:CH], pc[:, m, :, 0:CH - 1], ALU.mult)
                dve.tensor_copy(ar[:, m, :, 0, 0], ch(nkk)[:, :, 0])
                dve.tensor_copy(pend[:, m], pc[:, m, :, CH - 1])
                link(dve.reciprocal(tt[:, m, 0:SEQ], pp[:, m, :]))
                link(dve.tensor_tensor(bt[:, m], ch(bb), ch(tt), ALU.mult))
                link(dve.tensor_tensor(kt[:, m], ch(xm[:, 2:4, :]), ch(tt), ALU.mult))
                e = pend[:, m].unsqueeze(2).broadcast_to((P, NCH, CH))
                link(dve.tensor_tensor(bh[:, m], bt[:, m], e, ALU.mult))
                link(dve.tensor_tensor(kh[:, m], kt[:, m], e, ALU.mult))
            dve.sem_inc(reach("chunks_ready"), 1)

        def pe_rw_chunks(pe, T):
            pe.wait_ge(*stage("chunks_ready"))
            for m in range(2):
                if m:
                    pe.wait_ge(S("o_out"), 1)
                    pe.wait_ge(S("swk_ready"), 1)
                srcs = (bh[:, m], kh[:, m], xm[:, 4 + m, 0:SEQ].rearrange("p (c t) -> p c t", t=CH), ar[:, m, :, 0, :])
                for n, v in enumerate(srcs):
                    for c in range(NCH):
                        for g in range(2):
                            h = slice(g * HD, (g + 1) * HD)
                            ins = pe.matmul(ps[h, n, c * CH:(c + 1) * CH], v[h, c, :], ident[h, h], start=True,
                                            stop=True)
                    ins.then_inc(S("stack_t"), 1)
                for n, v in enumerate((bt, kt)):
                    for c in range(NCH):
                        for g in range(2):
                            h = slice(g * HD, (g + 1) * HD)
                            ins = pe.matmul(ps[h, 4 + 2 * n + c // 4, c % 4 * P:(c % 4 + 1) * P], v[h, m, c, :],
                                            ar[h, m, c].rearrange("p s t -> p (s t)"), start=True, stop=True)
                    ins.then_inc(S("mat_mm"), 1)
                for n in range(6):
                    for q in range(2):
                        if n == 0:
                            pe.wait_ge(S("mats_ready"), m + 1)
                            pe.wait_ge(S("stack_out"), 4 * (m + 1))
                        else:
                            pe.wait_ge(S("x_ready"), 12 * m + 2 * (n - 1) + q + 1)
                        for c in range(4 * q, 4 * q + 4):
                            ins = pe.matmul(ps[:, q, c % 4 * P:(c % 4 + 1) * P], mats[:, 0, c, :],
                                            ident if n == 0 else xi[:, c, :], start=True, stop=True)
                        ins.then_inc(S("y_mm"), 1)
                    if n == 0:
                        continue
                    for q in range(2):
                        pe.wait_ge(S("y_masked"), 12 * m + 2 * n + q + 1)
                        for c in range(4 * q, 4 * q + 4):
                            s = slice(c % 4 * P, (c % 4 + 1) * P)
                            pe.matmul(ps[:, 2 + q, s], xT[:, c, :], yy[:, c, :], start=True, stop=True)
                        for c in range(4 * q, 4 * q + 4):
                            s = slice(c % 4 * P, (c % 4 + 1) * P)
                            ins = pe.matmul(ps[:, 4 + q, s], yy[:, c, :], xT[:, c, :], start=True, stop=True)
                        ins.then_inc(S("dx_mm"), 1)
                for c in range(NCH):
                    ins = pe.matmul(ps[:, 6, c * CH:(c + 1) * CH], mats[:, 2, c, :], vst_[:, m, c, :],
                                    start=True, stop=True)
                ins.then_inc(S("akv_mm"), 1)
                pe.wait_ge(S("akv_out"), m + 1)
                pe.wait_ge(S("x_ready"), 12 * (m + 1))
                for c in range(NCH):
                    ins = pe.matmul(ps[:, c // 4, c % 4 * P:(c % 4 + 1) * P], xT[:, c, :],
                                    ag[:, c].rearrange("p s n -> p (s n)"), start=True, stop=True)
                ins.then_inc(S("wu_mm"), 1)
                pe.wait_ge(S("wu_out"), m + 1)
                for c in range(NCH):
                    for g in range(2):
                        h = slice(g * HD, (g + 1) * HD)
                        s = slice(c * CH, (c + 1) * CH)
                        pe.matmul(ps[h, 2, s], wu[h, c, 0, :], bst[h, m, c, :], start=True, stop=True)
                        pe.matmul(ps[h, 3, s], bst[h, m, c, :], wu[h, c, 1, :], start=True, stop=False)
                        pe.matmul(ps[h, 3, s], kst[h, m, c, :], vst_[h, m, c, :], start=False, stop=True)
                        ins = pe.matmul(ps[h, 4, s], wu[h, c, 0, :], mats[h, 1, c, g * CH:(g + 1) * CH],
                                        start=True, stop=True)
                ins.then_inc(S("trans_mm"), 1)
                for c in range(NCH):
                    pe.wait_ge(S("st_ready"), (NCH + 1) * m + c + 1)
                    for g in range(2):
                        h = slice(g * HD, (g + 1) * HD)
                        ins = pe.matmul(ps[h, 5, c * CH:(c + 1) * CH], gT[h, c, :], st[h, c, :], start=True, stop=True)
                    ins.then_inc(S("st_mm"), 1)
                    for g in range(2):
                        h = slice(g * HD, (g + 1) * HD)
                        s = slice(c * CH, (c + 1) * CH)
                        pe.matmul(ps[h, 7, s], st[h, c, :], rwt[h, c, :], start=True, stop=False)
                        pe.matmul(ps[h, 7, s], wu[h, c, 1, :], mats[h, 1, c, g * CH:(g + 1) * CH], start=False,
                                  stop=False)
                        ins = pe.matmul(ps[h, 7, s], vst_[h, m, c, :], mats[h, 3, c, g * CH:(g + 1) * CH],
                                        start=False, stop=True)
                ins.then_inc(S("o_mm"), 1)
                pe.wait_ge(S("st_ready"), (NCH + 1) * (m + 1))
                pe.transpose(ps[0:64, 6, 0:P], st[:, NCH, :], ident).then_inc(S("swk_t"), 1)

        def act_rw_chunks(act, T, link):
            for m in range(2):
                for n, dst in enumerate((bst[:, m], kst[:, m], vst_[:, m], ag[:, :, 0, :])):
                    act.wait_ge(S("stack_t"), 4 * m + n + 1)
                    act.activation(dst, ps[:, n, :].rearrange("p (c n) -> p c n", c=NCH), ACT.Copy)\
                        .then_inc(S("stack_out"), 1)
                act.wait_ge(S("akv_mm"), m + 1)
                act.activation(ag[:, :, 1, :], ps[:, 6, :].rearrange("p (c n) -> p c n", c=NCH), ACT.Copy)\
                    .then_inc(S("akv_out"), 1)
                act.wait_ge(S("wu_mm"), m + 1)
                act.activation(wdn[:, 2048:3072].rearrange("p (x n) -> p x n", x=2), ps[:, 0:2, :], ACT.Copy)\
                    .then_inc(S("wu_out"), 1)
                act.wait_ge(S("trans_mm"), m + 1)
                act.activation(hh, ps[:, 3, :].rearrange("p (c n) -> p c n", c=NCH), ACT.Copy)\
                    .then_inc(S("hh_out"), 1)
                act.wait_ge(S("o_mm"), m + 1)
                act.activation(oT[:, m, 0:SEQ], ps[:, 7, :], ACT.Copy).then_inc(S("o_out"), 1)
                act.wait_ge(S("swk_t"), m + 1)
                if m:
                    act.wait_ge(S("swk_free"), m)
                act.activation(swk, ps[0:64, 6, 0:P], ACT.Copy).then_inc(S("swk_ready"), 1)

        def pool_rwkv(pool, T, link):
            pool.wait_ge(*stage("dec_o"))
            link(pool.memset(fT[:, 0:4096], 0.0))
            pool.sem_inc(reach("mats_zero"), 1)

        def dve_rw_chunks(dve, T, link):
            dve.wait_ge(*stage("mats_zero"))
            masks = (cst[:, C_STR:C_STR + P], cst[:, C_INC:C_INC + P])
            for m in range(2):
                if m:
                    dve.wait_ge(S("o_mm"), m)
                for n in range(2):
                    dve.wait_ge(S("mat_mm"), 2 * m + n + 1)
                    src = ps[:, 4 + 2 * n:6 + 2 * n, :].rearrange("p b (c s t) -> p (b c) s t", s=2, t=CH)
                    for s in range(2):
                        for g in range(2):
                            h = slice(g * HD, (g + 1) * HD)
                            mask = masks[s][h, g * CH:(g + 1) * CH].unsqueeze(1).broadcast_to((HD, NCH, CH))
                            ins = dve.tensor_tensor(mats[h, 2 * n + s, :, g * CH:(g + 1) * CH], src[h, :, s, :], mask,
                                                    ALU.mult)
                    link(ins)
                dve.sem_inc(S("mats_ready"), 1)
                for q in range(2):
                    c4 = slice(4 * q, 4 * q + 4)
                    link(dve.tensor_tensor(xT[:, c4], mats[:, 0, c4], bc4(cst[:, C_LT1:C_LT1 + P], 4), ALU.mult))
                    link(dve.tensor_tensor(xT[:, c4], xT[:, c4], bc4(ident, 4), ALU.add))
                for n in range(6):
                    for q in range(2):
                        c4 = slice(4 * q, 4 * q + 4)
                        y4 = ps[:, q, :].rearrange("p (c n) -> p c n", c=4)
                        dve.wait_ge(S("y_mm"), 12 * m + 2 * n + q + 1)
                        dve.tensor_tensor(yy[:, c4], y4, bc4(levels(n), 4), ALU.mult).then_inc(S("y_masked"), 1)
                        if n == 0:
                            dve.wait_ge(S("y_masked"), 12 * m + q + 1)
                            dve.tensor_tensor(xi[:, c4], yy[:, c4], bc4(ident, 4), ALU.add).then_inc(S("x_ready"), 1)
                    if n == 0:
                        continue
                    for q in range(2):
                        c4 = slice(4 * q, 4 * q + 4)
                        dve.wait_ge(S("dx_mm"), 10 * m + 2 * (n - 1) + q + 1)
                        dx = ps[:, 2 + q, :].rearrange("p (c n) -> p c n", c=4)
                        dxT = ps[:, 4 + q, :].rearrange("p (c n) -> p c n", c=4)
                        link(dve.tensor_tensor(xi[:, c4], xi[:, c4], dx, ALU.add))
                        dve.tensor_tensor(xT[:, c4], xT[:, c4], dxT, ALU.add).then_inc(S("x_ready"), 1)
                e = pend[:, m].unsqueeze(2).broadcast_to((P, NCH, HD))
                link(dve.tensor_tensor(gT, i2.unsqueeze(1).broadcast_to((P, NCH, HD)), e, ALU.mult))
                dve.wait_ge(S("trans_mm"), m + 1)
                link(dve.tensor_tensor(gT, gT, ps[:, 2, :].rearrange("p (c n) -> p c n", c=NCH), ALU.add))
                link(dve.tensor_tensor(rwt, ar[:, m, :, 1, :], ps[:, 4, :].rearrange("p (c n) -> p c n", c=NCH),
                                       ALU.add))
                dve.memset(st[:, 0, :], 0.0).then_inc(S("st_ready"), 1)
                dve.wait_ge(S("hh_out"), m + 1)
                for c in range(NCH):
                    dve.wait_ge(S("st_mm"), NCH * m + c + 1)
                    dve.tensor_tensor(st[:, c + 1, :], ps[:, 5, c * CH:(c + 1) * CH], hh[:, c, :], ALU.add)\
                        .then_inc(S("st_ready"), 1)
                dve.wait_ge(S("st_ready"), (NCH + 1) * (m + 1))

        def pe_rw_out(pe, T):
            pe.wait_ge(S("o_out"), 2)
            pe.wait_ge(S("swk_ready"), 2)
            for m in range(2):
                ins = mm_tokens(pe, 2 * m, bones, oT[:, m, :], True, True)
            ins.then_inc(S("gmean"), 1)
            pe.wait_ge(S("gsq"), 1)
            for m in range(2):
                ins = mm_tokens(pe, 4 + 2 * m, bones, tt[:, m, :], True, True)
            ins.then_inc(S("gvar"), 1)
            pe.wait_ge(*stage("bonus_in"))
            for m in range(2):
                ins = mm_tokens(pe, 2 * m, bones, bb[:, m, :], True, True)
            ins.then_inc(S("bonus_mm"), 1)
            pe.wait_ge(S("gsq"), 2)
            for m in range(2):
                ins = mm_tokens(pe, 4, ones, tt[:, m, :], m == 0, m == 1)
            ins.then_inc(S("gvar"), 1)

        def act_rw_out(act, T, link):
            act.wait_ge(*stage("g_centered"))
            link(act.activation(tt, oT, ACT.Square))
            act.sem_inc(S("gsq"), 1)
            act.wait_ge(S("gvar"), 1)
            for m in range(2):
                ins = act.activation(halves(nkk[:, m, :]), pair(4 + 2 * m), ACT.Sqrt, scale=1 / HD,
                                     bias=cst[:, C_EPS + 2:C_EPS + 3])
            link(ins)
            act.sem_inc(S("groot"), 1)
            act.wait_ge(*stage("oc_ready"))
            link(act.activation(tt, oT, ACT.Square))
            act.sem_inc(S("gsq"), 1)
            act.wait_ge(S("gvar"), 2)
            act.activation(halves(aa[:, 0, :]), pair(4), ACT.Sqrt, scale=1 / 256, bias=cst[:, C_EPS:C_EPS + 1])\
                .then_inc(S("groot"), 1)

        def dve_rw_out(dve, T, link):
            dve.wait_ge(S("gmean"), 1)
            for m in range(2):
                link(dve.scalar_tensor_tensor(out=halves(oT[:, m, :]), in0=pair(2 * m), scalar=-1 / HD,
                                              in1=halves(oT[:, m, :]), op0=ALU.mult, op1=ALU.add))
            dve.sem_inc(reach("g_centered"), 1)
            link(dve.tensor_tensor(bb, xm[:, 0:2, :], xm[:, 2:4, :], ALU.mult))
            for m in range(2):
                link(dve.tensor_scalar(bb[:, m, :], bb[:, m, :], vec[:, V_RK + m:V_RK + m + 1], None, ALU.mult))
            dve.sem_inc(reach("bonus_in"), 1)
            dve.wait_ge(S("groot"), 1)
            link(dve.reciprocal(nkk, nkk))
            link(dve.tensor_tensor(oT, oT, nkk, ALU.mult))
            dve.wait_ge(S("bonus_mm"), 1)
            for m in range(2):
                link(dve.tensor_scalar(oT[:, m, :], oT[:, m, :], vec[:, V_LW + m:V_LW + m + 1],
                                       vec[:, V_LB + m:V_LB + m + 1], ALU.mult, ALU.add))
                link(dve.tensor_tensor(halves(wdec[:, m, :]), pair(2 * m), halves(xm[:, 4 + m, :]), ALU.mult))
            link(dve.tensor_tensor(oT, oT, wdec, ALU.add))
            link(dve.tensor_tensor(oT, oT, gate, ALU.mult))
            dve.sem_inc(reach("oc_ready"), 1)
            dve.wait_ge(S("groot"), 2)
            link(dve.reciprocal(aa[:, 0, :], aa[:, 0, :]))
            for m in range(2):
                link(dve.scalar_tensor_tensor(out=merged[:, 6 + m, :], in0=oT[:, m, :],
                                              scalar=vec[:, V_GRP + 6 + m:V_GRP + 7 + m], in1=aa[:, 0, :],
                                              op0=ALU.mult, op1=ALU.mult))
            dve.sem_inc(reach("merged_ready"), 1)

        def sp_wout(sp, T, l):
            for m in range(KC):
                if m < 3:
                    sp.wait_ge(S("p_ready"), 13 + m)
                else:
                    sp.wait_ge(S("f_ready"), KC + m - 2)
                w = a["w_out"][bass.ds(l, 1)]
                for g in range(2):
                    sp.dma_start(win[g * HD:(g + 1) * HD, m % 3, 0:4, :],
                                 w[:, g * 256:(g + 1) * 256, m * P:(m + 1) * P].rearrange("a (t d) n -> d (a t) n", d=HD))\
                        .then_inc(S(f"win_full{m % 3}"), 16)
                sp.dma_start(win[:, m % 3, 4:8, :], w[:, 512:1024, m * P:(m + 1) * P]
                             .rearrange("a (k p) n -> p (a k) n", p=P)).then_inc(S(f"win_full{m % 3}"), 16)

        def pe_wout(pe, T):
            for m in range(KC):
                pe_out_chunk(pe, T, m, S(f"win_full{m % 3}"), 160 + 48 * (m // 3 + 1), win[:, m % 3], merged, KC)
                if m:
                    pe_sumsq(pe, T, m - 1, False)
            pe_sumsq(pe, T, KC - 1, True)

        def sp_mixer(sp, T, l):
            sp_project(sp, T, l)
            sp_compress_in(sp, T, l)
            sp_rows_out(sp, T, l)
            sp_state_out(sp, T, l)
            sp_compress_w(sp, T, l, 0)
            sp_compress_w(sp, T, l, 1)
            sp_decode_in(sp, T, l)
            sp_rwkv(sp, T, l)
            sp.wait_ge(S("rows_st"), 16 * 14)
            sp.sem_inc(S("rows_free"), 1)
            sp_wout(sp, T, l)

        def pe_mixer(pe, T):
            pe_project(pe, T)
            pe_conv_state(pe, T)
            pe_compress(pe, T, 0)
            pe_compress(pe, T, 1)
            pe_cmp_rows(pe, T)
            pe_conv_norm(pe, T)
            pe_prompt(pe, T)
            pe_prompt_out(pe, T)
            pe_decode(pe, T)
            pe_rw_in(pe, T)
            pe_rw_decode(pe, T)
            pe_rw_chunks(pe, T)
            pe_rw_out(pe, T)
            pe.wait_ge(*stage("merged_ready"))
            pe_wout(pe, T)

        def act_mixer(act, T, link):
            act_project(act, T, link)
            act_conv_state(act, T, link)
            act_gates(act, T, link)
            act_compress(act, T, link, 0)
            act_compress(act, T, link, 1)
            act_conv_norm(act, T, link)
            act_prompt(act, T, link)
            act_decode(act, T, link)
            act_rw_in(act, T, link)
            act_rw_chunks(act, T, link)
            act_rw_out(act, T, link)
            act.wait_ge(S("rows_free"), 1)
            act_out(act, T)

        def dve_mixer(dve, T, link):
            dve_conv(dve, T, link)
            dve_rope(dve, T, link)
            dve_compress(dve, T, link, 0)
            dve_compress(dve, T, link, 1)
            dve_cmp_rows(dve, T, link)
            dve_conv_norm(dve, T, link)
            dve_prompt(dve, T, link)
            dve_decode(dve, T, link)
            dve_rw_in(dve, T, link)
            dve_rw_decode(dve, T, link)
            dve.sem_inc(reach("dec_o"), 1)
            dve_rw_decay(dve, T, link)
            dve_rw_chunks(dve, T, link)
            dve_rw_out(dve, T, link)

        def pool_mixer(pool, T, l, link):
            pool_rope(pool, T, link)
            pool_compress(pool, T, link)
            pool_qz(pool, T, link)
            pool_rwkv(pool, T, link)

        @block.sync
        def _(sp):
            T = Tally()
            sp_first(sp, T)
            with sp.Fori(0, DEPTH) as l:
                boundary(sp, l, T)
                sp_vectors(sp, T, l)
                for c in range(3):
                    sp_win_chunk(sp, l, c)
                sp_ffn(sp, T, l, 0)
                sp_down(sp, T, l, 0)
                sp_mixer(sp, T, l)
                sp_ffn(sp, T, l, 1)
                sp_down(sp, T, l, 1)
            sp_last(sp, T)

        @block.tensor
        def _(pe):
            T = Tally()
            pe_first(pe, T)
            with pe.Fori(0, DEPTH) as l:
                boundary(pe, l, T)
                pe_vectors(pe, T)
                pe_prenorm(pe, T)
                pe_ffn(pe, T, 0)
                pe_down(pe, T, 0)
                pe_prenorm(pe, T)
                pe_mixer(pe, T)
                pe_prenorm(pe, T)
                pe_ffn(pe, T, 1)
                pe_down(pe, T, 1)
                pe.wait_ge(S("h_ready"), KC * 3)
            pe_last(pe, T)

        @block.scalar
        def _(act):
            T = Tally()
            act_first(act, T)
            with act.Fori(0, DEPTH) as l:
                boundary(act, l, T)
                link = chain(act, "act_step", T)
                act.sem_inc(S("f_used"), 2)
                act_prenorm(act, T, 0)
                act_ffn(act, T, 0)
                act_out(act, T)
                act_prenorm(act, T, 1)
                act_mixer(act, T, link)
                act_prenorm(act, T, 2)
                act_ffn(act, T, 1)
                act_out(act, T)
            act_last(act, T)

        @block.vector
        def _(dve):
            T = Tally()
            dve_first(dve, T)
            with dve.Fori(0, DEPTH) as l:
                boundary(dve, l, T)
                link = chain(dve, "dve_step", T)
                dve.sem_inc(S("gu_used"), 2)
                dve_vectors(dve, T, link)
                dve_prenorm(dve, T, 0)
                dve_ffn(dve, T, 0)
                dve_postnorm(dve, T, 1)
                dve_prenorm(dve, T, 2)
                dve_mixer(dve, T, link)
                dve_postnorm(dve, T, 3)
                dve_prenorm(dve, T, 4)
                dve_ffn(dve, T, 1)
                dve_postnorm(dve, T, 5)

        @block.gpsimd
        def _(pool):
            T = Tally()
            for name in ("pool_step",):
                S(name)
            with pool.Fori(0, DEPTH) as l:
                boundary(pool, l, T)
                link = chain(pool, "pool_step", T)
                known = len(sems)
                pool_mixer(pool, T, l, link)
                assert known == len(sems), "a semaphore that the boundary doesn't clear"


_OUTS = [
    ("y_prompt", (1, SEQ, D)), ("y_sample", (DEC, 1, D)),
    *[(f"p_{n}", (DEPTH, 1, SEQ, NKV, HD)) for n in ("cmp_k", "cmp_v", "sel_k", "sel_v", "win_k", "win_v")],
    ("p_conv", (DEPTH, 1, CW - 1, 256)), ("p_shift", (DEPTH, 1, RWC)), ("p_wkv", (DEPTH, 1, 4, HD, HD)),
    *[(f"s_{n}", (DEPTH, DEC, 1, NKV, HD)) for n in ("cmp_k", "cmp_v", "sel_k", "sel_v")],
    *[(f"s_{n}", (DEPTH, DEC, PAST, NKV, HD)) for n in ("win_k", "win_v")],
    ("s_conv", (DEPTH, DEC, CW - 1, 256)), ("s_shift", (DEPTH, DEC, RWC)), ("s_wkv", (DEPTH, DEC, 4, HD, HD)),
]
def kernel(**inputs):
    import concourse.bacc as bacc
    from concourse.bass_utils import run_bass_kernel_spmd

    nc = bacc.Bacc("TRN2", target_bir_lowering=False, num_devices=1)
    const, rope = constants()
    arrays, a, o = {}, {}, {}
    for name, v in {**inputs, "const": const, "rope": rope}.items():
        v = np.ascontiguousarray(v)
        arrays[f"in_{name}"] = v
        a[name] = nc.dram_tensor(f"in_{name}", v.shape, mybir.dt.from_np(v.dtype), kind="ExternalInput").ap()
    for name, shape in _OUTS:
        o[name] = nc.dram_tensor(f"out_{name}", shape, F32, kind="ExternalOutput").ap()
    trunk(nc, a, o)
    r = run_bass_kernel_spmd(nc, [arrays], core_ids=[0])
    return tuple(r.results[0][f"out_{name}"] for name, _ in _OUTS)
```

```python
from contextlib import ExitStack

import concourse.bass as bass
from concourse import mybir
import numpy as np

F32 = mybir.dt.float32
F32R = mybir.dt.float32r
I32 = mybir.dt.int32
ALU = mybir.AluOpType
ACT = mybir.ActivationFunctionType
X = mybir.AxisListType.X

P = 128
DEPTH, D, SEQ, DEC = 2, 1024, 512, 8
TOK = SEQ + DEC
HALF = TOK // 2
KC = D // P
DFF = 2816
FC = DFF // P
HD = 64
NQ, NKV = 8, 2
QT = SEQ // P
PAST, PAGE = 256, 128
NPAGE = PAST // PAGE
CTX = PAST + 1
CB, CS = 32, 16
NCMP = (SEQ - CB) // CS + 1
NCMP_D = (CTX - CB) // CS + 1
XCOLS = SEQ + DEC * PAST
NWIN = (XCOLS + CB - CB) // CS + 1
CW = 31
CH = 64
NCH = SEQ // CH
RWC = 896
COL_ROWS = 512
N_ROWS = 6 * P + 3 * NQ
COL_T = COL_ROWS + N_ROWS
NEG = -1e30
SCALE = HD ** -0.5
RMS_EPS, LN_EPS, GN_EPS = 1e-6, 1e-5, 64e-5

C_ID, C_ONES, C_BONES, C_ROT, C_CAUS, C_CMPM, C_DMASK, C_LVL, C_LT1, C_STR, C_INC, C_COS, C_SIN, C_EPS, C_END = (
    int(v) for v in np.cumsum([0, 128, 128, 128, 128, 128, QT * NCMP, DEC, 6 * 128, 128, 128, 128, 40, 40, 8]))


def constants():
    c = np.zeros((P, C_END), np.float32)
    i = np.arange(P)
    c[:, C_ID:C_ID + P] = np.eye(P)
    c[:, C_ONES:C_ONES + P] = 1
    same = i[:, None] // 64 == i[None, :] // 64
    c[:, C_BONES:C_BONES + P] = same
    rot = np.zeros((P, P), np.float32)
    for b in (0, 64):
        for e in range(8):
            rot[b + 8 + e, b + e] = -1
            rot[b + e, b + 8 + e] = 1
    c[:, C_ROT:C_ROT + P] = rot
    c[:, C_CAUS:C_CAUS + P] = np.where(i[None, :] <= i[:, None], 0, NEG)
    end = np.arange(NCMP) * CS + CB - 1
    for t in range(QT):
        c[:, C_CMPM + t * NCMP:C_CMPM + (t + 1) * NCMP] = np.where(end[None, :] <= (t * P + i)[:, None], 0, NEG)
    c[:, C_DMASK:C_DMASK + DEC] = np.where(np.arange(DEC)[None, :] == (i // NQ)[:, None], 0, NEG)
    for n in range(6):
        m = 1 << n
        c[:, C_LVL + n * P:C_LVL + (n + 1) * P] = (
            same & (i[:, None] // (2 * m) == i[None, :] // (2 * m))
            & (i[:, None] // m % 2 == 1) & (i[None, :] // m % 2 == 0))
    c[:, C_LT1:C_LT1 + P] = c[:, C_LVL:C_LVL + P].T
    c[:, C_STR:C_STR + P] = same & (i[:, None] < i[None, :])
    c[:, C_INC:C_INC + P] = same & (i[:, None] <= i[None, :])
    inv = np.float32(500000.0) ** (-np.arange(8, dtype=np.float32) * np.float32(2.0) / np.float32(16))
    pos = np.arange(5 * P, dtype=np.float32)
    pos[SEQ:] = PAST
    ang = (pos[:, None] * inv[None, :].astype(np.float32)).astype(np.float32)
    c[:, C_COS:C_COS + 40] = np.cos(ang).reshape(5, P, 8).transpose(1, 0, 2).reshape(P, 40)
    c[:, C_SIN:C_SIN + 40] = np.sin(ang).reshape(5, P, 8).transpose(1, 0, 2).reshape(P, 40)
    c[:, C_EPS:C_EPS + 3] = (RMS_EPS, LN_EPS, GN_EPS)
    rope = np.zeros((P, 2, TOK), np.float32)
    rope[:, 0] = 1
    for b in (0, 64):
        for o in (0, 8):
            rope[b + o:b + o + 8, 0] = np.cos(ang[:TOK]).T
            rope[b + o:b + o + 8, 1] = np.sin(ang[:TOK]).T
    return c, rope


V_NORM, V_GRP, V_CB, V_CLG, V_CLB, V_PWB, V_MU, V_W0, V_A0, V_KK, V_KA, V_RK, V_LW, V_LB = (
    0, 48, 56, 58, 60, 62, 64, 71, 73, 75, 77, 79, 81, 83)
V_END = 85
V_CW = 88


UK = 8
U_UP = (0, 98)
U_DN = (44, 142)
U_IN, U_OUT, U_END = 68, 90, 166
DN_K = ((0, 8), (8, 8), (16, 6))
MILESTONES = {
    "dve_stage": ("conv_ready", "vc_ready", "c_centered", "c_scaled", "ob_ready", "oacc_ready",
                  "on_ready", "oD_ready", "attn_done", "xm_ready", "kk_raw", "sd_new", "dec_o",
                  "chunks_ready", "g_centered", "bonus_in", "oc_ready", "merged_ready"),
    "act_stage": ("state_rows", "gates_ready", "c_act", "oroot", "lora_act", "w_ready"),
    "pool_stage": ("wc_zero", "qz_ready", "mats_zero"),
}


class Tally:

    def __init__(self):
        self.n = {}

    def up(self, name, k=1):
        self.n[name] = self.n.get(name, 0) + k
        return self.n[name]

    def at(self, name):
        return self.n.get(name, 0)


def trunk(nc, a, o):
    es = ExitStack()
    with es:
        def sb(name, shape, dt=F32):
            return es.enter_context(nc.sbuf_tensor(name, shape, dt))

        sems = {}

        def S(name):
            if name not in sems:
                sems[name] = es.enter_context(nc.semaphore(name))
            return sems[name]

        reached = {}

        def stage(name):
            group = next(g for g, names in MILESTONES.items() if name in names)
            return S(group), MILESTONES[group].index(name) + 1

        def reach(name):
            sem, n = stage(name)
            group = next(g for g, names in MILESTONES.items() if name in names)
            assert reached.get(group, 0) == n - 1, f"{name} is out of order"
            reached[group] = n
            return sem

        layer_end = es.enter_context(nc.semaphore("layer_end"))
        fence = es.enter_context(nc.semaphore("fence"))
        layer_go = es.enter_context(nc.semaphore("layer_go"))

        ps = es.enter_context(nc.psum_tensor("ps", [P, 8, 512], F32))

        def arena(name, words):
            start = nc.sbuf_base
            sb(name, [P, words])
            return start

        def over(name, start, word, shape, dt=F32):
            return nc.alloc_sbuf_tensor_at(name, shape, dt, offset=start + 4 * word)

        hT = sb("hT", [P, KC, TOK])
        at_x = arena("arena_x", 2 * KC * TOK)
        xnH = over("xnH", at_x, 0, [P, KC, TOK], F32R)
        xnL = over("xnL", at_x, KC * TOK, [P, KC, TOK], F32R)
        merged = over("merged", at_x, 0, [P, KC, TOK])
        mid = over("mid", at_x, KC * TOK, [P, KC * TOK])
        at_a = arena("arena_a", 2 * FC * TOK)
        actH = over("actH", at_a, 0, [P, FC, TOK], F32R)
        actL = over("actL", at_a, FC * TOK, [P, FC, TOK], F32R)
        mH = over("mH", at_a, 0, [P, KC, TOK], F32R)
        mL = over("mL", at_a, KC * TOK, [P, KC, TOK], F32R)
        big = over("big", at_a, 0, [P, FC * TOK])
        mix = over("mix", at_a, FC * TOK, [P, FC * TOK])
        fT = sb("fT", [P, KC * TOK])
        at_w = arena("arena_w", 8 * UK * P)
        nat = over("nat", at_w, 0, [P, 4, UK, P])
        wH = over("wH", at_w, 4 * UK * P, [P, 2, UK, P], F32R)
        wL = over("wL", at_w, 6 * UK * P, [P, 2, UK, P], F32R)
        wks = over("wks", at_w, 0, [P, 8 * UK * P])
        cst = sb("cst", [P, C_END])
        vec = sb("vec", [P, 152])
        sq = sb("sq", [P, 2, TOK])
        rstd = sb("rstd", [P, TOK])
        sg = sb("sg", [P, 2, TOK])
        pages = sb("pages", [1, DEC * NPAGE], I32)

        f_v = fT[:, :].rearrange("p (c t) -> p c t", t=TOK)
        proj = mix[:, :].rearrange("p (c t) -> p c t", t=TOK)
        qrT = mid[:, 0:4 * TOK].rearrange("p (c t) -> p c t", t=TOK)
        rows = fT[:, 0:5 * N_ROWS].rearrange("p (i n) -> p i n", n=N_ROWS)
        ident = cst[:, C_ID:C_ID + P]
        ones = cst[:, C_ONES:C_ONES + P]
        bones = cst[:, C_BONES:C_BONES + P]

        def halves(v):
            return v.rearrange("p (h n) -> p h n", h=2)

        def pair(b):
            return ps[:, b:b + 2, 0:HALF]

        def chain(eng, name, tally):
            def link(ins):
                ins.then_inc(S(name), 1)
                eng.wait_ge(S(name), tally.up(name))
            return link

        block = es.enter_context(nc.Block())

        def boundary(eng, l, tally):
            eng.drain().then_inc(layer_end, 1)
            tally.n.clear()
            if eng is nc.gpsimd:
                eng.wait_ge(layer_end, l * 5 + 5)
                eng.sem_inc(fence, 1)
                for name in sorted(sems):
                    eng.sem_clear(sems[name])
                eng.sem_inc(layer_go, 1)
            else:
                eng.wait_ge(layer_go, l + 1)
                eng.sem_inc(fence, 1)

        def mm_tokens(pe, bank, w, x, first, last):
            for h in range(2):
                ins = pe.matmul(ps[:, bank + h, 0:HALF], w, x[:, h * HALF:(h + 1) * HALF], start=first, stop=last)
            return ins

        def act_prenorm(act, T, n):
            for c in range(KC):
                if n:
                    act.wait_ge(S("h_ready"), T.up("h_ready"))
                if T.up("_sq") > 2:
                    act.wait_ge(S("sq_used"), T.at("_sq") - 2)
                act.activation(sq[:, c % 2, :], hT[:, c, :], ACT.Square).then_inc(S("sq_ready"), 1)
            act_rstd(act, T, RMS_EPS, D)

        def act_rstd(act, T, eps, n, src=None, dst=None):
            col = C_EPS + (RMS_EPS, LN_EPS, GN_EPS).index(eps)
            act.wait_ge(S("sq_used"), T.at("_sq"))
            if T.up("_root") > 1:
                act.wait_ge(S("rstd_used"), T.at("_root") - 1)
            act.activation(halves(rstd[:, :]), pair(6), ACT.Sqrt, scale=1.0 / n,
                           bias=cst[:, col:col + 1]).then_inc(S("root_ready"), 1)

        def pe_sumsq(pe, T, c, last, n=KC, mat=None):
            pe.wait_ge(S("sq_ready"), T.up("sq_ready"))
            if c == 0 and T.up("_ss") > 1:
                pe.wait_ge(S("root_ready"), T.at("_ss") - 1)
            ins = mm_tokens(pe, 6, ones if mat is None else mat, sq[:, (T.at("sq_ready") - 1) % 2, :], c == 0, last)
            ins.then_inc(S("sq_used"), 1)

        def pe_prenorm(pe, T):
            for c in range(KC):
                pe_sumsq(pe, T, c, c == KC - 1)

        def dve_recip(dve, T):
            dve.wait_ge(S("root_ready"), T.up("root_ready"))
            dve.reciprocal(rstd[:, :], rstd[:, :]).then_inc(S("dve_rstd"), 1)
            dve.wait_ge(S("dve_rstd"), T.up("dve_rstd"))

        def dve_prenorm(dve, T, n):
            dve_recip(dve, T)
            base = T.at("xn_raw")
            for c in range(KC + 1):
                if c < KC:
                    if base + c >= 2:
                        dve.wait_ge(S("xl_ready"), base + c - 1)
                    dve.scalar_tensor_tensor(out=sg[:, c % 2, :], in0=hT[:, c, :],
                                             scalar=vec[:, V_NORM + n * KC + c:V_NORM + n * KC + c + 1],
                                             in1=rstd[:, :], op0=ALU.mult, op1=ALU.mult).then_inc(S("xn_raw"), 1)
                if c:
                    dve.wait_ge(S("xh_ready"), base + c)
                    dve.tensor_tensor(xnL[:, c - 1, :], sg[:, (c - 1) % 2, :], xnH[:, c - 1, :].bitcast(F32),
                                      ALU.subtract).then_inc(S("xl_ready"), 1)
            T.up("xn_raw", KC)
            dve.wait_ge(S("xl_ready"), base + KC)
            dve.sem_inc(S("rstd_used"), 1)

        def act_xn_split(act, T):
            for c in range(KC):
                act.wait_ge(S("xn_raw"), T.up("xn_raw"))
                act.activation(xnH[:, c, :], sg[:, c % 2, :], ACT.Copy).then_inc(S("xh_ready"), 1)

        def dve_postnorm(dve, T, n):
            dve_recip(dve, T)
            for c in range(KC):
                dve.scalar_tensor_tensor(out=f_v[:, c, :], in0=f_v[:, c, :],
                                         scalar=vec[:, V_NORM + n * KC + c:V_NORM + n * KC + c + 1],
                                         in1=rstd[:, :], op0=ALU.mult, op1=ALU.mult).then_inc(S("fn_ready"), 1)
            dve.wait_ge(S("fn_ready"), T.up("fn_ready", KC))
            dve.sem_inc(S("rstd_used"), 1)

        def pool_residual(pool, T):
            for c in range(KC):
                pool.wait_ge(S("fn_ready"), T.up("fn_ready"))
                pool.tensor_tensor(hT[:, c, :], hT[:, c, :], f_v[:, c, :], ALU.add).then_inc(S("h_ready"), 1)

        T_CV, T_CG, T_Q, T_KC, T_VC, T_KS, T_VS, T_KW, T_VW, T_GT, T_RW = 0, 2, 4, 8, 9, 10, 11, 12, 13, 14, 15
        NPROJ = 22

        def count(n, j):
            return n if j is None else j * 4 + n

        def sp_unit(sp, u, src, nk=UK, j=None):
            if u >= 4 or j is not None:
                sp.wait_ge(S("lo_ready"), count(u - 3, j))
                if j is not None:
                    sp.sem_inc(fence, 1)
            sp.dma_start(nat[:, u % 4, 0:nk, :], src.rearrange("a (k p) n -> p (a k) n", p=P))\
                .then_inc(S(f"nat_full{u % 4}"), 16)

        def landed(u):
            return 16 * sum(2 if U_IN + T_Q <= v < U_IN + T_Q + 4 else 3 if U_OUT <= v < U_OUT + KC else 1
                            for v in range(u % 4, u + 1, 4))

        def act_unit(act, u, nk=UK, j=None):
            act.wait_ge(S(f"nat_full{u % 4}"), landed(u) if j is None else j * 16 + (landed(u + 4) - 16))
            if u >= 2 or j is not None:
                act.wait_ge(S("unit_done"), count(u - 1, j))
            act.activation(wH[:, u % 2, 0:nk, :], nat[:, u % 4, 0:nk, :], ACT.Copy).then_inc(S("hi_ready"), 1)

        def dve_unit(dve, u, nk=UK, j=None):
            dve.wait_ge(S("hi_ready"), count(u + 1, j))
            dve.tensor_tensor(wL[:, u % 2, 0:nk, :], nat[:, u % 4, 0:nk, :], wH[:, u % 2, 0:nk, :].bitcast(F32),
                              ALU.subtract).then_inc(S("lo_ready"), 1)

        def pe_unit(pe, u, bank, xh, xl, k0=0, nk=UK, first=True, last=True, j=None, wait_x=None):
            pe.wait_ge(S("lo_ready"), count(u + 1, j))
            for k in range(nk):
                if wait_x is not None:
                    pe.wait_ge(S(wait_x[0]), wait_x[1] + k + 1)
                for h in range(2):
                    out, t = ps[:, bank + h, 0:HALF], slice(h * HALF, (h + 1) * HALF)
                    pe.matmul(out, wH[:, u % 2, k, :], xh[:, k0 + k, t], start=first and k == 0, stop=False)
                    pe.matmul(out, wH[:, u % 2, k, :], xl[:, k0 + k, t], start=False, stop=False)
                for h in range(2):
                    out, t = ps[:, bank + h, 0:HALF], slice(h * HALF, (h + 1) * HALF)
                    ins = pe.matmul(out, wL[:, u % 2, k, :], xh[:, k0 + k, t], start=False, stop=last and k == nk - 1)
            ins.then_inc(S("unit_done"), 1)

        def dn_units(f):
            return [(U_DN[f] + 3 * m + n, m, k0, nk) for m in range(KC) for n, (k0, nk) in enumerate(DN_K)]

        def size_of(u):
            for f in range(2):
                if U_DN[f] <= u < U_DN[f] + 24:
                    return DN_K[(u - U_DN[f]) % 3][1]
            return UK

        def sp_ffn(sp, T, l, f):
            L = bass.ds(l, 1)

            def chunk(c, u, j=None):
                col = c * P if j is None else bass.ds(j * 2 * P + c * P, P)
                col = slice(c * P, (c + 1) * P) if j is None else col
                for n, w in enumerate((a["ffn_gate"], a["ffn_up"])):
                    sp_unit(sp, u + n, w[L, f, :, col], j=j)
            for c in range(2):
                chunk(c, U_UP[f] + 2 * c)
            with sp.Fori(1, FC // 2) as j:
                for c in range(2):
                    chunk(c, U_UP[f] + 2 * c, j=j)
            for u, m, k0, nk in dn_units(f):
                sp_unit(sp, u, a["ffn_down"][L, f, k0 * P:(k0 + nk) * P, m * P:(m + 1) * P], nk)

        def pe_ffn(pe, T, f):
            base, xbase = f * FC, (0, 2 * KC)[f]

            def chunk(c, j=None, wait_x=None):
                pe.wait_ge(S("gu_used"), base + c + 1 if j is None else j * 2 + (base + c + 1))
                for n in range(2):
                    pe_unit(pe, U_UP[f] + 2 * c + n, 4 * (c % 2) + 2 * n, xnH, xnL, j=j,
                            wait_x=wait_x if n == 0 else None)
            for c in range(2):
                chunk(c, wait_x=("xl_ready", xbase) if c == 0 else None)
            with pe.Fori(1, FC // 2) as j:
                for c in range(2):
                    chunk(c, j=j)

        def act_ffn(act, T, f):
            base = f * FC
            with act.Fori(0, FC // 2) as j:
                for c in range(2):
                    for n in range(2):
                        act_unit(act, U_UP[f] + 2 * c + n + 2, j=j)
                    act.wait_ge(S("unit_done"), count(U_UP[f] + 2 * c + 2, j))
                    act.activation(halves(sg[:, c, :]), pair(4 * c), ACT.Silu).then_inc(S("sg_ready"), 1)
                    act.wait_ge(S("gm_ready"), j * 2 + (base + c + 1))
                    act.activation(actH[:, bass.ds(j * 2 + c, 1), :], sg[:, c:c + 1, :], ACT.Copy)\
                        .then_inc(S("ah_ready"), 1)

        def dve_ffn(dve, T, f):
            base = f * FC
            with dve.Fori(0, FC // 2) as j:
                for c in range(2):
                    for n in range(2):
                        dve_unit(dve, U_UP[f] + 2 * c + n + 2, j=j)
                    dve.wait_ge(S("sg_ready"), j * 2 + (base + c + 1))
                    dve.tensor_tensor(halves(sg[:, c, :]), halves(sg[:, c, :]), pair(4 * c + 2), ALU.mult)\
                        .then_inc(S("gm_ready"), 1)
                    dve.wait_ge(S("ah_ready"), j * 2 + (base + c + 1))
                    dve.tensor_tensor(actL[:, bass.ds(j * 2 + c, 1), :], sg[:, c:c + 1, :],
                                      actH[:, bass.ds(j * 2 + c, 1), :].bitcast(F32), ALU.subtract)\
                        .then_inc(S("gu_used"), 1)

        def pe_down(pe, T, f):
            pe.wait_ge(S("gu_used"), (f + 1) * FC + 2)
            for u, m, k0, nk in dn_units(f):
                if k0 == 0:
                    pe.wait_ge(S("f_used"), T.up("f_used"))
                pe_unit(pe, u, 2 * (m % 2), actH, actL, k0, nk, k0 == 0, k0 + nk == FC)
                if k0 == 8 and m:
                    pe_sumsq(pe, T, m - 1, False)
            pe_sumsq(pe, T, KC - 1, True)

        def dve_out(dve, T, units):
            for u in units:
                if u + 2 < U_END:
                    dve_unit(dve, u + 2, size_of(u + 2))

        def act_out(act, T, units, step):
            for m in range(KC):
                for u in units[m * step:(m + 1) * step]:
                    if u + 2 < U_END:
                        act_unit(act, u + 2, size_of(u + 2))
                act.wait_ge(S("unit_done"), u + 1)
                if T.up("_sq") > 2:
                    act.wait_ge(S("sq_used"), T.at("_sq") - 2)
                act.activation(halves(f_v[:, m, :]), pair(2 * (m % 2)), ACT.Copy).then_inc(S("f_out"), 1)
                act.activation(halves(sq[:, m % 2, :]), pair(2 * (m % 2)), ACT.Square).then_inc(S("sq_ready"), 1)
                act.wait_ge(S("f_out"), T.up("f_out"))
                act.wait_ge(S("sq_ready"), T.at("_sq"))
                act.sem_inc(S("f_used"), 1)
            act_rstd(act, T, RMS_EPS, D)

        xin = big[:, 0:QT * D].rearrange("p (i n) -> p i n", n=D)
        xin_d = big[0:DEC, QT * D:(QT + 1) * D]
        vst = sb("vst", [P, 2, P])

        def sp_first(sp, T):
            sp.dma_start(cst[:, :], a["const"]).then_inc(S("const_in"), 16)
            sp.dma_start(xin, a["x_prompt"].rearrange("b (i p) n -> p (b i) n", p=P)).then_inc(S("x_in"), 16)
            sp.dma_start(xin_d, a["x_sample"].rearrange("b t n -> (b t) n")).then_inc(S("x_in"), 16)
            sp.dma_start(pages[:, :], a["page_table"].rearrange("(o b) n -> o (b n)", o=1)).then_inc(S("page_in"), 16)
            for name, n in (("const_in", 1), ("x_in", 2), ("page_in", 1)):
                sp.wait_ge(S(name), 16 * n)

        def pe_first(pe, T):
            pe.wait_ge(S("const_in"), 16)
            pe.wait_ge(S("x_in"), 32)
            for c in range(KC):
                b = 2 * (c % 2)
                if c >= 2:
                    pe.wait_ge(S("x_rows_out"), c - 1)
                    pe.wait_ge(S("x_dec_out"), c - 1)
                for i in range(QT):
                    pe.transpose(ps[:, b, i * P:(i + 1) * P], xin[:, i, c * P:(c + 1) * P], ident)
                pe.transpose(ps[:, b + 1, 0:DEC], xin_d[:, c * P:(c + 1) * P], ident[0:DEC, 0:DEC]).then_inc(S("x_t"), 1)

        def act_first(act, T):
            for c in range(KC):
                act.wait_ge(S("x_t"), c + 1)
                act.activation(hT[:, c, 0:SEQ], ps[:, 2 * (c % 2), :], ACT.Copy).then_inc(S("x_rows_out"), 1)

        def dve_first(dve, T):
            for c in range(KC):
                dve.wait_ge(S("x_t"), c + 1)
                dve.tensor_copy(hT[:, c, SEQ:TOK], ps[:, 2 * (c % 2) + 1, 0:DEC]).then_inc(S("x_dec_out"), 1)

        def sp_vectors(sp, T, l):
            L = bass.ds(l, 1)

            def put(row, n, src, slot=0):
                sp.dma_start(vst[row:row + n, slot, :], src).then_inc(S("vec_in"), 16)

            put(V_NORM, 6 * KC, a["norms"][L].rearrange("a n (c p) -> (a n c) p", p=P))
            for g in range(2):
                sp.dma_start(vst[V_GRP:V_GRP + 4, 0, g * HD:(g + 1) * HD],
                               a["grp_norm"][L, g * 256:(g + 1) * 256].rearrange("a (t d) -> (a t) d", d=HD))\
                    .then_inc(S("vec_in"), 16)
            put(V_GRP + 4, 4, a["grp_norm"][L, 512:1024].rearrange("a (c p) -> (a c) p", p=P))
            for row, n, name in ((V_CB, 2, "conv_b"), (V_CLG, 2, "conv_ln_g"), (V_CLB, 2, "conv_ln_b"),
                                 (V_PWB, 2, "conv_pw_b"), (V_MU, 7, "rw_mu"), (V_W0, 2, "rw_w0"), (V_A0, 2, "rw_a0"),
                                 (V_KK, 2, "rw_kk"), (V_KA, 2, "rw_ka"), (V_LW, 2, "rw_ln_w"), (V_LB, 2, "rw_ln_b")):
                put(row, n, a[name][L].rearrange("a (c p) -> (a c) p", p=P))
            put(V_RK, 2, a["rw_rk"][L].rearrange("a (c h) d -> (a c) (h d)", c=2))
            put(0, 2 * CW, a["conv_w"][L].rearrange("a j (c p) -> (a j c) p", p=P), slot=1)

        def pe_vectors(pe, T):
            pe.wait_ge(S("vec_in"), 17 * 16)
            pe.transpose(ps[:, 0, 0:V_END], vst[0:V_END, 0, :], ident[0:V_END, 0:V_END])
            pe.transpose(ps[:, 0, V_CW:V_CW + 2 * CW], vst[0:2 * CW, 1, :], ident[0:2 * CW, 0:2 * CW])\
                .then_inc(S("vec_t"), 1)

        def dve_vectors(dve, T, link):
            dve.wait_ge(S("vec_t"), 1)
            link(dve.tensor_copy(vec[:, 0:V_END], ps[:, 0, 0:V_END]))
            link(dve.tensor_copy(vec[:, V_CW:V_CW + 2 * CW], ps[:, 0, V_CW:V_CW + 2 * CW]))
            for n in (1, 5):
                link(dve.tensor_scalar(vec[:, V_NORM + n * KC:V_NORM + (n + 1) * KC],
                                       vec[:, V_NORM + n * KC:V_NORM + (n + 1) * KC], 0.5, None, ALU.mult))

        def pe_last(pe, T):
            for i in range(QT + 1):
                m = P if i < QT else DEC
                if i >= 2:
                    pe.wait_ge(S("y_out"), 2 * i - 2)
                for n in range(2):
                    for c in range(4):
                        ins = pe.transpose(ps[0:m, 2 * (i % 2) + n, c * P:(c + 1) * P],
                                           hT[:, 4 * n + c, i * P:i * P + m], ident)
                    ins.then_inc(S("y_t"), 1)

        def act_last(act, T):
            for i in range(QT + 1):
                m = P if i < QT else DEC
                for n in range(2):
                    act.wait_ge(S("y_t"), 2 * i + n + 1)
                    act.activation(big[0:m, i * D + n * 512:i * D + (n + 1) * 512], ps[0:m, 2 * (i % 2) + n, :],
                                   ACT.Copy).then_inc(S("y_out"), 1)

        def sp_last(sp, T):
            for i in range(QT):
                sp.wait_ge(S("y_out"), 2 * i + 2)
                sp.dma_start(o["y_prompt"][0, i * P:(i + 1) * P, :], big[:, i * D:(i + 1) * D]).then_inc(S("y_st"), 16)
            sp.wait_ge(S("y_out"), 2 * QT + 2)
            sp.dma_start(o["y_sample"].rearrange("b t n -> (b t) n"), big[0:DEC, QT * D:(QT + 1) * D])\
                .then_inc(S("y_st"), 16)
            sp.wait_ge(S("y_st"), 16 * (QT + 1))

        CO = 6336
        uP = big[:, CO:CO + 1084].rearrange("p (t n) -> p t n", t=2)
        uD = big[:, CO + 1084:CO + 1580].rearrange("p (t b j) -> p t b j", t=2, b=DEC)
        cT = big[:, CO + 1580:CO + 2620].rearrange("p (t n) -> p t n", t=2)
        cst_in = big[0:120, CO + 2620:CO + 3132].rearrange("p (h n) -> p h n", h=2)
        pw = big[:, CO + 2620:CO + 3132].rearrange("p (h n) -> p h n", h=2)
        dtmp = big[:, CO + 3132:CO + 3628].rearrange("p (t b j) -> p t b j", t=2, b=DEC)
        cout = big[:, CO + 3628:CO + 4140]
        srow = big[:, CO + 4140:CO + 4140 + RWC]
        rope = fT[:, 0:2 * TOK].rearrange("p (s n) -> p s n", s=2)
        rtq = sq
        small = wks[:, 5632:6536]
        gates = wks[:, 6536:6656].rearrange("p (i n) -> p i n", n=3 * NQ)

        def sp_win_unit(sp, l, c):
            w = a["w_in"][bass.ds(l, 1)]
            u = U_IN + c
            if T_Q <= c < T_Q + 4:
                sp.wait_ge(S("lo_ready"), u - 3)
                for n in range(2):
                    col = n * 256 + (c - T_Q) * HD
                    sp.dma_start(nat[:, u % 4, :, n * HD:(n + 1) * HD],
                                 w[:, :, col:col + HD].rearrange("a (k p) n -> p (a k) n", p=P))\
                        .then_inc(S(f"nat_full{u % 4}"), 16)
                return
            col = (COL_T + c * P if c < T_Q else COL_ROWS + (c - T_KC) * P if c < T_RW
                   else COL_T + 512 + (c - T_RW) * P)
            sp_unit(sp, u, w[:, :, col:col + P])

        def sp_project(sp, T, l):
            L = bass.ds(l, 1)
            for c in range(4):
                sp_win_unit(sp, l, c)
            sp.wait_ge(S("unit_done"), U_IN)
            for n in range(2):
                sp.dma_start(cst_in[:, n, :], a["state_conv"][L, 4 * n:4 * n + 4]
                             .rearrange("a b j n -> (a b j) n")).then_inc(S("conv_in"), 16)
            sp_pages(sp, l, ("cmp_k",), (page_k,), "kpage_in")
            for c in range(4, 6):
                sp_win_unit(sp, l, c)
            sp_compress_w(sp, T, l, 0)
            sp.wait_ge(S("unit_done"), U_IN + 1)
            sp.dma_start(rope, a["rope"]).then_inc(S("rope_in"), 16)
            sp.wait_ge(S("conv_state_t"), 1)
            sp.dma_start(pw, a["conv_pw"][L].rearrange("a (k p) n -> p (a k) n", p=P)).then_inc(S("pw_in"), 16)
            for c in range(6, NPROJ):
                sp_win_unit(sp, l, c)
            sp.wait_ge(S("unit_done"), U_IN + NPROJ)
            sp_pages(sp, l, ("cmp_v",), (page_v,), "vpage_in")
            for v in range(2):
                for g in range(2):
                    sp.dma_start(peN[:, v, g * HD:(g + 1) * HD], a["cmp_pe"][L, v].rearrange("a j d -> (a j) d"))\
                        .then_inc(S("pe_in"), 16)

        def pe_project(pe, T):
            pe.wait_ge(S("conv_in"), 32)
            for n in range(2):
                for t in range(2):
                    ins = pe.transpose(ps[:, 4, t * 240 + n * 120:t * 240 + n * 120 + 120],
                                       cst_in[:, n, t * P:(t + 1) * P], ident[0:120, 0:120])
            ins.then_inc(S("conv_state_t"), 1)

            def chunk(c, j=None, wait_x=None):
                pe.wait_ge(S("p_used"), count(c + 1, j))
                pe_unit(pe, U_IN + c, 2 * (c % 2), xnH, xnL, j=j, wait_x=wait_x)
            for c in range(4):
                chunk(c, wait_x=("xl_ready", KC) if c == 0 else None)
            with pe.Fori(1, 5) as j:
                for c in range(4):
                    chunk(c, j=j)
            for c in range(20, NPROJ):
                chunk(c)
            pe.wait_ge(S("conv_state_out"), 1)
            for n, t in enumerate(ROT_TILES):
                if n == 0:
                    pe.wait_ge(S("p_used"), 2 + 14)
                if n >= 2:
                    pe.wait_ge(S("rot_used"), n - 1)
                mm_tokens(pe, 4 + 2 * (n % 2), cst[:, C_ROT:C_ROT + P], proj[:, t, :], True, True)\
                    .then_inc(S("rot_ready"), 1)
            pe.wait_ge(S("p_used"), 2 + NPROJ)
            for i in range(QT + 1):
                m = P if i < QT else DEC
                b = 2 * (i % 2)
                if i == 0:
                    pe.wait_ge(S("qr_ready"), 2)
                if i >= 2:
                    pe.wait_ge(S("r_used"), 2 * (i - 1))
                for n in range(6):
                    pe.transpose(ps[0:m, b + n // 4, n % 4 * P:(n % 4 + 1) * P], proj[:, T_KC + n, i * P:i * P + m],
                                 ident)
                pe.transpose(ps[0:m, b + 1, 256:256 + 3 * NQ], proj[0:3 * NQ, T_GT, i * P:i * P + m],
                             ident[0:3 * NQ, 0:3 * NQ]).then_inc(S("r_ready"), 1)

        ROT_TILES = (T_KS, T_KW, T_Q, T_Q + 1, T_Q + 2, T_Q + 3)

        def act_project(act, T, link):
            def chunk(c, j=None):
                if c + 2 < NPROJ:
                    act_unit(act, U_IN + c + 2, j=j)
                act.wait_ge(S("unit_done"), count(U_IN + c + 1, j))
                dst = proj[:, c, :] if j is None else proj[:, bass.ds(j * 4 + c, 1), :].rearrange("p a n -> p (a n)")
                act.activation(halves(dst), pair(2 * (c % 2)), ACT.Copy).then_inc(S("p_used"), 1)
            act.sem_inc(S("p_used"), 2)
            for c in range(4):
                chunk(c)
            act.wait_ge(S("p_used"), 2 + 4)
            act.activation(sg[:, :, :], proj[:, T_CG:T_CG + 2, :], ACT.Sigmoid).then_inc(S("cg_sig"), 1)
            with act.Fori(1, 5) as j:
                for c in range(4):
                    chunk(c, j=j)
            for c in range(20, NPROJ):
                chunk(c)

        def dve_project_units(dve, first, last):
            for c in range(first, last):
                dve_unit(dve, U_IN + c + 2)

        def act_rows(act, T, link):
            act.wait_ge(S("qr_ready"), 6)
            for i in range(QT + 1):
                m = P if i < QT else DEC
                b = 2 * (i % 2)
                act.wait_ge(S("r_ready"), i + 1)
                act.activation(rows[0:m, i, 0:512], ps[0:m, b, :], ACT.Copy).then_inc(S("r_used"), 1)
                act.activation(rows[0:m, i, 512:N_ROWS], ps[0:m, b + 1, 0:N_ROWS - 512], ACT.Copy)\
                    .then_inc(S("r_used"), 1)

        def dve_rope(dve, T, link):
            dve.wait_ge(S("rope_in"), 16)
            dve.wait_ge(S("unit_done"), U_IN + NPROJ)
            for n, t in enumerate(ROT_TILES):
                dst = proj[:, t, :] if n < 2 else qrT[:, n - 2, :]
                dve.wait_ge(S("rot_ready"), n + 1)
                dve.wait_ge(S("x_cos"), n + 1)
                dve.tensor_tensor(halves(dst), pair(4 + 2 * (n % 2)), halves(rope[:, 1, :]), ALU.mult)\
                    .then_inc(S("rot_used"), 1)
                dve.wait_ge(S("rot_used"), n + 1)
                dve.tensor_tensor(dst, dst, rtq[:, n % 2, :], ALU.add).then_inc(S("qr_ready"), 1)
            dve.wait_ge(S("qr_ready"), 6)

        def pool_rope(pool, T, link):
            pool.wait_ge(S("rope_in"), 16)
            pool.wait_ge(S("p_used"), 2 + 14)
            for n, t in enumerate(ROT_TILES):
                if n >= 2:
                    pool.wait_ge(S("qr_ready"), n - 1)
                pool.tensor_tensor(rtq[:, n % 2, :], proj[:, t, :], rope[:, 0, :], ALU.mult).then_inc(S("x_cos"), 1)

        def sp_rows_out(sp, T, l):
            L = bass.ds(l, 1)
            names = ("cmp_k", "cmp_v", "sel_k", "sel_v", "win_k", "win_v")
            sp.wait_ge(S("r_used"), 2 * (QT + 1))
            for n, name in enumerate(names):
                sp.dma_start(o[f"p_{name}"][L].rearrange("a b (i p) g d -> p (a b i) (g d)", p=P),
                             rows[:, 0:QT, n * P:(n + 1) * P]).then_inc(S("rows_st"), 16)
                if n < 4:
                    dst = o[f"s_{name}"][L].rearrange("a b t g d -> (a b t) (g d)")
                else:
                    dst = o[f"s_{name}"][L, :, PAST - 1].rearrange("a b g d -> (a b) (g d)")
                    src = a[f"cache_{name}"][L, :, 1:PAST].rearrange("a b t g d -> (a b) (t g d)")
                    sp.dma_start(o[f"s_{name}"][L, :, 0:PAST - 1].rearrange("a b t g d -> (a b) (t g d)"), src)\
                        .then_inc(S("rows_st"), 16)
                sp.dma_start(dst, rows[0:DEC, QT, n * P:(n + 1) * P]).then_inc(S("rows_st"), 16)

        def dve_conv(dve, T, link):
            dve.wait_ge(S("conv_state_t"), 1)
            dve.tensor_copy(uD[:, :, :, 0:CW - 1].rearrange("p t b j -> p (t b) j"),
                            ps[:, 4, 0:480].rearrange("p (x j) -> p x j", j=CW - 1)).then_inc(S("conv_state_out"), 1)
            link(dve.memset(uP[:, :, 0:CW - 1], 0.0))
            dve_project_units(dve, 0, 4)
            dve.wait_ge(S("cg_sig"), 1)
            link(dve.tensor_tensor(uP[:, :, CW - 1:CW - 1 + SEQ], proj[:, T_CV:T_CV + 2, 0:SEQ], sg[:, :, 0:SEQ], ALU.mult))
            dve.tensor_tensor(uD[:, :, :, CW - 1], proj[:, T_CV:T_CV + 2, SEQ:TOK], sg[:, :, SEQ:TOK], ALU.mult)\
                .then_inc(S("u_ready"), 1)
            dve.wait_ge(S("u_ready"), 1)
            dve.wait_ge(S("conv_state_out"), 1)
            base = T.at("dve_step")
            n = 0
            for j in range(CW):
                if j % 2 == 0 and 4 + j // 2 < NPROJ - 2:
                    dve_project_units(dve, 4 + j // 2, 5 + j // 2)
                for t in range(2):
                    w = vec[:, V_CW + 2 * j + t:V_CW + 2 * j + t + 1]
                    x = uP[:, t, j:j + SEQ]
                    if j == 0:
                        dve.tensor_scalar(cT[:, t, 0:SEQ], x, w, vec[:, V_CB + t:V_CB + t + 1], ALU.mult, ALU.add)\
                            .then_inc(S("dve_step"), 1)
                    else:
                        dve.wait_ge(S("dve_step"), base + n - 1)
                        dve.scalar_tensor_tensor(out=cT[:, t, 0:SEQ], in0=x, scalar=w, in1=cT[:, t, 0:SEQ],
                                                 op0=ALU.mult, op1=ALU.add).then_inc(S("dve_step"), 1)
                    n += 1
            dve.wait_ge(S("dve_step"), T.up("dve_step", n))
            taps = vec[:, V_CW:V_CW + 2 * CW].rearrange("p (j t) -> p t j", t=2).unsqueeze(2)\
                .broadcast_to((P, 2, DEC, CW))
            for t in range(2):
                link(dve.tensor_tensor(dtmp[:, t], uD[:, t], taps[:, t], ALU.mult))
                link(dve.tensor_reduce(cT[:, t, SEQ:TOK], dtmp[:, t], X, ALU.add))
                link(dve.tensor_scalar(cT[:, t, SEQ:TOK], cT[:, t, SEQ:TOK], vec[:, V_CB + t:V_CB + t + 1], None,
                                       ALU.add))
            dve.sem_inc(reach("conv_ready"), 1)

        def pe_conv_state(pe, T):
            pe.wait_ge(S("u_ready"), 1)
            pe.wait_ge(S("r_used"), 2 * (QT + 1))
            pe.wait_ge(S("rot_used"), 6)
            for t in range(2):
                pe.transpose(ps[0:CW - 1, 6, t * P:(t + 1) * P], uP[:, t, SEQ:SEQ + CW - 1], ident)
                ins = pe.transpose(ps[0:DEC, 6, 256 + t * P:256 + (t + 1) * P], uD[:, t, :, CW - 1], ident)
            for t in range(7):
                ins = pe.transpose(ps[0:DEC + 1, 7 if t < 4 else 0, (t % 4) * P:(t % 4 + 1) * P],
                                   proj[:, T_RW + t, SEQ - 1:TOK], ident)
            ins.then_inc(S("state_t"), 1)

        def act_conv_state(act, T, link):
            act.wait_ge(S("state_t"), 1)
            act.activation(cout[0:CW - 1, 0:256], ps[0:CW - 1, 6, 0:256], ACT.Copy)
            act.activation(cout[0:DEC, 256:512], ps[0:DEC, 6, 256:512], ACT.Copy)
            act.activation(srow[0:DEC + 1, 0:512], ps[0:DEC + 1, 7, :], ACT.Copy)
            link(act.activation(srow[0:DEC + 1, 512:RWC], ps[0:DEC + 1, 0, 0:RWC - 512], ACT.Copy))
            act.sem_inc(reach("state_rows"), 1)

        def sp_state_out(sp, T, l):
            L = bass.ds(l, 1)
            sp.wait_ge(*stage("state_rows"))
            for dst, src in ((o["p_conv"][L].rearrange("a b j n -> (a b j) n"), cout[0:CW - 1, 0:256]),
                             (o["s_conv"][L, :, CW - 2].rearrange("a b n -> (a b) n"), cout[0:DEC, 256:512]),
                             (o["p_shift"][L].rearrange("a b n -> (a b) n"), srow[0:1, :]),
                             (o["s_shift"][L].rearrange("a b n -> (a b) n"), srow[1:DEC + 1, :]),
                             (o["s_conv"][L, :, 0:CW - 2].rearrange("a b j n -> (a b) (j n)"),
                              a["state_conv"][L, :, 1:CW - 1].rearrange("a b j n -> (a b) (j n)"))):
                sp.dma_start(dst, src).then_inc(S("state_st"), 16)

        def dve_conv_norm(dve, T, link):
            dve.wait_ge(S("cmean"), 1)
            for t in range(2):
                ins = dve.scalar_tensor_tensor(out=halves(cT[:, t, :]), in0=pair(2), scalar=-1 / 256,
                                               in1=halves(cT[:, t, :]), op0=ALU.mult, op1=ALU.add)
            link(ins)
            dve.sem_inc(reach("c_centered"), 1)
            dve.wait_ge(S("croot"), 1)
            link(dve.reciprocal(rtq[:, 0, :], rtq[:, 0, :]))
            for t in range(2):
                link(dve.scalar_tensor_tensor(out=cT[:, t, :], in0=cT[:, t, :],
                                              scalar=vec[:, V_CLG + t:V_CLG + t + 1], in1=rtq[:, 0, :],
                                              op0=ALU.mult, op1=ALU.mult))
            dve.sem_inc(reach("c_scaled"), 1)
            dve.wait_ge(S("pw_ready"), 1)
            for t in range(2):
                link(dve.tensor_scalar(halves(cT[:, t, :]), pair(2 + 2 * t), vec[:, V_PWB + t:V_PWB + t + 1], None,
                                       ALU.add))
            dve.sem_inc(reach("ob_ready"), 1)
            dve.wait_ge(S("croot"), 2)
            link(dve.reciprocal(rtq[:, 1, :], rtq[:, 1, :]))
            for t in range(2):
                ins = dve.scalar_tensor_tensor(out=merged[:, 4 + t, :], in0=cT[:, t, :],
                                               scalar=vec[:, V_GRP + 4 + t:V_GRP + 5 + t], in1=rtq[:, 1, :],
                                               op0=ALU.mult, op1=ALU.mult)
            link(ins)

        def act_conv_norm(act, T, link):
            act.wait_ge(*stage("c_centered"))
            link(act.activation(sg[:, :, :], cT[:, :, :], ACT.Square))
            act.sem_inc(S("csq"), 1)
            act.wait_ge(S("cvar"), 1)
            act.activation(halves(rtq[:, 0, :]), pair(4), ACT.Sqrt, scale=1 / 256,
                           bias=cst[:, C_EPS + 1:C_EPS + 2]).then_inc(S("croot"), 1)
            act.wait_ge(*stage("c_scaled"))
            for t in range(2):
                ins = act.activation(sg[:, t, :], cT[:, t, :], ACT.Silu, bias=vec[:, V_CLB + t:V_CLB + t + 1])
            link(ins)
            act.sem_inc(reach("c_act"), 1)
            act.wait_ge(*stage("ob_ready"))
            link(act.activation(sg[:, :, :], cT[:, :, :], ACT.Square))
            act.sem_inc(S("csq"), 1)
            act.wait_ge(S("cvar"), 2)
            act.activation(halves(rtq[:, 1, :]), pair(6), ACT.Sqrt, scale=1 / 256,
                           bias=cst[:, C_EPS:C_EPS + 1]).then_inc(S("croot"), 1)

        def pe_conv_norm(pe, T):
            pe.wait_ge(*stage("conv_ready"))
            pe.wait_ge(*stage("vc_ready"))
            for t in range(2):
                ins = mm_tokens(pe, 2, ones, cT[:, t, :], t == 0, t == 1)
            ins.then_inc(S("cmean"), 1)
            pe.wait_ge(S("csq"), 1)
            for t in range(2):
                ins = mm_tokens(pe, 4, ones, sg[:, t, :], t == 0, t == 1)
            ins.then_inc(S("cvar"), 1)
            pe.wait_ge(S("pw_in"), 16)
            pe.wait_ge(*stage("c_act"))
            for m in range(2):
                for t in range(2):
                    ins = mm_tokens(pe, 2 + 2 * m, pw[:, t, m * P:(m + 1) * P], sg[:, t, :], t == 0, t == 1)
            ins.then_inc(S("pw_ready"), 1)
            pe.wait_ge(S("csq"), 2)
            pe.wait_ge(*stage("state_rows"))
            for t in range(2):
                ins = mm_tokens(pe, 6, ones, sg[:, t, :], t == 0, t == 1)
            ins.then_inc(S("cvar"), 1)

        xc = wks[:, 0:XCOLS + CB]
        PT = wks[:, 2592:4640].rearrange("p (s g n) -> p s g n", s=2, g=2)
        kcmp = wks[:, 4640:4640 + NWIN]
        vcmp = wks[:, 4804:4804 + NWIN]
        vcr = wks[:, 0:P]
        vcd = wks[:, P:9 * P].rearrange("p (b n) -> p b n", b=DEC)
        qz = [wks[:, 1152 + 512 * n:1664 + 512 * n].rearrange("p (b m) -> p b m", b=DEC) for n in range(2)]
        wc = big[:, 0:CB * P].rearrange("p (l e) -> p l e", e=P)
        prob = big[:, 4096:6144].rearrange("p (s g n) -> p s g n", s=2, g=2)
        oacc = big[:, 0:QT * 512].rearrange("p (i n) -> p i n", n=512)
        kT = [proj[:, t, :] for t in (T_KS, T_KW)]
        qT = proj[:, T_Q:T_Q + 4, :]
        otmp = big[:, 3100:3612]
        page_k = big[:, 4096:6144].rearrange("p (x n) -> p x n", n=P)
        page_v = mid[:, 2080:4128].rearrange("p (x n) -> p x n", n=P)
        kpage = page_v
        kdT = big[:, 0:2048]
        vdn = page_k
        dP = small[0:64, 0:264]
        dPT = small[:, 264:456].rearrange("p (n m) -> p n m", n=3)
        negm = small[:, 456:460]
        mx = small[:, 460:464]
        ssum = small[:, 464:560]
        coef = small[:, 560:568]
        osq = small[:, 568:572]
        gD = small[0:64, 572:575]
        dst_ = small[0:64, 576:580]
        cbias = small[:, 580:582]
        oD = small[:, 584:616].rearrange("p (t b) -> p t b", t=4)
        oD2 = small[:, 616:648].rearrange("p (t b) -> p t b", t=4)
        peN = small[0:CB, 648:904].rearrange("p (v n) -> p v n", v=2)

        def sp_pages(sp, l, names, dsts, sem_name):
            for x in range(DEC * NPAGE):
                pg = sp.value_load(pages[0:1, x:x + 1], min_val=0, max_val=a[f"cache_{names[0]}"].shape[1] - 1)
                for name, dst in zip(names, dsts):
                    sp.dma_start(dst[:, x, :], a[f"cache_{name}"][bass.ds(l, 1), bass.ds(pg, 1)]
                                 .rearrange("a b t g d -> t (a b) (g d)").squeeze(1)).then_inc(S(sem_name), 16)

        def sp_compress_w(sp, T, l, v):
            if v == 0:
                sp.wait_ge(*stage("wc_zero"))
            else:
                sp.wait_ge(S("win_ready"), 1)
            for g in range(2):
                sp.dma_start(wc[g * HD:(g + 1) * HD, :, g * HD:(g + 1) * HD], a["cmp_w"][bass.ds(l, 1), v]
                             .rearrange("a (j d) e -> d (a j) e", d=HD)).then_inc(S("wc_in"), 16)

        def pool_compress_zero(pool, T, link):
            pool.wait_ge(S("unit_done"), U_IN)
            link(pool.memset(big[:, 0:CB * P], 0.0))
            pool.sem_inc(reach("wc_zero"), 1)

        def pool_compress(pool, T, link):
            pool.wait_ge(S("unit_done"), U_IN + NPROJ)
            for v in range(2):
                if v:
                    pool.wait_ge(S("win_ready"), v)
                pool.tensor_copy(xc[:, 0:SEQ], proj[:, T_KC + v, 0:SEQ]).then_inc(S("xc_p"), 1)

        def pe_compress(pe, T, v):
            if v == 0:
                pe.wait_ge(S("kpage_in"), DEC * NPAGE * 16)
                pe.wait_ge(S("pe_in"), 64)
                pe.wait_ge(*stage("state_rows"))
            else:
                pe.wait_ge(S("vpage_in"), DEC * NPAGE * 16)
                pe.wait_ge(S("xc_a"), 1)
                pe.wait_ge(S("xc_d"), 1)
            for x in range(DEC * NPAGE):
                pe.transpose(ps[:, 1 + x // 4, x % 4 * P:(x % 4 + 1) * P], (page_k, page_v)[v][:, x, :], ident)
            pe.transpose(ps[:, 5, 0:CB], peN[:, v, :], ident[0:CB, 0:CB]).then_inc(S("xc_t"), 1)
            pe.wait_ge(S("wc_in"), 32 * (v + 1))
            pe.wait_ge(S("xc_p"), v + 1)
            pe.wait_ge(S("xc_a"), v + 1)
            pe.wait_ge(S("xc_d"), v + 1)
            for j in range(CB):
                ins = pe.matmul(ps[:, 6 + v, 0:NWIN], wc[:, j, :], xc[:, j:j + CS * (NWIN - 1) + 1:CS],
                                start=j == 0, stop=j == CB - 1)
            ins.then_inc(S("win_ready"), 1)

        def act_compress(act, T, link, v):
            act.wait_ge(S("xc_t"), v + 1)
            if v:
                act.wait_ge(S("win_ready"), v)
            act.activation(xc[:, 512:3 * 512].rearrange("p (x n) -> p x n", x=2), ps[:, 1:3, :], ACT.Copy)\
                .then_inc(S("xc_a"), 1)

        def dve_compress(dve, T, link, v):
            dve.wait_ge(S("xc_t"), v + 1)
            if v:
                dve.wait_ge(S("win_ready"), v)
            dve.tensor_copy(xc[:, 3 * 512:5 * 512].rearrange("p (x n) -> p x n", x=2), ps[:, 3:5, :])
            link(dve.tensor_copy(xc[:, XCOLS:XCOLS + CB], ps[:, 5, 0:CB]))
            dve.sem_inc(S("xc_d"), 1)
            dve.wait_ge(S("win_ready"), v + 1)
            link(dve.tensor_copy(cbias[:, v:v + 1], ps[:, 6 + v, NWIN - 1:NWIN]))
            link(dve.tensor_scalar((kcmp, vcmp)[v], ps[:, 6 + v, 0:NWIN], cbias[:, v:v + 1], None, ALU.add))
            dve.sem_inc(S("cmp_out"), 1)

        def pe_cmp_rows(pe, T):
            pe.wait_ge(S("cmp_out"), 2)
            pe.transpose(ps[0:NCMP, 0, 0:P], vcmp[:, 0:NCMP], ident)
            for b in range(DEC):
                o_ = P + b * P
                at = SEQ // CS + b * (PAST // CS)
                ins = pe.transpose(ps[0:NCMP_D, o_ // 512, o_ % 512:o_ % 512 + P], vcmp[:, at:at + NCMP_D], ident)
            ins.then_inc(S("vc_t"), 1)

        def dve_cmp_rows(dve, T, link):
            dve.wait_ge(S("vc_t"), 1)
            dve.tensor_copy(vcr[0:NCMP, :], ps[0:NCMP, 0, 0:P])
            dve.tensor_copy(vcd[0:NCMP_D, 0:3, :], ps[0:NCMP_D, 0, P:512].rearrange("p (b n) -> p b n", b=3))
            dve.tensor_copy(vcd[0:NCMP_D, 3:7, :], ps[0:NCMP_D, 1, :].rearrange("p (b n) -> p b n", b=4))
            link(dve.tensor_copy(vcd[0:NCMP_D, 7, :], ps[0:NCMP_D, 2, 0:P]))
            dve.sem_inc(reach("vc_ready"), 1)
            dve.wait_ge(*stage("gates_ready"))

        def act_gates(act, T, link):
            act.wait_ge(S("r_used"), 2 * (QT + 1))
            act.activation(gates[:, 0:QT, :], rows[:, 0:QT, 768:792], ACT.Sigmoid)
            link(act.activation(gates[0:DEC, QT, :], rows[0:DEC, QT, 768:792], ACT.Sigmoid))
            act.sem_inc(reach("gates_ready"), 1)

        UNITS = [(i, br, t) for i in range(QT) for br in range(3) for t in range(4)]
        CMPB = 0

        def keys_of(i, br):
            return (NCMP, 1, NCMP) if br == CMPB else ((i + 1) * P, i + 1, P)

        def pe_scores(pe, u):
            i, br, t = UNITS[u]
            nk = keys_of(i, br)[0]
            q, k = (qT, kcmp) if br == CMPB else (qrT, kT[br - 1])
            if u >= 2:
                pe.wait_ge(S("p_exp"), 2 * (u - 1))
            for g in range(2):
                h = slice(g * HD, (g + 1) * HD)
                ins = pe.matmul(ps[:, 2 * (u % 2) + g, 0:nk], q[h, t, i * P:(i + 1) * P], k[h, 0:nk],
                                start=True, stop=True)
            ins.then_inc(S("s_ready"), 1)

        def pe_prompt(pe, T):
            pe.wait_ge(*stage("vc_ready"))
            pe.wait_ge(S("qr_ready"), 6)
            pe_scores(pe, 0)
            pe_scores(pe, 1)
            for u, (i, br, t) in enumerate(UNITS):
                nk, nt, kk = keys_of(i, br)
                pe.wait_ge(S("p_exp"), 2 * (u + 1))
                if u:
                    pe.wait_ge(S("pt_a"), u)
                    pe.wait_ge(S("pt_d"), u)
                for g in range(2):
                    for n in range(nt):
                        ins = pe.transpose(ps[0:kk, 4 + g, n * P:(n + 1) * P],
                                           prob[:, u % 2, g, n * P:n * P + kk], ident)
                ins.then_inc(S("pt_ready"), 1)
                if u + 2 < len(UNITS):
                    pe_scores(pe, u + 2)
                pe.wait_ge(S("pt_a"), u + 1)
                pe.wait_ge(S("pt_d"), u + 1)
                k = u // 4
                if t == 0 and k >= 2:
                    pe.wait_ge(S("o_used"), k - 1)
                for g in range(2):
                    h = 2 * t + g
                    for n in range(nt):
                        v = vcr[0:kk] if br == CMPB else rows[:, n, 384 if br == 1 else 640:][:, 0:P]
                        ins = pe.matmul(ps[:, 6 + k % 2, h * HD:(h + 1) * HD], PT[0:kk, u % 2, g, n * P:(n + 1) * P],
                                        v[:, g * HD:(g + 1) * HD], start=n == 0, stop=n == nt - 1)
                ins.then_inc(S("pv_ready"), 1)

        def act_exps(act, u):
            i, br, t = UNITS[u]
            nk = keys_of(i, br)[0]
            act.wait_ge(S("nm_ready"), u + 1)
            if u >= 2:
                act.wait_ge(S("pt_ready"), u - 1)
            for g in range(2):
                at = (i * 3 + br) * 8 + 2 * t + g
                act.activation(prob[:, u % 2, g, 0:nk], ps[:, 2 * (u % 2) + g, 0:nk], ACT.Exp, scale=SCALE,
                               bias=negm[:, 2 * (u % 2) + g:2 * (u % 2) + g + 1],
                               accum_out=ssum[:, at:at + 1]).then_inc(S("p_exp"), 1)

        def act_prompt(act, T, link):
            act_exps(act, 0)
            for u, (i, br, t) in enumerate(UNITS):
                nk, nt, kk = keys_of(i, br)
                if u + 1 < len(UNITS):
                    act_exps(act, u + 1)
                act.wait_ge(S("pt_ready"), u + 1)
                if u >= 2:
                    act.wait_ge(S("pv_ready"), u - 1)
                act.activation(PT[0:kk, u % 2, 0, 0:nt * P], ps[0:kk, 4, 0:nt * P], ACT.Copy).then_inc(S("pt_a"), 1)
            act.wait_ge(*stage("oacc_ready"))
            for i in range(QT):
                ins = act.activation(prob[:, 0, 0, 0:512], oacc[:, i, :], ACT.Square, accum_out=osq[:, i:i + 1])
                link(ins)
            link(act.activation(osq, osq, ACT.Sqrt, scale=1 / 512, bias=cst[:, C_EPS:C_EPS + 1]))
            act.sem_inc(reach("oroot"), 1)

        def dve_softmax(dve, T, link, u):
            i, br, t = UNITS[u]
            nk = keys_of(i, br)[0]
            b = 2 * (u % 2)
            dve.wait_ge(S("s_ready"), u + 1)
            if br == CMPB:
                s, m = ps[:, b:b + 2, 0:nk], cst[:, C_CMPM + i * NCMP:C_CMPM + (i + 1) * NCMP]
            else:
                s, m = ps[:, b:b + 2, i * P:nk], cst[:, C_CAUS:C_CAUS + P]
            link(dve.tensor_tensor(s, s, m.unsqueeze(1).broadcast_to((P, 2, m.shape[1])), ALU.add))
            link(dve.tensor_reduce(mx[:, b:b + 2], ps[:, b:b + 2, 0:nk], X, ALU.max))
            dve.tensor_scalar(negm[:, b:b + 2], mx[:, b:b + 2], 0.1 * NEG, -SCALE, ALU.max, ALU.mult)\
                .then_inc(S("nm_ready"), 1)

        def dve_combine(dve, T, link, k):
            i, br = k // 3, k % 3
            dve.wait_ge(S("pv_ready"), 4 * (k + 1))
            link(dve.tensor_scalar(coef, ssum[:, k * 8:k * 8 + 8], 1e-30, None, ALU.max))
            link(dve.reciprocal(coef, coef))
            c2 = coef.rearrange("p (t g) -> p t g", g=2)
            link(dve.tensor_tensor(c2, c2, gates[:, i, :].rearrange("p (g t r) -> p t g r", g=2, r=3)[:, :, :, br],
                                   ALU.mult))
            f = coef.unsqueeze(2).broadcast_to((P, NQ, HD))
            src = ps[:, 6 + k % 2, :].rearrange("p (h d) -> p h d", d=HD)
            dst = oacc[:, i, :] if br == 0 else otmp
            dve.tensor_tensor(dst.rearrange("p (h d) -> p h d", d=HD), src, f, ALU.mult).then_inc(S("o_used"), 1)
            dve.wait_ge(S("o_used"), k + 1)
            if br:
                link(dve.tensor_tensor(oacc[:, i, :], oacc[:, i, :], otmp, ALU.add))

        def dve_prompt(dve, T, link):
            dve_softmax(dve, T, link, 0)
            for u, (i, br, t) in enumerate(UNITS):
                nk, nt, kk = keys_of(i, br)
                if u + 1 < len(UNITS):
                    dve_softmax(dve, T, link, u + 1)
                dve.wait_ge(S("pt_ready"), u + 1)
                if u >= 2:
                    dve.wait_ge(S("pv_ready"), u - 1)
                dve.tensor_copy(PT[0:kk, u % 2, 1, 0:nt * P], ps[0:kk, 5, 0:nt * P]).then_inc(S("pt_d"), 1)
                if u % 4 == 1 and u > 4:
                    dve_combine(dve, T, link, u // 4 - 1)
            dve_combine(dve, T, link, len(UNITS) // 4 - 1)
            dve.sem_inc(reach("oacc_ready"), 1)
            dve.wait_ge(*stage("oroot"))
            link(dve.reciprocal(osq, osq))
            for i in range(QT):
                link(dve.tensor_scalar(oacc[:, i, :], oacc[:, i, :], osq[:, i:i + 1], None, ALU.mult))
            dve.sem_inc(reach("on_ready"), 1)
            for t in range(4):
                dve.wait_ge(S("ot_ready"), t + 1)
                dve.tensor_scalar(merged[:, t, 0:SEQ], ps[:, t, :], vec[:, V_GRP + t:V_GRP + t + 1], None, ALU.mult)\
                    .then_inc(S("om_ready"), 1)
            dve.wait_ge(S("om_ready"), 4)

        def pe_prompt_out(pe, T):
            pe.wait_ge(*stage("on_ready"))
            for t in range(4):
                for i in range(QT):
                    heads = oacc[:, i, t * P:(t + 1) * P]
                    ins = pe.transpose(ps[:, t, i * P:(i + 1) * P], heads, ident)
                ins.then_inc(S("ot_ready"), 1)

        def pool_qz(pool, T, link):
            pool.wait_ge(S("win_ready"), 2)
            pool.wait_ge(S("qr_ready"), 6)
            link(pool.memset(wks[:, 1152:2176], 0.0))
            for n, q in enumerate((qT, qrT)):
                for g in range(2):
                    h = slice(g * HD, (g + 1) * HD)
                    dst = wks[h, 1152 + 512 * n:1152 + 512 * n + 576].rearrange("p (b x) -> p b x", x=72)
                    link(pool.tensor_copy(dst[:, :, 4 * g:4 * g + 4], q[h, :, SEQ:TOK].rearrange("p t b -> p b t")))
            pool.sem_inc(reach("qz_ready"), 1)

        def sp_decode_in(sp, T, l):
            def window(kind, dst):
                for n in range(2):
                    sp.dma_start(dst[:, 8 * n:8 * n + 8], a[f"cache_win_{kind}"][bass.ds(l, 1), 4 * n:4 * n + 4]
                                 .rearrange("a b (n t) g d -> t (a b n) (g d)", t=P)).then_inc(S("wwin_in"), 16)

            sp.wait_ge(*stage("gates_ready"))
            sp.dma_start(gD, gates[0:DEC, QT, :]).then_inc(S("gD_in"), 16)
            sp.wait_ge(S("xc_t"), 2)
            sp.wait_ge(S("pt_ready"), len(UNITS))
            sp.wait_ge(*stage("oroot"))
            sp_pages(sp, l, ("sel_k", "sel_v"), (kpage, vdn), "spage_in")
            sp.wait_ge(S("kd_t"), 4)
            window("k", kpage)
            sp.wait_ge(S("do_ready"), 2)
            window("v", vdn)

        def pe_decode(pe, T):
            pe.wait_ge(*stage("qz_ready"))
            pe.wait_ge(S("om_ready"), 4)
            for br in range(3):
                n = br - 1
                if br:
                    if br == 1:
                        pe.wait_ge(S("spage_in"), 32 * 16)
                    else:
                        pe.wait_ge(S("wwin_in"), 64)
                    for x in range(4):
                        if x >= 2 or br == 2:
                            pe.wait_ge(S("kd_out"), 4 * n + x - 1)
                        for y in range(4):
                            ins = pe.transpose(ps[:, x % 2, y * P:(y + 1) * P], kpage[:, 4 * x + y, :], ident)
                        ins.then_inc(S("kd_t"), 1)
                    pe.wait_ge(S("kd_out"), 4 * (n + 1))
                    for b in range(DEC):
                        pe.matmul(ps[0:64, 2, 0:PAST], qz[1][:, b, :], kdT[:, b * PAST:(b + 1) * PAST],
                                  start=b == 0, stop=b == DEC - 1, skip_group_check=True)
                    for b in range(DEC):
                        ins = pe.matmul(ps[0:64, 2, PAST:PAST + DEC], qz[1][:, b, :], kT[n][:, SEQ:TOK],
                                        start=False, stop=b == DEC - 1, skip_group_check=True)
                else:
                    for b in range(DEC):
                        at = SEQ // CS + b * (PAST // CS)
                        ins = pe.matmul(ps[0:64, 2, 0:NCMP_D], qz[0][:, b, :], kcmp[:, at:at + NCMP_D],
                                        start=b == 0, stop=b == DEC - 1)
                ins.then_inc(S("ds_ready"), 1)
                pe.wait_ge(S("dp_ready"), br + 1)
                if br:
                    for m in range(2):
                        pe.transpose(ps[:, 3, m * 64:(m + 1) * 64], dP[:, m * P:(m + 1) * P], ident[0:64, 0:64])
                    ins = pe.transpose(ps[0:DEC, 3, 128:192], dP[:, PAST:PAST + DEC], ident[0:64, 0:64])
                else:
                    ins = pe.transpose(ps[0:NCMP_D, 3, 0:64], dP[:, 0:NCMP_D], ident[0:64, 0:64])
                ins.then_inc(S("dpt_ready"), 1)
                pe.wait_ge(S("dpt_out"), br + 1)
                for b in range(DEC):
                    c = slice(b * NQ, (b + 1) * NQ)
                    for m in range(2 if br else 1):
                        v, w = (vdn[:, 2 * b + m, :], P) if br else (vcd[0:NCMP_D, b, :], NCMP_D)
                        ins = pe.matmul(ps[:, 7, c], v, dPT[0:w, m, c], start=br == 0 and b == 0,
                                        stop=False, skip_group_check=True)
                if br:
                    at = 384 if br == 1 else 640
                    ins = pe.matmul(ps[:, 7, 0:64], rows[0:DEC, QT, at:at + P], dPT[0:DEC, 2, :],
                                    start=False, stop=br == 2, skip_group_check=True)
                ins.then_inc(S("do_ready"), 1)
            pe.wait_ge(S("osq_ready"), 1)
            for t in range(4):
                ins = pe.matmul(ps[:, 6, 0:DEC], ones, oD2[:, t, :], start=t == 0, stop=t == 3)
            ins.then_inc(S("oss_ready"), 1)

        def act_decode(act, T, link):
            for br in range(3):
                if br:
                    for x in range(4):
                        act.wait_ge(S("kd_t"), 4 * (br - 1) + x + 1)
                        if x == 0 and br == 2:
                            act.wait_ge(S("ds_ready"), 2)
                        act.activation(kdT[:, x * 512:(x + 1) * 512], ps[:, x % 2, :], ACT.Copy)\
                            .then_inc(S("kd_out"), 1)
                act.wait_ge(S("dm_ready"), br + 1)
                nk = PAST + DEC if br else NCMP_D
                link(act.activation(dP[:, 0:nk], ps[0:64, 2, 0:nk], ACT.Exp, scale=SCALE, bias=dst_[:, 1:2],
                                    accum_out=dst_[:, 2:3]))
                act.sem_inc(S("de_ready"), 1)
            act.wait_ge(*stage("oD_ready"))
            act.activation(oD2, oD, ACT.Square).then_inc(S("osq_ready"), 1)
            act.wait_ge(S("oss_ready"), 1)
            act.activation(small[:, 0:DEC], ps[:, 6, 0:DEC], ACT.Sqrt, scale=1 / 512, bias=cst[:, C_EPS:C_EPS + 1])\
                .then_inc(S("odroot"), 1)

        def dve_decode(dve, T, link):
            for br in range(3):
                nk = PAST + DEC if br else NCMP_D
                dve.wait_ge(S("ds_ready"), br + 1)
                if br:
                    s = ps[0:64, 2, PAST:PAST + DEC]
                    link(dve.tensor_tensor(s, s, cst[0:64, C_DMASK:C_DMASK + DEC], ALU.add))
                link(dve.tensor_reduce(dst_[:, 0:1], ps[0:64, 2, 0:nk], X, ALU.max))
                link(dve.tensor_scalar(dst_[:, 1:2], dst_[:, 0:1], -SCALE, None, ALU.mult))
                dve.sem_inc(S("dm_ready"), 1)
                if br == 0:
                    dve.wait_ge(S("gD_in"), 16)
                dve.wait_ge(S("de_ready"), br + 1)
                link(dve.reciprocal(dst_[:, 3:4], dst_[:, 2:3]))
                link(dve.tensor_tensor(dst_[:, 3:4], dst_[:, 3:4], gD[:, br:br + 1], ALU.mult))
                link(dve.tensor_scalar(dP[:, 0:nk], dP[:, 0:nk], dst_[:, 3:4], None, ALU.mult))
                dve.sem_inc(S("dp_ready"), 1)
                dve.wait_ge(S("dpt_ready"), br + 1)
                if br:
                    dve.tensor_copy(dPT[:, 0:2, :], ps[:, 3, 0:128].rearrange("p (n m) -> p n m", n=2))
                    link(dve.tensor_copy(dPT[0:DEC, 2, :], ps[0:DEC, 3, 128:192]))
                else:
                    link(dve.tensor_copy(dPT[0:NCMP_D, 0, :], ps[0:NCMP_D, 3, 0:64]))
                dve.sem_inc(S("dpt_out"), 1)
            dve.wait_ge(S("do_ready"), 3)
            for g in range(2):
                h = slice(g * HD, (g + 1) * HD)
                ins = dve.tensor_copy(oD[h], ps[h, 7, 0:64].rearrange("p (b x) -> p x b", x=NQ)[:, 4 * g:4 * g + 4])
                link(ins)
            dve.sem_inc(reach("oD_ready"), 1)
            dve.wait_ge(S("odroot"), 1)
            link(dve.reciprocal(small[:, 0:DEC], small[:, 0:DEC]))
            for t in range(4):
                ins = dve.scalar_tensor_tensor(out=merged[:, t, SEQ:TOK], in0=oD[:, t, :],
                                               scalar=vec[:, V_GRP + t:V_GRP + t + 1], in1=small[:, 0:DEC],
                                               op0=ALU.mult, op1=ALU.mult)
                link(ins)
            dve.sem_inc(reach("attn_done"), 1)

        rw = proj[:, T_RW:NPROJ, :]
        xm = proj[:, 0:7, :]
        wdec, aa, gate, nkk, bb, tt = (big[:, 1040 * n:1040 * (n + 1)].rearrange("p (m t) -> p m t", m=2)
                                       for n in range(6))
        ar = big[:, 6240:8288].rearrange("p (m c s t) -> p m c s t", m=2, c=NCH, s=2)
        bt = big[:, 8288:9312].rearrange("p (m c t) -> p m c t", m=2, c=NCH)
        kt = big[:, 9312:10336].rearrange("p (m c t) -> p m c t", m=2, c=NCH)
        pp = big[:, 10336:11360].rearrange("p (m t) -> p m t", m=2)
        bh = wks[:, 0:1024].rearrange("p (m c t) -> p m c t", m=2, c=NCH)
        kh = wks[:, 1024:2048].rearrange("p (m c t) -> p m c t", m=2, c=NCH)
        wu = wks[:, 2048:3072].rearrange("p (c s n) -> p c s n", c=NCH, s=2)
        gT = wks[:, 3072:3584].rearrange("p (c n) -> p c n", c=NCH)
        hh = wks[:, 3584:4096].rearrange("p (c n) -> p c n", c=NCH)
        rwt = wks[:, 4096:4608].rearrange("p (c n) -> p c n", c=NCH)
        st = wks[:, 4608:5184].rearrange("p (c n) -> p c n", c=NCH + 1)
        swk = wks[0:64, 5184:5312]
        lora = wks[:, 5312:5568]
        tok = mix[:, 7 * TOK:7 * TOK + 4096]
        bst, kst, vst_ = (tok[:, 1024 * n:1024 * (n + 1)].rearrange("p (m c n) -> p m c n", m=2, c=NCH)
                          for n in range(3))
        ag = tok[:, 3072:4096].rearrange("p (c s n) -> p c s n", c=NCH, s=2)
        mats = fT[:, 0:4096].rearrange("p (k c n) -> p k c n", k=4, c=NCH)
        inv = proj[:, T_RW:NPROJ, :].rearrange("p c t -> p (c t)")
        xi, xT, yy = (inv[:, 1024 * n:1024 * (n + 1)].rearrange("p (c n) -> p c n", c=NCH) for n in range(3))
        oT = mid[:, 0:2 * TOK].rearrange("p (m t) -> p m t", m=2)
        sd = mid[:, 2 * TOK:2 * TOK + 1024].rearrange("p (x k) -> p x k", k=HD)
        zz = fT[:, 0:1024].rearrange("p (x k) -> p x k", k=HD)
        zt = fT[:, 1024:2048].rearrange("p (x k) -> p x k", k=HD)
        shn = wks[0:DEC, 2048:2048 + RWC]
        shT = small[:, 700:756].rearrange("p (c b) -> p c b", c=7)
        sk = small[:, 760:776]
        pend = small[:, 776:792].rearrange("p (m c) -> p m c", m=2)
        i2 = small[:, 792:856]

        def levels(n):
            return cst[:, C_LVL + n * P:C_LVL + (n + 1) * P]

        def bc4(v, n):
            return v.unsqueeze(1).broadcast_to((P, n, v.shape[1]))

        def sp_rwkv(sp, T, l):
            L = bass.ds(l, 1)
            sp.wait_ge(S("rows_st"), 16 * 14)
            sp.wait_ge(S("state_st"), 16 * 5)
            sp.wait_ge(*stage("attn_done"))
            sp.dma_start(shn, a["state_shift"][L].rearrange("a b n -> (a b) n")).then_inc(S("rw_in"), 16)
            for n, (name, r0, r1) in enumerate((("rw_w2", 0, 32), ("rw_a2", 32, 64), ("rw_g2", 64, 128))):
                sp.dma_start(lora[r0:r1, :], a[name][L].rearrange("a r n -> (a r) n")).then_inc(S("rw_in"), 16)
            for m in range(2):
                sp.dma_start(sd[:, m * DEC:(m + 1) * DEC, :],
                             a["state_wkv"][L, :, 2 * m:2 * m + 2].rearrange("a b q v k -> (q v) (a b) k"))\
                    .then_inc(S("rw_in"), 16)
            sp.wait_ge(*stage("sd_new"))
            for m in range(2):
                sp.dma_start(o["s_wkv"][L, :, 2 * m:2 * m + 2].rearrange("a b q v k -> (q v) (a b) k"),
                             sd[:, m * DEC:(m + 1) * DEC, :]).then_inc(S("wkv_st"), 16)
            for m in range(2):
                sp.wait_ge(S("swk_ready"), m + 1)
                sp.dma_start(o["p_wkv"][L, :, 2 * m:2 * m + 2].rearrange("a b q v k -> v (a b q) k"),
                             swk.rearrange("p (q k) -> p q k", q=2)).then_inc(S("wkv_st"), 16)
                sp.wait_ge(S("wkv_st"), 32 + 16 * (m + 1))
                sp.sem_inc(S("swk_free"), 1)

        def pe_rw_in(pe, T):
            pe.wait_ge(S("rw_in"), 6 * 16)
            pe.wait_ge(*stage("attn_done"))
            for c in range(7):
                ins = pe.transpose(ps[:, 6, c * DEC:(c + 1) * DEC], shn[:, c * P:(c + 1) * P], ident[0:DEC, 0:DEC])
            ins.then_inc(S("sh_t"), 1)
            pe.wait_ge(*stage("lora_act"))
            for m in range(2):
                if m:
                    pe.wait_ge(S("lora_out"), 1)
                for n, (r0, r1) in enumerate(((0, 32), (32, 64), (64, 128))):
                    for h in range(2):
                        ins = pe.matmul(ps[:, 2 * n + h, 0:HALF], lora[r0:r1, m * P:(m + 1) * P],
                                        xm[r0:r1, 6, h * HALF:(h + 1) * HALF], start=True, stop=True)
                ins.then_inc(S("lora_mm"), 1)
            for m in range(2):
                pe.wait_ge(S("kksq"), m + 1)
                if m:
                    pe.wait_ge(S("kkroot"), 1)
                mm_tokens(pe, 6, bones, tt[:, m, :], True, True).then_inc(S("kkss"), 1)

        def act_rw_in(act, T, link):
            act.wait_ge(*stage("xm_ready"))
            act.activation(xm[0:32, 6, :], xm[0:32, 6, :], ACT.Tanh)
            link(act.activation(xm[64:128, 6, :], xm[64:128, 6, :], ACT.Sigmoid))
            act.sem_inc(reach("lora_act"), 1)
            for m in range(2):
                act.wait_ge(S("lora_mm"), m + 1)
                act.activation(halves(wdec[:, m, :]), pair(0), ACT.Sigmoid,
                               bias=vec[:, V_W0 + m:V_W0 + m + 1])
                act.activation(halves(aa[:, m, :]), pair(2), ACT.Sigmoid, bias=vec[:, V_A0 + m:V_A0 + m + 1])
                link(act.activation(halves(gate[:, m, :]), pair(4), ACT.Copy))
                act.sem_inc(S("lora_out"), 1)
            act.wait_ge(S("lora_out"), 2)
            link(act.activation(wdec, wdec, ACT.Exp, scale=-float(np.exp(-0.5))))
            act.sem_inc(reach("w_ready"), 1)
            act.wait_ge(*stage("kk_raw"))
            for m in range(2):
                act.activation(tt[:, m, :], nkk[:, m, :], ACT.Square).then_inc(S("kksq"), 1)
            for m in range(2):
                act.wait_ge(S("kkss"), m + 1)
                act.activation(halves(tt[:, m, :]), pair(6), ACT.Sqrt).then_inc(S("kkroot"), 1)

        def dve_rw_in(dve, T, link):
            link(dve.tensor_tensor(i2, ident[:, 0:HD], ident[:, HD:P], ALU.add))
            link(dve.tensor_tensor(xm[:, :, 1:SEQ], rw[:, :, 0:SEQ - 1], rw[:, :, 1:SEQ], ALU.subtract))
            link(dve.tensor_scalar(xm[:, :, 0], rw[:, :, 0], -1.0, None, ALU.mult))
            dve.wait_ge(S("sh_t"), 1)
            link(dve.tensor_copy(shT, ps[:, 6, 0:7 * DEC].rearrange("p (c b) -> p c b", c=7)))
            link(dve.tensor_tensor(xm[:, :, SEQ:TOK], shT, rw[:, :, SEQ:TOK], ALU.subtract))
            for c in range(7):
                ins = dve.scalar_tensor_tensor(out=xm[:, c, :], in0=xm[:, c, :], scalar=vec[:, V_MU + c:V_MU + c + 1],
                                               in1=rw[:, c, :], op0=ALU.mult, op1=ALU.add)
            link(ins)
            dve.sem_inc(reach("xm_ready"), 1)
            for m in range(2):
                ins = dve.tensor_scalar(nkk[:, m, :], xm[:, 2 + m, :], vec[:, V_KK + m:V_KK + m + 1], -1.0,
                                        ALU.mult, ALU.mult)
            link(ins)
            dve.sem_inc(reach("kk_raw"), 1)
            dve.wait_ge(S("lora_out"), 2)
            for m in range(2):
                link(dve.tensor_scalar(bb[:, m, :], aa[:, m, :], -1.0, vec[:, V_KA + m:V_KA + m + 1], ALU.add,
                                       ALU.mult))
                link(dve.scalar_tensor_tensor(out=xm[:, 2 + m, :], in0=bb[:, m, :], scalar=1.0, in1=xm[:, 2 + m, :],
                                              op0=ALU.add, op1=ALU.mult))
            dve.wait_ge(S("kkroot"), 2)
            link(dve.tensor_scalar(tt, tt, 1e-12, None, ALU.max))
            link(dve.reciprocal(tt, tt))
            link(dve.tensor_tensor(nkk, nkk, tt, ALU.mult))
            link(dve.scalar_tensor_tensor(out=bb, in0=nkk, scalar=-1.0, in1=aa, op0=ALU.mult, op1=ALU.mult))
            dve.wait_ge(*stage("w_ready"))

        def pe_rw_decode(pe, T):
            for n in range(5):
                b = 2 * (n % 2)
                pe.wait_ge(S("z_ready"), n + 1)
                for h in range(2):
                    ins = pe.matmul(ps[:, b + h, :], bones, zz[:, 8 * h:8 * h + 8, :].rearrange("p x k -> p (x k)"),
                                    start=True, stop=True)
                ins.then_inc(S("zb_ready"), 1)

        def dve_rw_decode(dve, T, link):
            def x16(v):
                return v[:, :, SEQ:TOK]

            def spread(n):
                v = x16((nkk, wdec, bb, xm[:, 2:4, :], xm[:, 0:2, :])[n])
                for m in range(2):
                    ins = dve.tensor_tensor(zz[:, m * DEC:(m + 1) * DEC, :],
                                            v[:, m].unsqueeze(2).broadcast_to((P, DEC, HD)),
                                            i2.unsqueeze(1).broadcast_to((P, DEC, HD)), ALU.mult)
                link(ins)
                dve.sem_inc(S("z_ready"), 1)
                dve.wait_ge(S("zb_ready"), n + 1)
                return ps[:, 2 * (n % 2):2 * (n % 2) + 2, :].rearrange("p h (x k) -> p (h x) k", k=HD)

            def per_row(v):
                return v.unsqueeze(2).broadcast_to((P, 2 * DEC, HD))

            z = spread(0)
            link(dve.tensor_tensor(zt, sd, z, ALU.mult))
            link(dve.tensor_reduce(sk, zt, X, ALU.add))
            z = spread(1)
            link(dve.tensor_tensor(sd, sd, z, ALU.mult))
            z = spread(2)
            link(dve.tensor_tensor(zt, z, per_row(sk), ALU.mult))
            link(dve.tensor_tensor(sd, sd, zt, ALU.add))
            z = spread(3)
            for m in range(2):
                ins = dve.tensor_tensor(zt[:, m * DEC:(m + 1) * DEC], z[:, m * DEC:(m + 1) * DEC],
                                        xm[:, 4 + m, SEQ:TOK].unsqueeze(2).broadcast_to((P, DEC, HD)), ALU.mult)
            link(ins)
            link(dve.tensor_tensor(sd, sd, zt, ALU.add))
            dve.sem_inc(reach("sd_new"), 1)
            z = spread(4)
            link(dve.tensor_tensor(zt, sd, z, ALU.mult))
            for m in range(2):
                link(dve.tensor_reduce(oT[:, m, SEQ:TOK], zt[:, m * DEC:(m + 1) * DEC], X, ALU.add))

        def dve_rw_decay(dve, T, link):
            for m in range(2):
                for c in range(NCH):
                    s = slice(c * CH, (c + 1) * CH)
                    ins = dve.tensor_tensor_scan(pp[:, m, s], wdec[:, m, s], wdec[:, m, s], 1.0, ALU.mult, ALU.bypass)
            link(ins)
            pc = pp.rearrange("p m (c t) -> p m c t", t=CH)
            for m in range(2):
                def ch(v):
                    return v[:, m, 0:SEQ].rearrange("p (c t) -> p c t", t=CH)
                dve.tensor_tensor(ar[:, m, :, 1, :], ch(xm[:, 0:2, :]), pc[:, m], ALU.mult)
                dve.tensor_tensor(ar[:, m, :, 0, 1:CH], ch(nkk)[:, :, 1:CH], pc[:, m, :, 0:CH - 1], ALU.mult)
                dve.tensor_copy(ar[:, m, :, 0, 0], ch(nkk)[:, :, 0])
                dve.tensor_copy(pend[:, m], pc[:, m, :, CH - 1])
                link(dve.reciprocal(tt[:, m, 0:SEQ], pp[:, m, :]))
                link(dve.tensor_tensor(bt[:, m], ch(bb), ch(tt), ALU.mult))
                link(dve.tensor_tensor(kt[:, m], ch(xm[:, 2:4, :]), ch(tt), ALU.mult))
                e = pend[:, m].unsqueeze(2).broadcast_to((P, NCH, CH))
                link(dve.tensor_tensor(bh[:, m], bt[:, m], e, ALU.mult))
                link(dve.tensor_tensor(kh[:, m], kt[:, m], e, ALU.mult))
            dve.sem_inc(reach("chunks_ready"), 1)

        def pe_rw_chunks(pe, T):
            pe.wait_ge(*stage("chunks_ready"))
            for m in range(2):
                if m:
                    pe.wait_ge(S("o_out"), 1)
                    pe.wait_ge(S("swk_ready"), 1)
                srcs = (bh[:, m], kh[:, m], xm[:, 4 + m, 0:SEQ].rearrange("p (c t) -> p c t", t=CH), ar[:, m, :, 0, :])
                for n, v in enumerate(srcs):
                    for c in range(NCH):
                        for g in range(2):
                            h = slice(g * HD, (g + 1) * HD)
                            ins = pe.matmul(ps[h, n, c * CH:(c + 1) * CH], v[h, c, :], ident[h, h], start=True,
                                            stop=True)
                    ins.then_inc(S("stack_t"), 1)
                for n, v in enumerate((bt, kt)):
                    for c in range(NCH):
                        for g in range(2):
                            h = slice(g * HD, (g + 1) * HD)
                            ins = pe.matmul(ps[h, 4 + 2 * n + c // 4, c % 4 * P:(c % 4 + 1) * P], v[h, m, c, :],
                                            ar[h, m, c].rearrange("p s t -> p (s t)"), start=True, stop=True)
                    ins.then_inc(S("mat_mm"), 1)
                for n in range(6):
                    for q in range(2):
                        if n == 0:
                            pe.wait_ge(S("mats_ready"), m + 1)
                            pe.wait_ge(S("stack_out"), 4 * (m + 1))
                        else:
                            pe.wait_ge(S("x_ready"), 12 * m + 2 * (n - 1) + q + 1)
                        for c in range(4 * q, 4 * q + 4):
                            ins = pe.matmul(ps[:, q, c % 4 * P:(c % 4 + 1) * P], mats[:, 0, c, :],
                                            ident if n == 0 else xi[:, c, :], start=True, stop=True)
                        ins.then_inc(S("y_mm"), 1)
                    if n == 0:
                        continue
                    for q in range(2):
                        pe.wait_ge(S("y_masked"), 12 * m + 2 * n + q + 1)
                        for c in range(4 * q, 4 * q + 4):
                            s = slice(c % 4 * P, (c % 4 + 1) * P)
                            pe.matmul(ps[:, 2 + q, s], xT[:, c, :], yy[:, c, :], start=True, stop=True)
                        for c in range(4 * q, 4 * q + 4):
                            s = slice(c % 4 * P, (c % 4 + 1) * P)
                            ins = pe.matmul(ps[:, 4 + q, s], yy[:, c, :], xT[:, c, :], start=True, stop=True)
                        ins.then_inc(S("dx_mm"), 1)
                for c in range(NCH):
                    ins = pe.matmul(ps[:, 6, c * CH:(c + 1) * CH], mats[:, 2, c, :], vst_[:, m, c, :],
                                    start=True, stop=True)
                ins.then_inc(S("akv_mm"), 1)
                pe.wait_ge(S("akv_out"), m + 1)
                pe.wait_ge(S("x_ready"), 12 * (m + 1))
                for c in range(NCH):
                    ins = pe.matmul(ps[:, c // 4, c % 4 * P:(c % 4 + 1) * P], xT[:, c, :],
                                    ag[:, c].rearrange("p s n -> p (s n)"), start=True, stop=True)
                ins.then_inc(S("wu_mm"), 1)
                pe.wait_ge(S("wu_out"), m + 1)
                for c in range(NCH):
                    for g in range(2):
                        h = slice(g * HD, (g + 1) * HD)
                        s = slice(c * CH, (c + 1) * CH)
                        pe.matmul(ps[h, 2, s], wu[h, c, 0, :], bst[h, m, c, :], start=True, stop=True)
                        pe.matmul(ps[h, 3, s], bst[h, m, c, :], wu[h, c, 1, :], start=True, stop=False)
                        pe.matmul(ps[h, 3, s], kst[h, m, c, :], vst_[h, m, c, :], start=False, stop=True)
                        ins = pe.matmul(ps[h, 4, s], wu[h, c, 0, :], mats[h, 1, c, g * CH:(g + 1) * CH],
                                        start=True, stop=True)
                ins.then_inc(S("trans_mm"), 1)
                for c in range(NCH):
                    pe.wait_ge(S("st_ready"), (NCH + 1) * m + c + 1)
                    for g in range(2):
                        h = slice(g * HD, (g + 1) * HD)
                        ins = pe.matmul(ps[h, 5, c * CH:(c + 1) * CH], gT[h, c, :], st[h, c, :], start=True, stop=True)
                    ins.then_inc(S("st_mm"), 1)
                    for g in range(2):
                        h = slice(g * HD, (g + 1) * HD)
                        s = slice(c * CH, (c + 1) * CH)
                        pe.matmul(ps[h, 7, s], st[h, c, :], rwt[h, c, :], start=True, stop=False)
                        pe.matmul(ps[h, 7, s], wu[h, c, 1, :], mats[h, 1, c, g * CH:(g + 1) * CH], start=False,
                                  stop=False)
                        ins = pe.matmul(ps[h, 7, s], vst_[h, m, c, :], mats[h, 3, c, g * CH:(g + 1) * CH],
                                        start=False, stop=True)
                ins.then_inc(S("o_mm"), 1)
                pe.wait_ge(S("st_ready"), (NCH + 1) * (m + 1))
                pe.transpose(ps[0:64, 6, 0:P], st[:, NCH, :], ident).then_inc(S("swk_t"), 1)

        def act_rw_chunks(act, T, link):
            for m in range(2):
                for n, dst in enumerate((bst[:, m], kst[:, m], vst_[:, m], ag[:, :, 0, :])):
                    act.wait_ge(S("stack_t"), 4 * m + n + 1)
                    act.activation(dst, ps[:, n, :].rearrange("p (c n) -> p c n", c=NCH), ACT.Copy)\
                        .then_inc(S("stack_out"), 1)
                act.wait_ge(S("akv_mm"), m + 1)
                act.activation(ag[:, :, 1, :], ps[:, 6, :].rearrange("p (c n) -> p c n", c=NCH), ACT.Copy)\
                    .then_inc(S("akv_out"), 1)
                act.wait_ge(S("wu_mm"), m + 1)
                act.activation(wks[:, 2048:3072].rearrange("p (x n) -> p x n", x=2), ps[:, 0:2, :], ACT.Copy)\
                    .then_inc(S("wu_out"), 1)
                act.wait_ge(S("trans_mm"), m + 1)
                act.activation(hh, ps[:, 3, :].rearrange("p (c n) -> p c n", c=NCH), ACT.Copy)\
                    .then_inc(S("hh_out"), 1)
                act.wait_ge(S("o_mm"), m + 1)
                act.activation(oT[:, m, 0:SEQ], ps[:, 7, :], ACT.Copy).then_inc(S("o_out"), 1)
                act.wait_ge(S("swk_t"), m + 1)
                if m:
                    act.wait_ge(S("swk_free"), m)
                act.activation(swk, ps[0:64, 6, 0:P], ACT.Copy).then_inc(S("swk_ready"), 1)

        def pool_rwkv(pool, T, link):
            pool.wait_ge(*stage("dec_o"))
            link(pool.memset(fT[:, 0:4096], 0.0))
            pool.sem_inc(reach("mats_zero"), 1)

        def dve_rw_chunks(dve, T, link):
            dve.wait_ge(*stage("mats_zero"))
            masks = (cst[:, C_STR:C_STR + P], cst[:, C_INC:C_INC + P])
            for m in range(2):
                if m:
                    dve.wait_ge(S("o_mm"), m)
                for n in range(2):
                    dve.wait_ge(S("mat_mm"), 2 * m + n + 1)
                    src = ps[:, 4 + 2 * n:6 + 2 * n, :].rearrange("p b (c s t) -> p (b c) s t", s=2, t=CH)
                    for s in range(2):
                        for g in range(2):
                            h = slice(g * HD, (g + 1) * HD)
                            mask = masks[s][h, g * CH:(g + 1) * CH].unsqueeze(1).broadcast_to((HD, NCH, CH))
                            ins = dve.tensor_tensor(mats[h, 2 * n + s, :, g * CH:(g + 1) * CH], src[h, :, s, :], mask,
                                                    ALU.mult)
                    link(ins)
                dve.sem_inc(S("mats_ready"), 1)
                for q in range(2):
                    c4 = slice(4 * q, 4 * q + 4)
                    link(dve.tensor_tensor(xT[:, c4], mats[:, 0, c4], bc4(cst[:, C_LT1:C_LT1 + P], 4), ALU.mult))
                    link(dve.tensor_tensor(xT[:, c4], xT[:, c4], bc4(ident, 4), ALU.add))
                for n in range(6):
                    for q in range(2):
                        c4 = slice(4 * q, 4 * q + 4)
                        y4 = ps[:, q, :].rearrange("p (c n) -> p c n", c=4)
                        dve.wait_ge(S("y_mm"), 12 * m + 2 * n + q + 1)
                        dve.tensor_tensor(yy[:, c4], y4, bc4(levels(n), 4), ALU.mult).then_inc(S("y_masked"), 1)
                        if n == 0:
                            dve.wait_ge(S("y_masked"), 12 * m + q + 1)
                            dve.tensor_tensor(xi[:, c4], yy[:, c4], bc4(ident, 4), ALU.add).then_inc(S("x_ready"), 1)
                    if n == 0:
                        continue
                    for q in range(2):
                        c4 = slice(4 * q, 4 * q + 4)
                        dve.wait_ge(S("dx_mm"), 10 * m + 2 * (n - 1) + q + 1)
                        dx = ps[:, 2 + q, :].rearrange("p (c n) -> p c n", c=4)
                        dxT = ps[:, 4 + q, :].rearrange("p (c n) -> p c n", c=4)
                        link(dve.tensor_tensor(xi[:, c4], xi[:, c4], dx, ALU.add))
                        dve.tensor_tensor(xT[:, c4], xT[:, c4], dxT, ALU.add).then_inc(S("x_ready"), 1)
                e = pend[:, m].unsqueeze(2).broadcast_to((P, NCH, HD))
                link(dve.tensor_tensor(gT, i2.unsqueeze(1).broadcast_to((P, NCH, HD)), e, ALU.mult))
                dve.wait_ge(S("trans_mm"), m + 1)
                link(dve.tensor_tensor(gT, gT, ps[:, 2, :].rearrange("p (c n) -> p c n", c=NCH), ALU.add))
                link(dve.tensor_tensor(rwt, ar[:, m, :, 1, :], ps[:, 4, :].rearrange("p (c n) -> p c n", c=NCH),
                                       ALU.add))
                dve.memset(st[:, 0, :], 0.0).then_inc(S("st_ready"), 1)
                dve.wait_ge(S("hh_out"), m + 1)
                for c in range(NCH):
                    dve.wait_ge(S("st_mm"), NCH * m + c + 1)
                    dve.tensor_tensor(st[:, c + 1, :], ps[:, 5, c * CH:(c + 1) * CH], hh[:, c, :], ALU.add)\
                        .then_inc(S("st_ready"), 1)
                dve.wait_ge(S("st_ready"), (NCH + 1) * (m + 1))

        def pe_rw_out(pe, T):
            pe.wait_ge(S("o_out"), 2)
            pe.wait_ge(S("swk_ready"), 2)
            for m in range(2):
                ins = mm_tokens(pe, 2 * m, bones, oT[:, m, :], True, True)
            ins.then_inc(S("gmean"), 1)
            pe.wait_ge(S("gsq"), 1)
            for m in range(2):
                ins = mm_tokens(pe, 4 + 2 * m, bones, tt[:, m, :], True, True)
            ins.then_inc(S("gvar"), 1)
            pe.wait_ge(*stage("bonus_in"))
            for m in range(2):
                ins = mm_tokens(pe, 2 * m, bones, bb[:, m, :], True, True)
            ins.then_inc(S("bonus_mm"), 1)
            pe.wait_ge(S("gsq"), 2)
            for m in range(2):
                ins = mm_tokens(pe, 4, ones, tt[:, m, :], m == 0, m == 1)
            ins.then_inc(S("gvar"), 1)

        def act_rw_out(act, T, link):
            act.wait_ge(*stage("g_centered"))
            link(act.activation(tt, oT, ACT.Square))
            act.sem_inc(S("gsq"), 1)
            act.wait_ge(S("gvar"), 1)
            for m in range(2):
                ins = act.activation(halves(nkk[:, m, :]), pair(4 + 2 * m), ACT.Sqrt, scale=1 / HD,
                                     bias=cst[:, C_EPS + 2:C_EPS + 3])
            link(ins)
            act.sem_inc(S("groot"), 1)
            act.wait_ge(*stage("oc_ready"))
            link(act.activation(tt, oT, ACT.Square))
            act.sem_inc(S("gsq"), 1)
            act.wait_ge(S("gvar"), 2)
            act.activation(halves(aa[:, 0, :]), pair(4), ACT.Sqrt, scale=1 / 256, bias=cst[:, C_EPS:C_EPS + 1])\
                .then_inc(S("groot"), 1)

        def dve_rw_out(dve, T, link):
            dve.wait_ge(S("gmean"), 1)
            for m in range(2):
                link(dve.scalar_tensor_tensor(out=halves(oT[:, m, :]), in0=pair(2 * m), scalar=-1 / HD,
                                              in1=halves(oT[:, m, :]), op0=ALU.mult, op1=ALU.add))
            dve.sem_inc(reach("g_centered"), 1)
            link(dve.tensor_tensor(bb, xm[:, 0:2, :], xm[:, 2:4, :], ALU.mult))
            for m in range(2):
                link(dve.tensor_scalar(bb[:, m, :], bb[:, m, :], vec[:, V_RK + m:V_RK + m + 1], None, ALU.mult))
            dve.sem_inc(reach("bonus_in"), 1)
            dve.wait_ge(S("groot"), 1)
            link(dve.reciprocal(nkk, nkk))
            link(dve.tensor_tensor(oT, oT, nkk, ALU.mult))
            dve.wait_ge(S("bonus_mm"), 1)
            for m in range(2):
                link(dve.tensor_scalar(oT[:, m, :], oT[:, m, :], vec[:, V_LW + m:V_LW + m + 1],
                                       vec[:, V_LB + m:V_LB + m + 1], ALU.mult, ALU.add))
                link(dve.tensor_tensor(halves(wdec[:, m, :]), pair(2 * m), halves(xm[:, 4 + m, :]), ALU.mult))
            link(dve.tensor_tensor(oT, oT, wdec, ALU.add))
            link(dve.tensor_tensor(oT, oT, gate, ALU.mult))
            dve.sem_inc(reach("oc_ready"), 1)
            dve.wait_ge(S("groot"), 2)
            link(dve.reciprocal(aa[:, 0, :], aa[:, 0, :]))
            for m in range(2):
                link(dve.scalar_tensor_tensor(out=merged[:, 6 + m, :], in0=oT[:, m, :],
                                              scalar=vec[:, V_GRP + 6 + m:V_GRP + 7 + m], in1=aa[:, 0, :],
                                              op0=ALU.mult, op1=ALU.mult))
            dve.sem_inc(reach("merged_ready"), 1)

        OUT_UNITS = list(range(U_OUT, U_OUT + KC))

        def sp_wout(sp, T, l):
            sp.wait_ge(*stage("merged_ready"))
            sp.wait_ge(S("wkv_st"), 64)
            w = a["w_out"][bass.ds(l, 1)]
            for m, u in enumerate(OUT_UNITS):
                sp.wait_ge(S("lo_ready"), u - 3)
                for g in range(2):
                    sp.dma_start(nat[g * HD:(g + 1) * HD, u % 4, 0:4, :],
                                 w[:, g * 256:(g + 1) * 256, m * P:(m + 1) * P]
                                 .rearrange("a (t d) n -> d (a t) n", d=HD)).then_inc(S(f"nat_full{u % 4}"), 16)
                sp.dma_start(nat[:, u % 4, 4:8, :], w[:, 512:1024, m * P:(m + 1) * P]
                             .rearrange("a (k p) n -> p (a k) n", p=P)).then_inc(S(f"nat_full{u % 4}"), 16)

        def act_merged_split(act, T):
            act.wait_ge(*stage("merged_ready"))
            for c in range(KC):
                act.activation(mH[:, c, :], merged[:, c, :], ACT.Copy).then_inc(S("mh_ready"), 1)
            for u in OUT_UNITS[0:2]:
                act_unit(act, u)

        def dve_merged_split(dve, T):
            for c in range(KC):
                dve.wait_ge(S("mh_ready"), c + 1)
                dve.tensor_tensor(mL[:, c, :], merged[:, c, :], mH[:, c, :].bitcast(F32), ALU.subtract)\
                    .then_inc(S("ml_ready"), 1)
            for u in OUT_UNITS[0:2]:
                dve_unit(dve, u)

        def pe_wout(pe, T):
            for m, u in enumerate(OUT_UNITS):
                pe.wait_ge(S("f_used"), T.up("f_used"))
                pe_unit(pe, u, 2 * (m % 2), mH, mL, wait_x=("ml_ready", 0) if m == 0 else None)
                if m:
                    pe_sumsq(pe, T, m - 1, False)
            pe_sumsq(pe, T, KC - 1, True)

        def sp_mixer(sp, T, l):
            sp_project(sp, T, l)
            sp_rows_out(sp, T, l)
            sp_state_out(sp, T, l)
            sp_compress_w(sp, T, l, 1)
            sp_decode_in(sp, T, l)
            sp_rwkv(sp, T, l)
            sp_wout(sp, T, l)

        def pe_mixer(pe, T):
            pe_project(pe, T)
            pe_conv_state(pe, T)
            pe_compress(pe, T, 0)
            pe_compress(pe, T, 1)
            pe_cmp_rows(pe, T)
            pe_conv_norm(pe, T)
            pe_prompt(pe, T)
            pe_prompt_out(pe, T)
            pe_decode(pe, T)
            pe_rw_in(pe, T)
            pe_rw_decode(pe, T)
            pe_rw_chunks(pe, T)
            pe_rw_out(pe, T)
            pe_wout(pe, T)

        def act_mixer(act, T, link):
            act_project(act, T, link)
            act_rows(act, T, link)
            act_conv_state(act, T, link)
            act_gates(act, T, link)
            act_compress(act, T, link, 0)
            act_compress(act, T, link, 1)
            act_conv_norm(act, T, link)
            act_prompt(act, T, link)
            act_decode(act, T, link)
            act_rw_in(act, T, link)
            act_rw_chunks(act, T, link)
            act_rw_out(act, T, link)
            act_merged_split(act, T)
            act_out(act, T, OUT_UNITS, 1)

        def dve_mixer(dve, T, link):
            dve_conv(dve, T, link)
            dve_rope(dve, T, link)
            dve_compress(dve, T, link, 0)
            dve_compress(dve, T, link, 1)
            dve_cmp_rows(dve, T, link)
            dve_conv_norm(dve, T, link)
            dve_prompt(dve, T, link)
            dve_decode(dve, T, link)
            dve_rw_in(dve, T, link)
            dve_rw_decode(dve, T, link)
            dve.sem_inc(reach("dec_o"), 1)
            dve_rw_decay(dve, T, link)
            dve_rw_chunks(dve, T, link)
            dve_rw_out(dve, T, link)
            dve_merged_split(dve, T)
            dve_out(dve, T, OUT_UNITS)

        def pool_mixer(pool, T, l, link):
            pool_compress_zero(pool, T, link)
            pool_rope(pool, T, link)
            pool_compress(pool, T, link)
            pool_qz(pool, T, link)
            pool_rwkv(pool, T, link)

        @block.sync
        def _(sp):
            T = Tally()
            sp_first(sp, T)
            with sp.Fori(0, DEPTH) as l:
                boundary(sp, l, T)
                sp_vectors(sp, T, l)
                sp_ffn(sp, T, l, 0)
                sp_mixer(sp, T, l)
                sp_ffn(sp, T, l, 1)
            sp_last(sp, T)

        @block.tensor
        def _(pe):
            T = Tally()
            pe_first(pe, T)
            with pe.Fori(0, DEPTH) as l:
                boundary(pe, l, T)
                pe_vectors(pe, T)
                pe_prenorm(pe, T)
                pe_ffn(pe, T, 0)
                pe_down(pe, T, 0)
                pe_prenorm(pe, T)
                pe_mixer(pe, T)
                pe_prenorm(pe, T)
                pe_ffn(pe, T, 1)
                pe_down(pe, T, 1)
                pe.wait_ge(S("h_ready"), 3 * KC)
            pe_last(pe, T)

        @block.scalar
        def _(act):
            T = Tally()
            act_first(act, T)
            with act.Fori(0, DEPTH) as l:
                boundary(act, l, T)
                link = chain(act, "act_step", T)
                act.sem_inc(S("f_used"), 2)
                act_prenorm(act, T, 0)
                for u in range(2):
                    act_unit(act, u)
                act_xn_split(act, T)
                act_ffn(act, T, 0)
                act_out(act, T, [u for u, *_ in dn_units(0)], 3)
                act_prenorm(act, T, 1)
                act_xn_split(act, T)
                act_mixer(act, T, link)
                act_prenorm(act, T, 2)
                act_xn_split(act, T)
                act_ffn(act, T, 1)
                act_out(act, T, [u for u, *_ in dn_units(1)], 3)
            act_last(act, T)

        @block.vector
        def _(dve):
            T = Tally()
            dve_first(dve, T)
            with dve.Fori(0, DEPTH) as l:
                boundary(dve, l, T)
                link = chain(dve, "dve_step", T)
                dve.sem_inc(S("gu_used"), 2)
                dve_vectors(dve, T, link)
                for u in range(2):
                    dve_unit(dve, u)
                dve_prenorm(dve, T, 0)
                dve_ffn(dve, T, 0)
                dve_out(dve, T, [u for u, *_ in dn_units(0)])
                dve_postnorm(dve, T, 1)
                dve_prenorm(dve, T, 2)
                dve_mixer(dve, T, link)
                dve_postnorm(dve, T, 3)
                dve_prenorm(dve, T, 4)
                dve_ffn(dve, T, 1)
                dve_out(dve, T, [u for u, *_ in dn_units(1)])
                dve_postnorm(dve, T, 5)

        @block.gpsimd
        def _(pool):
            T = Tally()
            S("pool_step")
            known = len(sems)
            with pool.Fori(0, DEPTH) as l:
                boundary(pool, l, T)
                link = chain(pool, "pool_step", T)
                pool_residual(pool, T)
                pool_mixer(pool, T, l, link)
                pool_residual(pool, T)
                pool_residual(pool, T)
                assert known == len(sems), "a semaphore that the boundary doesn't clear"


_OUTS = [
    ("y_prompt", (1, SEQ, D)), ("y_sample", (DEC, 1, D)),
    *[(f"p_{n}", (DEPTH, 1, SEQ, NKV, HD)) for n in ("cmp_k", "cmp_v", "sel_k", "sel_v", "win_k", "win_v")],
    ("p_conv", (DEPTH, 1, CW - 1, 256)), ("p_shift", (DEPTH, 1, RWC)), ("p_wkv", (DEPTH, 1, 4, HD, HD)),
    *[(f"s_{n}", (DEPTH, DEC, 1, NKV, HD)) for n in ("cmp_k", "cmp_v", "sel_k", "sel_v")],
    *[(f"s_{n}", (DEPTH, DEC, PAST, NKV, HD)) for n in ("win_k", "win_v")],
    ("s_conv", (DEPTH, DEC, CW - 1, 256)), ("s_shift", (DEPTH, DEC, RWC)), ("s_wkv", (DEPTH, DEC, 4, HD, HD)),
]
def kernel(**inputs):
    import concourse.bacc as bacc
    from concourse.bass_utils import run_bass_kernel_spmd

    nc = bacc.Bacc("TRN2", target_bir_lowering=False, num_devices=1)
    const, rope = constants()
    arrays, a, o = {}, {}, {}
    for name, v in {**inputs, "const": const, "rope": rope}.items():
        v = np.ascontiguousarray(v)
        arrays[f"in_{name}"] = v
        a[name] = nc.dram_tensor(f"in_{name}", v.shape, mybir.dt.from_np(v.dtype), kind="ExternalInput").ap()
    for name, shape in _OUTS:
        o[name] = nc.dram_tensor(f"out_{name}", shape, F32, kind="ExternalOutput").ap()
    trunk(nc, a, o)
    r = run_bass_kernel_spmd(nc, [arrays], core_ids=[0])
    return tuple(r.results[0][f"out_{name}"] for name, _ in _OUTS)
```

```python
from contextlib import ExitStack

import concourse.bass as bass
from concourse import mybir
import numpy as np

F32 = mybir.dt.float32
F32R = mybir.dt.float32r
I32 = mybir.dt.int32
ALU = mybir.AluOpType
ACT = mybir.ActivationFunctionType
X = mybir.AxisListType.X

P = 128
DEPTH, D, SEQ, DEC = 2, 1024, 512, 8
TOK = SEQ + DEC
HALF = TOK // 2
KC = D // P
DFF = 2816
FC = DFF // P
HD = 64
NQ, NKV = 8, 2
QT = SEQ // P
PAST, PAGE = 256, 128
NPAGE = PAST // PAGE
CTX = PAST + 1
CB, CS = 32, 16
NCMP = (SEQ - CB) // CS + 1
NCMP_D = (CTX - CB) // CS + 1
XCOLS = SEQ + DEC * PAST
NWIN = (XCOLS + CB - CB) // CS + 1
CW = 31
CH = 64
NCH = SEQ // CH
RWC = 896
COL_ROWS = 512
N_ROWS = 6 * P + 3 * NQ
COL_T = COL_ROWS + N_ROWS
NEG = -1e30
SCALE = HD ** -0.5
RMS_EPS, LN_EPS, GN_EPS = 1e-6, 1e-5, 64e-5

C_ID, C_ONES, C_BONES, C_ROT, C_CAUS, C_CMPM, C_DMASK, C_LVL, C_LT1, C_STR, C_INC, C_COS, C_SIN, C_EPS, C_END = (
    int(v) for v in np.cumsum([0, 128, 128, 128, 128, 128, QT * NCMP, DEC, 6 * 128, 128, 128, 128, 40, 40, 8]))


def constants():
    c = np.zeros((P, C_END), np.float32)
    i = np.arange(P)
    c[:, C_ID:C_ID + P] = np.eye(P)
    c[:, C_ONES:C_ONES + P] = 1
    same = i[:, None] // 64 == i[None, :] // 64
    c[:, C_BONES:C_BONES + P] = same
    rot = np.zeros((P, P), np.float32)
    for b in (0, 64):
        for e in range(8):
            rot[b + 8 + e, b + e] = -1
            rot[b + e, b + 8 + e] = 1
    c[:, C_ROT:C_ROT + P] = rot
    c[:, C_CAUS:C_CAUS + P] = np.where(i[None, :] <= i[:, None], 0, NEG)
    end = np.arange(NCMP) * CS + CB - 1
    for t in range(QT):
        c[:, C_CMPM + t * NCMP:C_CMPM + (t + 1) * NCMP] = np.where(end[None, :] <= (t * P + i)[:, None], 0, NEG)
    c[:, C_DMASK:C_DMASK + DEC] = np.where(np.arange(DEC)[None, :] == (i // NQ)[:, None], 0, NEG)
    for n in range(6):
        m = 1 << n
        c[:, C_LVL + n * P:C_LVL + (n + 1) * P] = (
            same & (i[:, None] // (2 * m) == i[None, :] // (2 * m))
            & (i[:, None] // m % 2 == 1) & (i[None, :] // m % 2 == 0))
    c[:, C_LT1:C_LT1 + P] = c[:, C_LVL:C_LVL + P].T
    c[:, C_STR:C_STR + P] = same & (i[:, None] < i[None, :])
    c[:, C_INC:C_INC + P] = same & (i[:, None] <= i[None, :])
    inv = np.float32(500000.0) ** (-np.arange(8, dtype=np.float32) * np.float32(2.0) / np.float32(16))
    pos = np.arange(5 * P, dtype=np.float32)
    pos[SEQ:] = PAST
    ang = (pos[:, None] * inv[None, :].astype(np.float32)).astype(np.float32)
    c[:, C_COS:C_COS + 40] = np.cos(ang).reshape(5, P, 8).transpose(1, 0, 2).reshape(P, 40)
    c[:, C_SIN:C_SIN + 40] = np.sin(ang).reshape(5, P, 8).transpose(1, 0, 2).reshape(P, 40)
    c[:, C_EPS:C_EPS + 3] = (RMS_EPS, LN_EPS, GN_EPS)
    rope = np.zeros((P, 2, TOK), np.float32)
    rope[:, 0] = 1
    for b in (0, 64):
        for o in (0, 8):
            rope[b + o:b + o + 8, 0] = np.cos(ang[:TOK]).T
            rope[b + o:b + o + 8, 1] = np.sin(ang[:TOK]).T
    return c, rope


V_NORM, V_GRP, V_CB, V_CLG, V_CLB, V_PWB, V_MU, V_W0, V_A0, V_KK, V_KA, V_RK, V_LW, V_LB = (
    0, 48, 56, 58, 60, 62, 64, 71, 73, 75, 77, 79, 81, 83)
V_END = 85
V_CW = 88


UK = 8
U_UP = (0, 98)
U_DN = (44, 142)
U_IN, U_OUT = 68, 90
U_END = 166
DN_K = ((0, 8), (8, 8), (16, 6))


MILESTONES = {
    "dve_stage": ("conv_ready", "c_centered", "c_scaled", "ob_ready", "lora_in", "conv_done", "kk_raw",
                  "vc_ready", "oacc_ready", "on_ready", "sd_new", "oD_ready", "attn_done",
                  "bonus_in", "g_centered", "oc_ready", "merged_ready"),
    "act_stage": ("c_act", "state_rows", "lora_act", "gates_ready", "w_ready", "oroot"),
    "pool_stage": ("wc_zero", "qz_ready", "mats_zero"),
}


SIGNALS = (
    "act_stage act_step ah_ready akv_mm akv_out bonus_mm cg_sig cmean cmp_out const_in conv_in conv_state_out "
    "conv_state_t croot csq cvar de_ready decayed dm_ready do_ready dp_ready dpt_out dpt_ready ds_ready dve_rstd "
    "dve_stage dve_step dx_mm f_out f_used fn_ready gD_in gm_ready gmean groot gsq gu_used gvar h_ready hd_ready "
    "hh_out hi_ready kd_out kd_t kkroot kksq kkss kpage_in lo_ready lora_mm lora_out lora_w_in mat_mm mats_ready "
    "mh_ready ml_ready nat_full0 nat_full1 nat_full2 nat_full3 nm_ready o_mm o_out o_used odroot om_ready osq_ready "
    "oss_ready ot_ready p_exp p_used page_in pe_in pool_stage pool_step pt_a pt_d pt_ready pv_ready pw_in pw_ready "
    "qr_ready r_ready r_used root_ready rope_in rot_ready rot_used rows_st rstd_used rw_in s_ready sd_in sg_ready "
    "skpage_in sq_added sq_ready sq_used st_mm st_ready stack_out stack_t state_st state_t svpage_in swk_free "
    "swk_ready swk_t trans_mm u_ready unit_done vc_t vec_in vec_t vpage_in wc_in win_ready wkv_st wu_mm wu_out "
    "wwin_in x_cos x_dec_out x_in x_ready x_rows_out x_t xc_a xc_d xc_p xc_t xh_ready xl_ready xn_raw y_masked y_mm "
    "y_out y_st y_t z_ready zb_ready "
).split()


class Tally:

    def __init__(self):
        self.n = {}

    def up(self, name, k=1):
        self.n[name] = self.n.get(name, 0) + k
        return self.n[name]

    def at(self, name):
        return self.n.get(name, 0)


def trunk(nc, a, o):
    es = ExitStack()
    with es:
        def sb(name, shape, dt=F32):
            return es.enter_context(nc.sbuf_tensor(name, shape, dt))

        sems = {name: es.enter_context(nc.semaphore(name)) for name in SIGNALS}

        def S(name):
            return sems[name]

        reached = {}

        def stage(name):
            group = next(g for g, names in MILESTONES.items() if name in names)
            return S(group), MILESTONES[group].index(name) + 1

        def reach(name):
            sem, n = stage(name)
            group = next(g for g, names in MILESTONES.items() if name in names)
            assert reached.get(group, 0) == n - 1, f"{name} is out of order"
            reached[group] = n
            return sem

        layer_end = es.enter_context(nc.semaphore("layer_end"))
        fence = es.enter_context(nc.semaphore("fence"))
        layer_go = es.enter_context(nc.semaphore("layer_go"))

        ps = es.enter_context(nc.psum_tensor("ps", [P, 8, 512], F32))

        def arena(name, words):
            start = nc.sbuf_base
            sb(name, [P, words])
            return start

        def over(name, start, word, shape, dt=F32):
            return nc.alloc_sbuf_tensor_at(name, shape, dt, offset=start + 4 * word)

        hT = sb("hT", [P, KC, TOK])
        at_x = arena("arena_x", 2 * KC * TOK)
        xnH = over("xnH", at_x, 0, [P, KC, TOK], F32R)
        xnL = over("xnL", at_x, KC * TOK, [P, KC, TOK], F32R)
        merged = over("merged", at_x, 0, [P, KC, TOK])
        mid = over("mid", at_x, KC * TOK, [P, KC * TOK])
        at_a = arena("arena_a", 2 * FC * TOK)
        actH = over("actH", at_a, 0, [P, FC, TOK], F32R)
        actL = over("actL", at_a, FC * TOK, [P, FC, TOK], F32R)
        mH = over("mH", at_a, 0, [P, KC, TOK], F32R)
        mL = over("mL", at_a, KC * TOK, [P, KC, TOK], F32R)
        big = over("big", at_a, 0, [P, FC * TOK])
        mix = over("mix", at_a, FC * TOK, [P, FC * TOK])
        fT = sb("fT", [P, KC * TOK])
        at_w = arena("arena_w", 8 * UK * P)
        nat = over("nat", at_w, 0, [P, 4, UK, P])
        wH = over("wH", at_w, 4 * UK * P, [P, 2, UK, P], F32R)
        wL = over("wL", at_w, 6 * UK * P, [P, 2, UK, P], F32R)
        wks = over("wks", at_w, 0, [P, 8 * UK * P])
        cst = sb("cst", [P, C_END])
        vec = sb("vec", [P, 152])
        sq = sb("sq", [P, 2, TOK])
        rstd = sb("rstd", [P, TOK])
        sg = sb("sg", [P, 2, TOK])
        pages = sb("pages", [1, DEC * NPAGE], I32)

        f_v = fT[:, :].rearrange("p (c t) -> p c t", t=TOK)
        proj = mix[:, :].rearrange("p (c t) -> p c t", t=TOK)
        qrT = mid[:, 0:4 * TOK].rearrange("p (c t) -> p c t", t=TOK)
        rows = fT[:, 0:5 * N_ROWS].rearrange("p (i n) -> p i n", n=N_ROWS)
        ident = cst[:, C_ID:C_ID + P]
        ones = cst[:, C_ONES:C_ONES + P]
        bones = cst[:, C_BONES:C_BONES + P]

        def halves(v):
            return v.rearrange("p (h n) -> p h n", h=2)

        def pair(b):
            return ps[:, b:b + 2, 0:HALF]

        def chain(eng, name, tally):
            def link(ins):
                ins.then_inc(S(name), 1)
                eng.wait_ge(S(name), tally.up(name))
            return link

        block = es.enter_context(nc.Block())

        def boundary(eng, l, tally):
            engines = (nc.sync, nc.tensor, nc.scalar, nc.vector, nc.gpsimd)
            n = len(engines)
            eng.drain().then_inc(layer_end, 1)
            tally.n.clear()
            eng.wait_ge(layer_end, l * n + n)
            eng.sem_inc(fence, 1)
            share = next(k for k, e in enumerate(engines) if e is eng)
            for name in SIGNALS[share::n]:
                eng.sem_clear(sems[name])
            eng.sem_inc(layer_go, 1)
            eng.wait_ge(layer_go, l * n + n)
            eng.sem_inc(fence, 1)

        def mm_tokens(pe, bank, w, x, first, last):
            for h in range(2):
                ins = pe.matmul(ps[:, bank + h, 0:HALF], w, x[:, h * HALF:(h + 1) * HALF], start=first, stop=last)
            return ins

        def act_prenorm(act, T, n):
            used = T.at("_used")
            T.up("_sq", KC)
            T.up("_used", KC)
            for c in range(KC):
                if n:
                    h = ("h_ready", "hd_ready")[c % 2]
                    act.wait_ge(S(h), T.up(h))
                if c >= 2:
                    act.wait_ge(S("sq_used"), used + c - 1)
                act.activation(sq[:, c % 2, :], hT[:, c, :], ACT.Square).then_inc(S("sq_ready"), 1)
            act_rstd(act, T, RMS_EPS, D)

        def act_rstd(act, T, eps, n):
            col = C_EPS + (RMS_EPS, LN_EPS, GN_EPS).index(eps)
            act.wait_ge(S("sq_used"), T.at("_used"))
            if T.up("_root") > 1:
                act.wait_ge(S("rstd_used"), T.at("_root") - 1)
            act.activation(halves(rstd[:, :]), pair(6), ACT.Sqrt, scale=1.0 / n,
                           bias=cst[:, col:col + 1]).then_inc(S("root_ready"), 1)

        def pe_sumsq(pe, T, c, last):
            pe.wait_ge(S("sq_ready"), T.up("sq_ready"))
            if c == 0 and T.up("_ss") > 1:
                pe.wait_ge(S("root_ready"), T.at("_ss") - 1)
            ins = mm_tokens(pe, 6, ones, sq[:, (T.at("sq_ready") - 1) % 2, :], c == 0, last)
            ins.then_inc(S("sq_used"), 1)

        def pe_sumsq_out(pe, T):
            pe.wait_ge(S("root_ready"), T.up("_ss") - 1)
            pe.wait_ge(S("sq_added"), T.up("sq_added", KC - 2))
            mm_tokens(pe, 6, ones, rstd[:, :], True, False)
            pe.wait_ge(S("sq_ready"), T.up("sq_ready", KC))
            mm_tokens(pe, 6, ones, sq[:, 1, :], False, True).then_inc(S("sq_used"), 1)

        def pool_sumsq(pool, T):
            base = T.up("sq_ready", KC)
            T.up("sq_ready", KC)
            for m in range(1, KC - 1):
                pool.wait_ge(S("sq_ready"), base + m + 1)
                if m > 1:
                    pool.wait_ge(S("sq_added"), T.at("sq_added"))
                pool.tensor_tensor(rstd[:, :], sq[:, 0, :] if m == 1 else rstd[:, :], sq[:, m % 2, :], ALU.add)\
                    .then_inc(S("sq_added"), 1)
                T.up("sq_added")

        def pe_prenorm(pe, T):
            for c in range(KC):
                pe_sumsq(pe, T, c, c == KC - 1)

        def dve_recip(dve, T):
            dve.wait_ge(S("root_ready"), T.up("root_ready"))
            dve.reciprocal(rstd[:, :], rstd[:, :]).then_inc(S("dve_rstd"), 1)
            dve.wait_ge(S("dve_rstd"), T.up("dve_rstd"))

        def dve_prenorm(dve, T, n, link=None):
            if n == 0:
                dve_vectors(dve, T, link)
            dve_recip(dve, T)
            base = T.at("xn_raw")
            for c in range(KC + 1):
                if c < KC:
                    if base + c >= 2:
                        dve.wait_ge(S("xl_ready"), base + c - 1)
                    dve.scalar_tensor_tensor(out=sg[:, c % 2, :], in0=hT[:, c, :],
                                             scalar=vec[:, V_NORM + n * KC + c:V_NORM + n * KC + c + 1],
                                             in1=rstd[:, :], op0=ALU.mult, op1=ALU.mult).then_inc(S("xn_raw"), 1)
                if c:
                    dve.wait_ge(S("xh_ready"), base + c)
                    dve.tensor_tensor(xnL[:, c - 1, :], sg[:, (c - 1) % 2, :], xnH[:, c - 1, :].bitcast(F32),
                                      ALU.subtract).then_inc(S("xl_ready"), 1)
            T.up("xn_raw", KC)
            dve.wait_ge(S("xl_ready"), base + KC)
            dve.sem_inc(S("rstd_used"), 1)

        def act_xn_split(act, T):
            for c in range(KC):
                act.wait_ge(S("xn_raw"), T.up("xn_raw"))
                act.activation(xnH[:, c, :], sg[:, c % 2, :], ACT.Copy).then_inc(S("xh_ready"), 1)

        def dve_postnorm(dve, T, n):
            dve_recip(dve, T)
            for c in range(KC):
                dve.scalar_tensor_tensor(out=f_v[:, c, :], in0=f_v[:, c, :],
                                         scalar=vec[:, V_NORM + n * KC + c:V_NORM + n * KC + c + 1],
                                         in1=rstd[:, :], op0=ALU.mult, op1=ALU.mult).then_inc(S("fn_ready"), 1)
                if c > 2 and c % 2:
                    dve_residual(dve, T, c - 2)
            dve_residual(dve, T, KC - 1)
            dve.wait_ge(S("hd_ready"), T.up("hd_ready", KC // 2))
            T.up("fn_ready", KC)
            dve.sem_inc(S("rstd_used"), 1)

        def dve_residual(dve, T, c):
            dve.wait_ge(S("fn_ready"), T.at("fn_ready") + c + 1)
            dve.tensor_tensor(hT[:, c, :], hT[:, c, :], f_v[:, c, :], ALU.add).then_inc(S("hd_ready"), 1)

        def pool_residual(pool, T):
            for c in range(0, KC, 2):
                pool.wait_ge(S("fn_ready"), T.up("fn_ready", 2) - 1)
                pool.tensor_tensor(hT[:, c, :], hT[:, c, :], f_v[:, c, :], ALU.add).then_inc(S("h_ready"), 1)

        T_CV, T_CG, T_KC, T_VC, T_GT, T_KS, T_VS, T_KW, T_Q, T_VW, T_RW = 0, 2, 4, 5, 6, 7, 8, 9, 10, 14, 15
        ROW_TILES = (T_KC, T_VC, T_KS, T_VS, T_KW, T_VW)
        NPROJ = 22

        def count(n, j):
            return n if j is None else j * 4 + n

        def sp_unit(sp, u, src, nk=UK, j=None):
            if u >= 4 or j is not None:
                sp.wait_ge(S("lo_ready"), count(u - 3, j))
                if j is not None:
                    sp.sem_inc(fence, 1)
            sp.dma_start(nat[:, u % 4, 0:nk, :], src.rearrange("a (k p) n -> p (a k) n", p=P))\
                .then_inc(S(f"nat_full{u % 4}"), 16)

        def landed(u):
            return 16 * sum(2 if U_IN + T_Q <= v < U_IN + T_Q + 4 else 3 if U_OUT <= v < U_OUT + KC else 1
                            for v in range(u % 4, u + 1, 4))

        def act_unit(act, u, nk=UK, j=None):
            act.wait_ge(S(f"nat_full{u % 4}"), landed(u) if j is None else j * 16 + (landed(u + 4) - 16))
            if u >= 2 or j is not None:
                act.wait_ge(S("unit_done"), count(u - 1, j))
            act.activation(wH[:, u % 2, 0:nk, :], nat[:, u % 4, 0:nk, :], ACT.Copy).then_inc(S("hi_ready"), 1)

        def dve_unit(dve, u, nk=UK, j=None):
            dve.wait_ge(S("hi_ready"), count(u + 1, j))
            dve.tensor_tensor(wL[:, u % 2, 0:nk, :], nat[:, u % 4, 0:nk, :], wH[:, u % 2, 0:nk, :].bitcast(F32),
                              ALU.subtract).then_inc(S("lo_ready"), 1)

        def pe_unit(pe, u, bank, xh, xl, k0=0, nk=UK, first=True, last=True, j=None, wait_x=None):
            pe.wait_ge(S("lo_ready"), count(u + 1, j))
            for k in range(nk):
                if wait_x is not None:
                    pe.wait_ge(S(wait_x[0]), wait_x[1] + k + 1)
                for h in range(2):
                    out, t = ps[:, bank + h, 0:HALF], slice(h * HALF, (h + 1) * HALF)
                    pe.matmul(out, wH[:, u % 2, k, :], xh[:, k0 + k, t], start=first and k == 0, stop=False)
                    pe.matmul(out, wH[:, u % 2, k, :], xl[:, k0 + k, t], start=False, stop=False)
                for h in range(2):
                    out, t = ps[:, bank + h, 0:HALF], slice(h * HALF, (h + 1) * HALF)
                    ins = pe.matmul(out, wL[:, u % 2, k, :], xh[:, k0 + k, t], start=False, stop=last and k == nk - 1)
            ins.then_inc(S("unit_done"), 1)

        def dn_units(f):
            return [(U_DN[f] + 3 * m + n, m, k0, nk) for m in range(KC) for n, (k0, nk) in enumerate(DN_K)]

        def size_of(u):
            for f in range(2):
                if U_DN[f] <= u < U_DN[f] + 24:
                    return DN_K[(u - U_DN[f]) % 3][1]
            return UK

        def sp_ffn(sp, T, l, f):
            L = bass.ds(l, 1)

            def chunk(c, u, j=None):
                col = c * P if j is None else bass.ds(j * 2 * P + c * P, P)
                col = slice(c * P, (c + 1) * P) if j is None else col
                for n, w in enumerate((a["ffn_gate"], a["ffn_up"])):
                    sp_unit(sp, u + n, w[L, f, :, col], j=j)
            for c in range(2):
                chunk(c, U_UP[f] + 2 * c)
            if f == 0:
                sp_vectors(sp, T, l)
            with sp.Fori(1, FC // 2) as j:
                for c in range(2):
                    chunk(c, U_UP[f] + 2 * c, j=j)
            for u, m, k0, nk in dn_units(f):
                sp_unit(sp, u, a["ffn_down"][L, f, k0 * P:(k0 + nk) * P, m * P:(m + 1) * P], nk)

        def pe_ffn(pe, T, f):
            base, xbase = f * FC, (0, 2 * KC)[f]

            def chunk(c, j=None, wait_x=None):
                pe.wait_ge(S("gu_used"), base + c + 1 if j is None else j * 2 + (base + c + 1))
                for n in range(2):
                    pe_unit(pe, U_UP[f] + 2 * c + n, 4 * (c % 2) + 2 * n, xnH, xnL, j=j,
                            wait_x=wait_x if n == 0 else None)
            for c in range(2):
                chunk(c, wait_x=("xl_ready", xbase) if c == 0 else None)
            with pe.Fori(1, FC // 2) as j:
                for c in range(2):
                    chunk(c, j=j)

        def act_ffn(act, T, f):
            base = f * FC
            with act.Fori(0, FC // 2) as j:
                for c in range(2):
                    for n in range(2):
                        act_unit(act, U_UP[f] + 2 * c + n + 2, j=j)
                    act.wait_ge(S("unit_done"), count(U_UP[f] + 2 * c + 2, j))
                    act.activation(halves(sg[:, c, :]), pair(4 * c), ACT.Silu).then_inc(S("sg_ready"), 1)
                    act.wait_ge(S("gm_ready"), j * 2 + (base + c + 1))
                    act.activation(actH[:, bass.ds(j * 2 + c, 1), :], sg[:, c:c + 1, :], ACT.Copy)\
                        .then_inc(S("ah_ready"), 1)

        def dve_ffn(dve, T, f):
            base = f * FC
            with dve.Fori(0, FC // 2) as j:
                for c in range(2):
                    for n in range(2):
                        dve_unit(dve, U_UP[f] + 2 * c + n + 2, j=j)
                    dve.wait_ge(S("sg_ready"), j * 2 + (base + c + 1))
                    dve.tensor_tensor(halves(sg[:, c, :]), halves(sg[:, c, :]), pair(4 * c + 2), ALU.mult)\
                        .then_inc(S("gm_ready"), 1)
                    dve.wait_ge(S("ah_ready"), j * 2 + (base + c + 1))
                    dve.tensor_tensor(actL[:, bass.ds(j * 2 + c, 1), :], sg[:, c:c + 1, :],
                                      actH[:, bass.ds(j * 2 + c, 1), :].bitcast(F32), ALU.subtract)\
                        .then_inc(S("gu_used"), 1)

        def pe_down(pe, T, f):
            pe.wait_ge(S("gu_used"), (f + 1) * FC + 1)
            for u, m, k0, nk in dn_units(f):
                if m == 0 and k0 + nk == FC:
                    pe.wait_ge(S("gu_used"), (f + 1) * FC + 2)
                if k0 == 0:
                    pe.wait_ge(S("f_used"), T.up("f_used"))
                pe_unit(pe, u, 2 * (m % 2), actH, actL, k0, nk, k0 == 0, k0 + nk == FC)
            pe_sumsq_out(pe, T)

        def dve_out(dve, T, units):
            for u in units:
                if u + 2 < U_END:
                    dve_unit(dve, u + 2, size_of(u + 2))

        def act_out(act, T, units, step):
            for m in range(KC):
                for u in units[m * step:(m + 1) * step]:
                    if u + 2 < U_END:
                        act_unit(act, u + 2, size_of(u + 2))
                act.wait_ge(S("unit_done"), u + 1)
                if m >= 2:
                    act.wait_ge(S("sq_added"), T.at("_added") + max(1, m - 2))
                act.activation(halves(f_v[:, m, :]), pair(2 * (m % 2)), ACT.Copy).then_inc(S("f_out"), 1)
                act.activation(halves(sq[:, m % 2, :]), pair(2 * (m % 2)), ACT.Square).then_inc(S("sq_ready"), 1)
                act.wait_ge(S("f_out"), T.up("f_out"))
                act.wait_ge(S("sq_ready"), T.at("_sq") + m + 1)
                act.sem_inc(S("f_used"), 1)
            T.up("_sq", KC)
            T.up("_added", KC - 2)
            T.up("_used")
            act_rstd(act, T, RMS_EPS, D)

        xin = big[:, 0:QT * D].rearrange("p (i n) -> p i n", n=D)
        xin_d = big[0:DEC, QT * D:(QT + 1) * D]
        vst = sb("vst", [P, 2, P])

        def sp_first(sp, T):
            sp.dma_start(cst[:, :], a["const"]).then_inc(S("const_in"), 16)
            sp.dma_start(xin, a["x_prompt"].rearrange("b (i p) n -> p (b i) n", p=P)).then_inc(S("x_in"), 16)
            sp.dma_start(xin_d, a["x_sample"].rearrange("b t n -> (b t) n")).then_inc(S("x_in"), 16)
            sp.dma_start(pages[:, :], a["page_table"].rearrange("(o b) n -> o (b n)", o=1)).then_inc(S("page_in"), 16)
            for name, n in (("const_in", 1), ("x_in", 2), ("page_in", 1)):
                sp.wait_ge(S(name), 16 * n)

        def pe_first(pe, T):
            pe.wait_ge(S("const_in"), 16)
            pe.wait_ge(S("x_in"), 32)
            for c in range(KC):
                b = 2 * (c % 2)
                if c >= 2:
                    pe.wait_ge(S("x_rows_out"), c - 1)
                    pe.wait_ge(S("x_dec_out"), c - 1)
                for i in range(QT):
                    pe.transpose(ps[:, b, i * P:(i + 1) * P], xin[:, i, c * P:(c + 1) * P], ident)
                pe.transpose(ps[:, b + 1, 0:DEC], xin_d[:, c * P:(c + 1) * P], ident[0:DEC, 0:DEC])\
                    .then_inc(S("x_t"), 1)

        def act_first(act, T):
            for c in range(KC):
                act.wait_ge(S("x_t"), c + 1)
                act.activation(hT[:, c, 0:SEQ], ps[:, 2 * (c % 2), :], ACT.Copy).then_inc(S("x_rows_out"), 1)

        def dve_first(dve, T):
            for c in range(KC):
                dve.wait_ge(S("x_t"), c + 1)
                dve.tensor_copy(hT[:, c, SEQ:TOK], ps[:, 2 * (c % 2) + 1, 0:DEC]).then_inc(S("x_dec_out"), 1)

        def sp_vectors(sp, T, l):
            L = bass.ds(l, 1)

            def put(row, n, src, slot=0):
                sp.dma_start(vst[row:row + n, slot, :], src).then_inc(S("vec_in"), 16)

            put(V_NORM, 6 * KC, a["norms"][L].rearrange("a n (c p) -> (a n c) p", p=P))
            for g in range(2):
                sp.dma_start(vst[V_GRP:V_GRP + 4, 0, g * HD:(g + 1) * HD],
                               a["grp_norm"][L, g * 256:(g + 1) * 256].rearrange("a (t d) -> (a t) d", d=HD))\
                    .then_inc(S("vec_in"), 16)
            put(V_GRP + 4, 4, a["grp_norm"][L, 512:1024].rearrange("a (c p) -> (a c) p", p=P))
            for row, n, name in ((V_CB, 2, "conv_b"), (V_CLG, 2, "conv_ln_g"), (V_CLB, 2, "conv_ln_b"),
                                 (V_PWB, 2, "conv_pw_b"), (V_MU, 7, "rw_mu"), (V_W0, 2, "rw_w0"), (V_A0, 2, "rw_a0"),
                                 (V_KK, 2, "rw_kk"), (V_KA, 2, "rw_ka"), (V_LW, 2, "rw_ln_w"), (V_LB, 2, "rw_ln_b")):
                put(row, n, a[name][L].rearrange("a (c p) -> (a c) p", p=P))
            put(V_RK, 2, a["rw_rk"][L].rearrange("a (c h) d -> (a c) (h d)", c=2))
            put(0, 2 * CW, a["conv_w"][L].rearrange("a j (c p) -> (a j c) p", p=P), slot=1)

        def pe_vectors(pe, T):
            pe.wait_ge(S("vec_in"), 17 * 16)
            pe.transpose(ps[:, 0, 0:V_END], vst[0:V_END, 0, :], ident[0:V_END, 0:V_END])
            pe.transpose(ps[:, 0, V_CW:V_CW + 2 * CW], vst[0:2 * CW, 1, :], ident[0:2 * CW, 0:2 * CW])\
                .then_inc(S("vec_t"), 1)

        def dve_vectors(dve, T, link):
            dve.wait_ge(S("vec_t"), 1)
            link(dve.tensor_copy(vec[:, 0:V_END], ps[:, 0, 0:V_END]))
            link(dve.tensor_copy(vec[:, V_CW:V_CW + 2 * CW], ps[:, 0, V_CW:V_CW + 2 * CW]))
            for n in (1, 5):
                link(dve.tensor_scalar(vec[:, V_NORM + n * KC:V_NORM + (n + 1) * KC],
                                       vec[:, V_NORM + n * KC:V_NORM + (n + 1) * KC], 0.5, None, ALU.mult))

        def pe_last(pe, T):
            for i in range(QT + 1):
                m = P if i < QT else DEC
                if i >= 2:
                    pe.wait_ge(S("y_out"), 2 * i - 2)
                for n in range(2):
                    for c in range(4):
                        ins = pe.transpose(ps[0:m, 2 * (i % 2) + n, c * P:(c + 1) * P],
                                           hT[:, 4 * n + c, i * P:i * P + m], ident)
                    ins.then_inc(S("y_t"), 1)

        def act_last(act, T):
            for i in range(QT + 1):
                m = P if i < QT else DEC
                for n in range(2):
                    act.wait_ge(S("y_t"), 2 * i + n + 1)
                    act.activation(big[0:m, i * D + n * 512:i * D + (n + 1) * 512], ps[0:m, 2 * (i % 2) + n, :],
                                   ACT.Copy).then_inc(S("y_out"), 1)

        def sp_last(sp, T):
            for i in range(QT):
                sp.wait_ge(S("y_out"), 2 * i + 2)
                sp.dma_start(o["y_prompt"][0, i * P:(i + 1) * P, :], big[:, i * D:(i + 1) * D]).then_inc(S("y_st"), 16)
            sp.wait_ge(S("y_out"), 2 * QT + 2)
            sp.dma_start(o["y_sample"].rearrange("b t n -> (b t) n"), big[0:DEC, QT * D:(QT + 1) * D])\
                .then_inc(S("y_st"), 16)
            sp.wait_ge(S("y_st"), 16 * (QT + 1))

        CO = 6336
        uP = big[:, CO:CO + 1084].rearrange("p (t n) -> p t n", t=2)
        uD = big[:, CO + 1084:CO + 1580].rearrange("p (t b j) -> p t b j", t=2, b=DEC)
        cT = big[:, CO + 1580:CO + 2620].rearrange("p (t n) -> p t n", t=2)
        cst_in = big[0:120, CO + 2620:CO + 3132].rearrange("p (h n) -> p h n", h=2)
        pw = big[:, CO + 2620:CO + 3132].rearrange("p (h n) -> p h n", h=2)
        dtmp = big[:, CO + 3132:CO + 3628].rearrange("p (t b j) -> p t b j", t=2, b=DEC)
        cout = big[:, CO + 3628:CO + 4140]
        srow = big[:, CO + 4140:CO + 4140 + RWC]
        rope = big[:, CO + 3628:CO + 3628 + 2 * TOK].rearrange("p (s n) -> p s n", s=2)
        rtq = sq
        small = wks[:, 5632:6536]
        gates = wks[:, 6536:6656].rearrange("p (i n) -> p i n", n=3 * NQ)

        def sp_win_unit(sp, l, c):
            w = a["w_in"][bass.ds(l, 1)]
            u = U_IN + c
            if T_Q <= c < T_Q + 4:
                sp.wait_ge(S("lo_ready"), u - 3)
                for n in range(2):
                    col = n * 256 + (c - T_Q) * HD
                    sp.dma_start(nat[:, u % 4, :, n * HD:(n + 1) * HD],
                                 w[:, :, col:col + HD].rearrange("a (k p) n -> p (a k) n", p=P))\
                        .then_inc(S(f"nat_full{u % 4}"), 16)
                return
            if c < T_KC:
                col = COL_T + c * P
            elif c < T_RW:
                col = COL_ROWS + (*ROW_TILES, T_GT).index(c) * P
            else:
                col = COL_T + 512 + (c - T_RW) * P
            sp_unit(sp, u, w[:, :, col:col + P])

        def sp_project(sp, T, l):
            L = bass.ds(l, 1)
            for c in range(4):
                sp_win_unit(sp, l, c)
            sp.wait_ge(S("unit_done"), U_IN)
            for n in range(2):
                sp.dma_start(cst_in[:, n, :], a["state_conv"][L, 4 * n:4 * n + 4]
                             .rearrange("a b j n -> (a b j) n")).then_inc(S("conv_in"), 16)
            sp_pages(sp, l, ("cmp_k",), (page_k,), "kpage_in")
            for c in range(4, 6):
                sp_win_unit(sp, l, c)
            sp_compress_w(sp, T, l, 0)
            sp.dma_start(rope, a["rope"]).then_inc(S("rope_in"), 16)
            sp.wait_ge(S("conv_state_t"), 1)
            sp.dma_start(pw, a["conv_pw"][L].rearrange("a (k p) n -> p (a k) n", p=P)).then_inc(S("pw_in"), 16)
            for c in range(6, NPROJ):
                sp_win_unit(sp, l, c)
            sp.wait_ge(S("unit_done"), U_IN + NPROJ)
            sp.dma_start(shn, a["state_shift"][L].rearrange("a b n -> (a b) n")).then_inc(S("rw_in"), 16)
            for v in range(2):
                for g in range(2):
                    sp.dma_start(peN[:, v, g * HD:(g + 1) * HD], a["cmp_pe"][L, v].rearrange("a j d -> (a j) d"))\
                        .then_inc(S("pe_in"), 16)
            for name, r0, r1 in (("rw_w2", 0, 32), ("rw_a2", 32, 64), ("rw_g2", 64, 128)):
                sp.dma_start(lora[r0:r1, :], a[name][L].rearrange("a r n -> (a r) n")).then_inc(S("lora_w_in"), 16)
            sp_pages(sp, l, ("cmp_v",), (page_v,), "vpage_in")

        def pe_project(pe, T):
            pe.wait_ge(S("conv_in"), 32)
            for n in range(2):
                for t in range(2):
                    ins = pe.transpose(ps[:, 4, t * 240 + n * 120:t * 240 + n * 120 + 120],
                                       cst_in[:, n, t * P:(t + 1) * P], ident[0:120, 0:120])
            ins.then_inc(S("conv_state_t"), 1)

            def chunk(c, j=None, wait_x=None):
                pe.wait_ge(S("p_used"), count(c + 1, j))
                pe_unit(pe, U_IN + c, 2 * (c % 2), xnH, xnL, j=j, wait_x=wait_x)
            for c in range(4):
                chunk(c, wait_x=("xl_ready", KC) if c == 0 else None)
            with pe.Fori(1, 4) as j:
                for c in range(4):
                    chunk(c, j=j)
            for c in range(16, NPROJ):
                if c == 16:
                    pe_turn(pe, 0, 2)
                chunk(c)
                if c == 16:
                    pe_conv_mean(pe, T)
                elif c == 17:
                    pe_conv_var(pe, T)
                elif c >= 19:
                    pe_rows(pe, 2 * (c - 19), min(2 * (c - 18), QT + 1))
            pe_conv_pw(pe, T)
            pe_turn(pe, 2, 6)

        def pe_turn(pe, first, last):
            for n in range(first, last):
                b = 4 + 2 * n if n < 2 else 2 * (n % 2)
                if n == 0:
                    pe.wait_ge(S("p_used"), 2 + 10)
                    pe.wait_ge(S("conv_state_out"), 1)
                if n == 2:
                    pe.wait_ge(S("p_used"), 2 + NPROJ)
                if n >= 4:
                    pe.wait_ge(S("rot_used"), n - 1)
                mm_tokens(pe, b, cst[:, C_ROT:C_ROT + P], proj[:, ROT_TILES[n], :], True, True)\
                    .then_inc(S("rot_ready"), 1)

        def pe_rows(pe, first, last):
            for i in range(first, last):
                m = P if i < QT else DEC
                b = 4 + 2 * (i % 2)
                if i == 0:
                    pe.wait_ge(S("p_used"), 2 + T_VW + 1)
                    pe.wait_ge(S("qr_ready"), 2)
                    pe.wait_ge(S("croot"), 1)
                if i >= 2:
                    pe.wait_ge(S("r_used"), 2 * (i - 1))
                for n in range(6):
                    pe.transpose(ps[0:m, b + n // 4, n % 4 * P:(n % 4 + 1) * P], proj[:, ROW_TILES[n], i * P:i * P + m],
                                 ident)
                pe.transpose(ps[0:m, b + 1, 256:256 + 3 * NQ], proj[0:3 * NQ, T_GT, i * P:i * P + m],
                             ident[0:3 * NQ, 0:3 * NQ]).then_inc(S("r_ready"), 1)

        ROT_TILES = (T_KS, T_KW, T_Q, T_Q + 1, T_Q + 2, T_Q + 3)

        def act_project(act, T, link):
            for c in range(NPROJ):
                if c + 2 < NPROJ:
                    act_unit(act, U_IN + c + 2)
                act.wait_ge(S("unit_done"), U_IN + c + 1)
                act.activation(halves(proj[:, c, :]), pair(2 * (c % 2)), ACT.Copy).then_inc(S("p_used"), 1)
                if c == 3:
                    act.wait_ge(S("p_used"), 2 + 4)
                    act.activation(sg[:, :, :], proj[:, T_CG:T_CG + 2, :], ACT.Sigmoid).then_inc(S("cg_sig"), 1)
                elif c == 16:
                    act_conv_square(act, T, link)
                elif c == 17:
                    act_conv_root(act, T)
                elif c == 18:
                    act_conv_silu(act, T, link)
                elif c >= 19:
                    act_rows(act, 2 * (c - 19), min(2 * (c - 18), QT + 1))

        def dve_project_units(dve, first, last):
            for c in range(first, last):
                dve_unit(dve, U_IN + c + 2)

        def dve_project(dve, T, link):
            dve_project_units(dve, 15, 16)
            dve_rope(dve, T, link, 0, 2)
            dve_project_units(dve, 16, 17)
            dve_conv_centre(dve, T, link)
            dve_project_units(dve, 17, 18)
            dve_conv_scale(dve, T, link)
            dve_project_units(dve, 18, 20)
            dve_conv_bias(dve, T, link)
            dve_rope(dve, T, link, 2, 6)

        def act_rows(act, first, last):
            for i in range(first, last):
                m = P if i < QT else DEC
                b = 4 + 2 * (i % 2)
                act.wait_ge(S("r_ready"), i + 1)
                act.activation(rows[0:m, i, 0:512], ps[0:m, b, :], ACT.Copy).then_inc(S("r_used"), 1)
                act.activation(rows[0:m, i, 512:N_ROWS], ps[0:m, b + 1, 0:N_ROWS - 512], ACT.Copy)\
                    .then_inc(S("r_used"), 1)

        def dve_rope(dve, T, link, first, last):
            for n in range(first, last):
                t = ROT_TILES[n]
                if n == 0:
                    dve.wait_ge(S("rope_in"), 16)
                if n == 2:
                    dve.wait_ge(S("unit_done"), U_IN + NPROJ)
                b = 4 + 2 * n if n < 2 else 2 * (n % 2)
                dst = proj[:, t, :] if n < 2 else qrT[:, n - 2, :]
                dve.wait_ge(S("rot_ready"), n + 1)
                dve.wait_ge(S("x_cos"), n + 1)
                dve.tensor_tensor(halves(dst), pair(b), halves(rope[:, 1, :]), ALU.mult)\
                    .then_inc(S("rot_used"), 1)
                dve.wait_ge(S("rot_used"), n + 1)
                dve.tensor_tensor(dst, dst, rtq[:, n % 2, :], ALU.add).then_inc(S("qr_ready"), 1)
            dve.wait_ge(S("qr_ready"), last)

        def pool_rope(pool, T, link):
            pool.wait_ge(S("rope_in"), 16)
            pool.wait_ge(S("p_used"), 2 + 14)
            for n, t in enumerate(ROT_TILES):
                if n >= 2:
                    pool.wait_ge(S("qr_ready"), n - 1)
                pool.tensor_tensor(rtq[:, n % 2, :], proj[:, t, :], rope[:, 0, :], ALU.mult).then_inc(S("x_cos"), 1)

        def sp_rows_out(sp, T, l):
            L = bass.ds(l, 1)
            names = ("cmp_k", "cmp_v", "sel_k", "sel_v", "win_k", "win_v")
            sp.wait_ge(S("r_used"), 2 * (QT + 1))
            for n, name in enumerate(names):
                sp.dma_start(o[f"p_{name}"][L].rearrange("a b (i p) g d -> p (a b i) (g d)", p=P),
                             rows[:, 0:QT, n * P:(n + 1) * P]).then_inc(S("rows_st"), 16)
                if n < 4:
                    dst = o[f"s_{name}"][L].rearrange("a b t g d -> (a b t) (g d)")
                else:
                    dst = o[f"s_{name}"][L, :, PAST - 1].rearrange("a b g d -> (a b) (g d)")
                    src = a[f"cache_{name}"][L, :, 1:PAST].rearrange("a b t g d -> (a b) (t g d)")
                    sp.dma_start(o[f"s_{name}"][L, :, 0:PAST - 1].rearrange("a b t g d -> (a b) (t g d)"), src)\
                        .then_inc(S("rows_st"), 16)
                sp.dma_start(dst, rows[0:DEC, QT, n * P:(n + 1) * P]).then_inc(S("rows_st"), 16)

        def dve_conv(dve, T, link):
            dve.wait_ge(S("conv_state_t"), 1)
            dve.tensor_copy(uD[:, :, :, 0:CW - 1].rearrange("p t b j -> p (t b) j"),
                            ps[:, 4, 0:480].rearrange("p (x j) -> p x j", j=CW - 1)).then_inc(S("conv_state_out"), 1)
            link(dve.memset(uP[:, :, 0:CW - 1], 0.0))
            dve_project_units(dve, 0, 4)
            dve.wait_ge(S("cg_sig"), 1)
            link(dve.tensor_tensor(uP[:, :, CW - 1:CW - 1 + SEQ], proj[:, T_CV:T_CV + 2, 0:SEQ], sg[:, :, 0:SEQ],
                                   ALU.mult))
            dve.tensor_tensor(uD[:, :, :, CW - 1], proj[:, T_CV:T_CV + 2, SEQ:TOK], sg[:, :, SEQ:TOK], ALU.mult)\
                .then_inc(S("u_ready"), 1)
            dve.wait_ge(S("u_ready"), 1)
            dve.wait_ge(S("conv_state_out"), 1)
            base = T.at("dve_step")
            n = 0
            for j in range(CW):
                if j % 3 == 0:
                    dve_project_units(dve, 4 + j // 3, 5 + j // 3)
                for t in range(2):
                    w = vec[:, V_CW + 2 * j + t:V_CW + 2 * j + t + 1]
                    x = uP[:, t, j:j + SEQ]
                    if j == 0:
                        dve.tensor_scalar(cT[:, t, 0:SEQ], x, w, vec[:, V_CB + t:V_CB + t + 1], ALU.mult, ALU.add)\
                            .then_inc(S("dve_step"), 1)
                    else:
                        dve.wait_ge(S("dve_step"), base + n - 1)
                        dve.scalar_tensor_tensor(out=cT[:, t, 0:SEQ], in0=x, scalar=w, in1=cT[:, t, 0:SEQ],
                                                 op0=ALU.mult, op1=ALU.add).then_inc(S("dve_step"), 1)
                    n += 1
            dve.wait_ge(S("dve_step"), T.up("dve_step", n))
            taps = vec[:, V_CW:V_CW + 2 * CW].rearrange("p (j t) -> p t j", t=2).unsqueeze(2)\
                .broadcast_to((P, 2, DEC, CW))
            for t in range(2):
                link(dve.tensor_tensor(dtmp[:, t], uD[:, t], taps[:, t], ALU.mult))
                link(dve.tensor_reduce(cT[:, t, SEQ:TOK], dtmp[:, t], X, ALU.add))
                link(dve.tensor_scalar(cT[:, t, SEQ:TOK], cT[:, t, SEQ:TOK], vec[:, V_CB + t:V_CB + t + 1], None,
                                       ALU.add))
            dve.sem_inc(reach("conv_ready"), 1)

        def pe_conv_state(pe, T):
            pe.wait_ge(S("u_ready"), 1)
            pe.wait_ge(*stage("ob_ready"))
            pe.wait_ge(S("rot_used"), 6)
            for t in range(2):
                pe.transpose(ps[0:CW - 1, 6, t * P:(t + 1) * P], uP[:, t, SEQ:SEQ + CW - 1], ident)
                ins = pe.transpose(ps[0:DEC, 6, 256 + t * P:256 + (t + 1) * P], uD[:, t, :, CW - 1], ident)
            for t in range(7):
                pe.transpose(ps[0:DEC + 1, 7 if t < 4 else 0, (t % 4) * P:(t % 4 + 1) * P],
                             proj[:, T_RW + t, SEQ - 1:TOK], ident)
            pe.wait_ge(S("pe_in"), 64)
            for v in range(2):
                pe.transpose(ps[:, 0, 384 + v * CB:384 + (v + 1) * CB], peN[:, v, :], ident[0:CB, 0:CB])
            pe.wait_ge(S("rw_in"), 16)
            for c in range(7):
                ins = pe.transpose(ps[:, 0, 448 + c * DEC:448 + (c + 1) * DEC], shn[:, c * P:(c + 1) * P],
                                   ident[0:DEC, 0:DEC])
            ins.then_inc(S("state_t"), 1)

        def act_conv_state(act, T, link):
            act.wait_ge(S("state_t"), 1)
            act.activation(cout[0:CW - 1, 0:256], ps[0:CW - 1, 6, 0:256], ACT.Copy)
            act.activation(cout[0:DEC, 256:512], ps[0:DEC, 6, 256:512], ACT.Copy)
            act.activation(srow[0:DEC + 1, 0:512], ps[0:DEC + 1, 7, :], ACT.Copy)
            act.activation(peT, ps[:, 0, 384:384 + 2 * CB].rearrange("p (v j) -> p v j", v=2), ACT.Copy)
            act.activation(shT, ps[:, 0, 448:448 + 7 * DEC].rearrange("p (c b) -> p c b", c=7), ACT.Copy)
            link(act.activation(srow[0:DEC + 1, 512:RWC], ps[0:DEC + 1, 0, 0:RWC - 512], ACT.Copy))
            act.sem_inc(reach("state_rows"), 1)

        def sp_state_out(sp, T, l):
            L = bass.ds(l, 1)
            sp.wait_ge(*stage("state_rows"))
            for dst, src in ((o["p_conv"][L].rearrange("a b j n -> (a b j) n"), cout[0:CW - 1, 0:256]),
                             (o["s_conv"][L, :, CW - 2].rearrange("a b n -> (a b) n"), cout[0:DEC, 256:512]),
                             (o["p_shift"][L].rearrange("a b n -> (a b) n"), srow[0:1, :]),
                             (o["s_shift"][L].rearrange("a b n -> (a b) n"), srow[1:DEC + 1, :]),
                             (o["s_conv"][L, :, 0:CW - 2].rearrange("a b j n -> (a b) (j n)"),
                              a["state_conv"][L, :, 1:CW - 1].rearrange("a b j n -> (a b) (j n)"))):
                sp.dma_start(dst, src).then_inc(S("state_st"), 16)

        def dve_conv_centre(dve, T, link):
            dve.wait_ge(S("cmean"), 1)
            for t in range(2):
                ins = dve.scalar_tensor_tensor(out=halves(cT[:, t, :]), in0=pair(4), scalar=-1 / 256,
                                               in1=halves(cT[:, t, :]), op0=ALU.mult, op1=ALU.add)
            link(ins)
            dve.sem_inc(reach("c_centered"), 1)

        def dve_conv_scale(dve, T, link):
            dve.wait_ge(S("croot"), 1)
            link(dve.reciprocal(rstd[:, :], rstd[:, :]))
            for t in range(2):
                link(dve.scalar_tensor_tensor(out=cT[:, t, :], in0=cT[:, t, :],
                                              scalar=vec[:, V_CLG + t:V_CLG + t + 1], in1=rstd[:, :],
                                              op0=ALU.mult, op1=ALU.mult))
            dve.sem_inc(reach("c_scaled"), 1)

        def dve_conv_bias(dve, T, link):
            dve.wait_ge(S("pw_ready"), 1)
            for t in range(2):
                ins = dve.tensor_scalar(halves(cT[:, t, :]), pair(4 + 2 * t), vec[:, V_PWB + t:V_PWB + t + 1], None,
                                        ALU.add)
            link(ins)
            dve.sem_inc(reach("ob_ready"), 1)

        def dve_conv_merge(dve, T, link):
            dve.wait_ge(S("croot"), 2)
            link(dve.reciprocal(rstd[:, :], rstd[:, :]))
            for t in range(2):
                ins = dve.scalar_tensor_tensor(out=merged[:, 4 + t, :], in0=cT[:, t, :],
                                               scalar=vec[:, V_GRP + 4 + t:V_GRP + 5 + t], in1=rstd[:, :],
                                               op0=ALU.mult, op1=ALU.mult)
            link(ins)
            dve.sem_inc(reach("conv_done"), 1)

        def act_conv_square(act, T, link):
            act.wait_ge(*stage("c_centered"))
            link(act.activation(sg[:, :, :], cT[:, :, :], ACT.Square))
            act.sem_inc(S("csq"), 1)

        def act_conv_root(act, T):
            act.wait_ge(S("cvar"), 1)
            act.activation(halves(rstd[:, :]), pair(4), ACT.Sqrt, scale=1 / 256,
                           bias=cst[:, C_EPS + 1:C_EPS + 2]).then_inc(S("croot"), 1)

        def act_conv_silu(act, T, link):
            act.wait_ge(*stage("c_scaled"))
            for t in range(2):
                ins = act.activation(sg[:, t, :], cT[:, t, :], ACT.Silu, bias=vec[:, V_CLB + t:V_CLB + t + 1])
            link(ins)
            act.sem_inc(reach("c_act"), 1)

        def act_conv_sum(act, T, link):
            act.wait_ge(*stage("ob_ready"))
            link(act.activation(sg[:, :, :], cT[:, :, :], ACT.Square))
            act.sem_inc(S("csq"), 1)
            act.wait_ge(S("cvar"), 2)
            act.activation(halves(rstd[:, :]), pair(2), ACT.Sqrt, scale=1 / 256,
                           bias=cst[:, C_EPS:C_EPS + 1]).then_inc(S("croot"), 1)

        def pe_conv_mean(pe, T):
            pe.wait_ge(*stage("conv_ready"))
            pe.wait_ge(S("rot_used"), 1)
            for t in range(2):
                ins = mm_tokens(pe, 4, ones, cT[:, t, :], t == 0, t == 1)
            ins.then_inc(S("cmean"), 1)

        def pe_conv_var(pe, T):
            pe.wait_ge(S("csq"), 1)
            for t in range(2):
                ins = mm_tokens(pe, 4, ones, sg[:, t, :], t == 0, t == 1)
            ins.then_inc(S("cvar"), 1)

        def pe_conv_pw(pe, T):
            pe.wait_ge(S("pw_in"), 16)
            pe.wait_ge(*stage("c_act"))
            pe.wait_ge(S("r_used"), 2 * (QT + 1))
            for m in range(2):
                for t in range(2):
                    ins = mm_tokens(pe, 4 + 2 * m, pw[:, t, m * P:(m + 1) * P], sg[:, t, :], t == 0, t == 1)
            ins.then_inc(S("pw_ready"), 1)

        def pe_conv_sum(pe, T):
            pe.wait_ge(S("csq"), 2)
            for t in range(2):
                ins = mm_tokens(pe, 2, ones, sg[:, t, :], t == 0, t == 1)
            ins.then_inc(S("cvar"), 1)

        xc = wks[:, 0:XCOLS + CB]
        PT = wks[:, 2592:4640].rearrange("p (s g n) -> p s g n", s=2, g=2)
        kcmp = wks[:, 4640:4640 + NWIN]
        vcmp = wks[:, 4804:4804 + NWIN]
        vcr = wks[:, 0:P]
        vcd = wks[:, P:9 * P].rearrange("p (b n) -> p b n", b=DEC)
        qz = [wks[:, 1152 + 512 * n:1664 + 512 * n].rearrange("p (b m) -> p b m", b=DEC) for n in range(2)]
        wc = big[:, 0:CB * P].rearrange("p (l e) -> p l e", e=P)
        prob = big[:, 4096:6144].rearrange("p (s g n) -> p s g n", s=2, g=2)
        oacc = big[:, 0:QT * 512].rearrange("p (i n) -> p i n", n=512)
        kT = [proj[:, t, :] for t in (T_KS, T_KW)]
        qT = proj[:, T_Q:T_Q + 4, :]
        otmp = big[:, 3100:3612]
        page_k = big[:, 4096:6144].rearrange("p (x n) -> p x n", n=P)
        page_v = mid[:, 2080:4128].rearrange("p (x n) -> p x n", n=P)
        kpage = page_v
        kdT = big[:, 0:2048]
        vdn = page_k
        wkd = wks[:, 2592:4640].rearrange("p (x n) -> p x n", n=P)
        wvd = mix[:, T_Q * TOK:T_Q * TOK + 2048].rearrange("p (x n) -> p x n", n=P)
        dP = small[0:64, 0:264]
        dPT = small[:, 264:456].rearrange("p (n m) -> p n m", n=3)
        negm = small[:, 700:716]
        mx = small[:, 716:732]
        ssum = small[:, 464:560]
        coef = small[:, 560:568]
        osq = small[:, 568:572]
        gD = small[0:64, 572:575]
        dst_ = small[0:64, 576:580]
        cbias = small[:, 580:582]
        oD = small[:, 584:616].rearrange("p (t b) -> p t b", t=4)
        oD2 = small[:, 616:648].rearrange("p (t b) -> p t b", t=4)
        peT = wks[:, 4968:4968 + 2 * CB].rearrange("p (v j) -> p v j", v=2)
        peN = small[0:CB, 648:904].rearrange("p (v n) -> p v n", v=2)

        def sp_pages(sp, l, names, dsts, sem_name):
            for x in range(DEC * NPAGE):
                pg = sp.value_load(pages[0:1, x:x + 1], min_val=0, max_val=a[f"cache_{names[0]}"].shape[1] - 1)
                for name, dst in zip(names, dsts):
                    sp.dma_start(dst[:, x, :], a[f"cache_{name}"][bass.ds(l, 1), bass.ds(pg, 1)]
                                 .rearrange("a b t g d -> t (a b) (g d)").squeeze(1)).then_inc(S(sem_name), 16)

        def sp_compress_w(sp, T, l, v):
            if v == 0:
                sp.wait_ge(*stage("wc_zero"))
            else:
                sp.wait_ge(S("win_ready"), 1)
            for g in range(2):
                sp.dma_start(wc[g * HD:(g + 1) * HD, :, g * HD:(g + 1) * HD], a["cmp_w"][bass.ds(l, 1), v]
                             .rearrange("a (j d) e -> d (a j) e", d=HD)).then_inc(S("wc_in"), 16)

        def pool_compress_zero(pool, T, link):
            pool.wait_ge(S("unit_done"), U_IN)
            link(pool.memset(big[:, 0:CB * P], 0.0))
            pool.sem_inc(reach("wc_zero"), 1)

        def pool_compress(pool, T, link):
            pool.wait_ge(S("unit_done"), U_IN + NPROJ)
            for v in range(2):
                if v:
                    pool.wait_ge(S("win_ready"), v)
                pool.tensor_copy(xc[:, 0:SEQ], proj[:, T_KC + v, 0:SEQ]).then_inc(S("xc_p"), 1)
                if v == 0:
                    pool.wait_ge(*stage("state_rows"))
                pool.tensor_copy(xc[:, XCOLS:XCOLS + CB], peT[:, v, :]).then_inc(S("xc_p"), 1)

        XB = (0, 1, 6, 7)

        def pe_compress_t(pe, T, v):
            if v == 0:
                pe.wait_ge(S("kpage_in"), DEC * NPAGE * 16)
                pe.wait_ge(*stage("state_rows"))
            else:
                pe.wait_ge(S("vpage_in"), DEC * NPAGE * 16)
                pe.wait_ge(S("xc_a"), 1)
                pe.wait_ge(S("xc_d"), 1)
            for x in range(DEC * NPAGE):
                ins = pe.transpose(ps[:, XB[x // 4], x % 4 * P:(x % 4 + 1) * P], (page_k, page_v)[v][:, x, :], ident)
            ins.then_inc(S("xc_t"), 1)

        def pe_compress(pe, T, v):
            pe.wait_ge(S("wc_in"), 32 * (v + 1))
            pe.wait_ge(*stage("ob_ready"))
            pe.wait_ge(S("xc_p"), 2 * (v + 1))
            pe.wait_ge(S("xc_a"), v + 1)
            pe.wait_ge(S("xc_d"), v + 1)
            for j in range(CB):
                ins = pe.matmul(ps[:, 4 + v, 0:NWIN], wc[:, j, :], xc[:, j:j + CS * (NWIN - 1) + 1:CS],
                                start=j == 0, stop=j == CB - 1)
            ins.then_inc(S("win_ready"), 1)

        def act_compress(act, T, link, v):
            act.wait_ge(S("xc_t"), v + 1)
            if v:
                act.wait_ge(S("win_ready"), v)
            act.activation(xc[:, 512:3 * 512].rearrange("p (x n) -> p x n", x=2), ps[:, 0:2, :], ACT.Copy)\
                .then_inc(S("xc_a"), 1)

        def dve_compress_in(dve, T, v):
            dve.wait_ge(S("xc_t"), v + 1)
            if v:
                dve.wait_ge(S("win_ready"), v)
            dve.tensor_copy(xc[:, 3 * 512:5 * 512].rearrange("p (x n) -> p x n", x=2), ps[:, 6:8, :])\
                .then_inc(S("xc_d"), 1)

        def dve_compress(dve, T, link, v):
            dve.wait_ge(S("win_ready"), v + 1)
            link(dve.tensor_copy(cbias[:, v:v + 1], ps[:, 4 + v, NWIN - 1:NWIN]))
            link(dve.tensor_scalar((kcmp, vcmp)[v], ps[:, 4 + v, 0:NWIN], cbias[:, v:v + 1], None, ALU.add))
            dve.sem_inc(S("cmp_out"), 1)

        VB = (4, 5, 0)

        def pe_cmp_rows(pe, T):
            pe.wait_ge(S("cmp_out"), 2)
            pe.transpose(ps[0:NCMP, VB[0], 0:P], vcmp[:, 0:NCMP], ident)
            for b in range(DEC):
                o_ = P + b * P
                at = SEQ // CS + b * (PAST // CS)
                ins = pe.transpose(ps[0:NCMP_D, VB[o_ // 512], o_ % 512:o_ % 512 + P], vcmp[:, at:at + NCMP_D], ident)
            ins.then_inc(S("vc_t"), 1)

        def dve_cmp_rows(dve, T, link):
            dve.wait_ge(S("vc_t"), 1)
            dve.tensor_copy(vcr[0:NCMP, :], ps[0:NCMP, VB[0], 0:P])
            dve.tensor_copy(vcd[0:NCMP_D, 0:3, :], ps[0:NCMP_D, VB[0], P:512].rearrange("p (b n) -> p b n", b=3))
            dve.tensor_copy(vcd[0:NCMP_D, 3:7, :], ps[0:NCMP_D, VB[1], :].rearrange("p (b n) -> p b n", b=4))
            link(dve.tensor_copy(vcd[0:NCMP_D, 7, :], ps[0:NCMP_D, VB[2], 0:P]))
            dve.sem_inc(reach("vc_ready"), 1)
            dve.wait_ge(*stage("gates_ready"))

        def act_gates(act, T, link):
            act.wait_ge(S("r_used"), 2 * (QT + 1))
            act.activation(gates[:, 0:QT, :], rows[:, 0:QT, 768:792], ACT.Sigmoid)
            link(act.activation(gates[0:DEC, QT, :], rows[0:DEC, QT, 768:792], ACT.Sigmoid))
            act.sem_inc(reach("gates_ready"), 1)

        CMPB = 0

        def keys_of(i, br):
            return (NCMP, 1, NCMP) if br == CMPB else ((i + 1) * P, i + 1, P)

        def width_of(i, br):
            return P if br == CMPB else (128, 256, 512, 512)[i]

        UNITS = [(i, br, t) for i in range(QT) for br in range(3) for t in range(0, 4, 512 // width_of(i, br))]
        DONE = [max(n for n, v in enumerate(UNITS) if v[:2] == (k // 3, k % 3)) + 1 for k in range(3 * QT)]

        def heads_of(u):
            i, br, t0 = UNITS[u]
            w = width_of(i, br)
            return [(t0 + x, g, x * w) for x in range(512 // w) for g in range(2)]

        def pe_scores(pe, u):
            i, br, _ = UNITS[u]
            nk = keys_of(i, br)[0]
            q, k = (qT, kcmp) if br == CMPB else (qrT, kT[br - 1])
            if u >= 2:
                pe.wait_ge(S("p_exp"), u - 1)
            if u == 1:
                pe.wait_ge(S("kkroot"), 2)
            for t, g, c in heads_of(u):
                h = slice(g * HD, (g + 1) * HD)
                ins = pe.matmul(ps[:, 2 * (u % 2) + g, c:c + nk], q[h, t, i * P:(i + 1) * P], k[h, 0:nk],
                                start=True, stop=True)
            ins.then_inc(S("s_ready"), 1)

        def pe_prompt(pe, T):
            pe.wait_ge(*stage("vc_ready"))
            pe.wait_ge(S("qr_ready"), 6)
            pe_scores(pe, 0)
            pe_scores(pe, 1)
            for u, (i, br, t0) in enumerate(UNITS):
                nk, nt, kk = keys_of(i, br)
                pe.wait_ge(S("p_exp"), u + 1)
                if u:
                    pe.wait_ge(S("pt_a"), u)
                    pe.wait_ge(S("pt_d"), u)
                for t, g, c in heads_of(u):
                    for n in range(nt):
                        ins = pe.transpose(ps[0:kk, 4 + g, c + n * P:c + (n + 1) * P],
                                           prob[:, u % 2, g, c + n * P:c + n * P + kk], ident)
                ins.then_inc(S("pt_ready"), 1)
                if u + 2 < len(UNITS):
                    pe_scores(pe, u + 2)
                pe.wait_ge(S("pt_a"), u + 1)
                pe.wait_ge(S("pt_d"), u + 1)
                k = 3 * i + br
                if t0 == 0 and k >= 2:
                    pe.wait_ge(S("o_used"), k - 1)
                for t, g, c in heads_of(u):
                    h = 2 * t + g
                    for n in range(nt):
                        v = vcr[0:kk] if br == CMPB else rows[:, n, 384 if br == 1 else 640:][:, 0:P]
                        ins = pe.matmul(ps[:, 6 + k % 2, h * HD:(h + 1) * HD],
                                        PT[0:kk, u % 2, g, c + n * P:c + (n + 1) * P],
                                        v[:, g * HD:(g + 1) * HD], start=n == 0, stop=n == nt - 1)
                ins.then_inc(S("pv_ready"), 1)

        def act_exps(act, u):
            i, br, _ = UNITS[u]
            nk = keys_of(i, br)[0]
            act.wait_ge(S("nm_ready"), u + 1)
            if u >= 2:
                act.wait_ge(S("pt_ready"), u - 1)
            for t, g, c in heads_of(u):
                at = (i * 3 + br) * 8 + 2 * t + g
                n = 8 * (u % 2) + (g * 512 + c) // width_of(i, br)
                ins = act.activation(prob[:, u % 2, g, c:c + nk], ps[:, 2 * (u % 2) + g, c:c + nk], ACT.Exp,
                                     scale=SCALE, bias=negm[:, n:n + 1], accum_out=ssum[:, at:at + 1])
            ins.then_inc(S("p_exp"), 1)

        def turned(v, u):
            i, br, _ = UNITS[u]
            return v.rearrange("p (x w) -> p x w", w=width_of(i, br))[:, :, 0:keys_of(i, br)[1] * P]

        def act_prompt(act, T, link):
            act_exps(act, 0)
            for u, (i, br, _) in enumerate(UNITS):
                kk = keys_of(i, br)[2]
                if u + 1 < len(UNITS):
                    act_exps(act, u + 1)
                act.wait_ge(S("pt_ready"), u + 1)
                if u >= 2:
                    act.wait_ge(S("pv_ready"), u - 1)
                act.activation(turned(PT[0:kk, u % 2, 0, :], u), turned(ps[0:kk, 4, :], u), ACT.Copy)\
                    .then_inc(S("pt_a"), 1)

        def act_prompt_root(act, T, link):
            act.wait_ge(*stage("oacc_ready"))
            for i in range(QT):
                ins = act.activation(sg[:, 0, 0:512], oacc[:, i, :], ACT.Square, accum_out=osq[:, i:i + 1])
                link(ins)
            link(act.activation(osq, osq, ACT.Sqrt, scale=1 / 512, bias=cst[:, C_EPS:C_EPS + 1]))
            act.sem_inc(reach("oroot"), 1)

        def dve_softmax(dve, T, link, u):
            i, br, _ = UNITS[u]
            nk = keys_of(i, br)[0]
            w = width_of(i, br)
            b, m0 = 2 * (u % 2), 8 * (u % 2)
            dve.wait_ge(S("s_ready"), u + 1)
            scores = ps[:, b:b + 2, :].rearrange("p b (x w) -> p (b x) w", w=w)
            nh = 1024 // w
            if br == CMPB:
                s, m = scores[:, :, 0:nk], cst[:, C_CMPM + i * NCMP:C_CMPM + (i + 1) * NCMP]
            else:
                s, m = scores[:, :, i * P:nk], cst[:, C_CAUS:C_CAUS + P]
            link(dve.tensor_tensor(s, s, m.unsqueeze(1).broadcast_to((P, nh, m.shape[1])), ALU.add))
            link(dve.tensor_reduce(mx[:, m0:m0 + nh], scores[:, :, 0:nk], X, ALU.max))
            dve.tensor_scalar(negm[:, m0:m0 + nh], mx[:, m0:m0 + nh], 0.1 * NEG, -SCALE, ALU.max, ALU.mult)\
                .then_inc(S("nm_ready"), 1)

        def dve_combine(dve, T, link, k):
            i, br = k // 3, k % 3
            dve.wait_ge(S("pv_ready"), DONE[k])
            link(dve.tensor_scalar(coef, ssum[:, k * 8:k * 8 + 8], 1e-30, None, ALU.max))
            link(dve.reciprocal(coef, coef))
            c2 = coef.rearrange("p (t g) -> p t g", g=2)
            link(dve.tensor_tensor(c2, c2, gates[:, i, :].rearrange("p (g t r) -> p t g r", g=2, r=3)[:, :, :, br],
                                   ALU.mult))
            f = coef.unsqueeze(2).broadcast_to((P, NQ, HD))
            src = ps[:, 6 + k % 2, :].rearrange("p (h d) -> p h d", d=HD)
            dst = oacc[:, i, :] if br == 0 else otmp
            dve.tensor_tensor(dst.rearrange("p (h d) -> p h d", d=HD), src, f, ALU.mult).then_inc(S("o_used"), 1)
            dve.wait_ge(S("o_used"), k + 1)
            if br:
                link(dve.tensor_tensor(oacc[:, i, :], oacc[:, i, :], otmp, ALU.add))

        def dve_prompt(dve, T, link):
            dve_softmax(dve, T, link, 0)
            for u, (i, br, _) in enumerate(UNITS):
                kk = keys_of(i, br)[2]
                if u + 1 < len(UNITS):
                    dve_softmax(dve, T, link, u + 1)
                dve.wait_ge(S("pt_ready"), u + 1)
                if u >= 2:
                    dve.wait_ge(S("pv_ready"), u - 1)
                dve.tensor_copy(turned(PT[0:kk, u % 2, 1, :], u), turned(ps[0:kk, 5, :], u)).then_inc(S("pt_d"), 1)
                if u in DONE:
                    dve_combine(dve, T, link, DONE.index(u))
                if RW_KEY_UNIT <= u < RW_KEY_UNIT + RW_KEY_PARTS:
                    dve_rw_keys(dve, T, link, u - RW_KEY_UNIT)
            dve_combine(dve, T, link, 3 * QT - 1)
            dve.sem_inc(reach("oacc_ready"), 1)

        def dve_prompt_out(dve, T, link):
            dve.wait_ge(*stage("oroot"))
            link(dve.reciprocal(osq, osq))
            for i in range(QT):
                link(dve.tensor_scalar(oacc[:, i, :], oacc[:, i, :], osq[:, i:i + 1], None, ALU.mult))
            dve.sem_inc(reach("on_ready"), 1)
            for t in range(4):
                dve.wait_ge(S("ot_ready"), t + 1)
                dve.tensor_scalar(merged[:, t, 0:SEQ], ps[:, t, :], vec[:, V_GRP + t:V_GRP + t + 1], None, ALU.mult)\
                    .then_inc(S("om_ready"), 1)
            dve.wait_ge(S("om_ready"), 4)

        def pe_prompt_out(pe, T):
            pe.wait_ge(*stage("on_ready"))
            for t in range(4):
                for i in range(QT):
                    heads = oacc[:, i, t * P:(t + 1) * P]
                    ins = pe.transpose(ps[:, t, i * P:(i + 1) * P], heads, ident)
                ins.then_inc(S("ot_ready"), 1)

        def pool_qz(pool, T, link):
            pool.wait_ge(S("win_ready"), 2)
            pool.wait_ge(S("qr_ready"), 6)
            link(pool.memset(wks[:, 1152:2176], 0.0))
            for n, q in enumerate((qT, qrT)):
                for g in range(2):
                    h = slice(g * HD, (g + 1) * HD)
                    dst = wks[h, 1152 + 512 * n:1152 + 512 * n + 576].rearrange("p (b x) -> p b x", x=72)
                    link(pool.tensor_copy(dst[:, :, 4 * g:4 * g + 4], q[h, :, SEQ:TOK].rearrange("p t b -> p b t")))
            pool.sem_inc(reach("qz_ready"), 1)

        def sp_decode_in(sp, T, l):
            def window(kind, dst):
                for n in range(2):
                    sp.dma_start(dst[:, 8 * n:8 * n + 8], a[f"cache_win_{kind}"][bass.ds(l, 1), 4 * n:4 * n + 4]
                                 .rearrange("a b (n t) g d -> t (a b n) (g d)", t=P)).then_inc(S("wwin_in"), 16)

            sp.wait_ge(S("xc_t"), 2)
            sp_pages(sp, l, ("sel_k",), (kpage,), "skpage_in")

            sp.wait_ge(*stage("gates_ready"))
            sp.dma_start(gD, gates[0:DEC, QT, :]).then_inc(S("gD_in"), 16)
            sp.wait_ge(S("pt_ready"), len(UNITS))
            sp.wait_ge(*stage("qz_ready"))
            for m in range(2):
                sp.dma_start(sd[:, m * DEC:(m + 1) * DEC, :],
                             a["state_wkv"][bass.ds(l, 1), :, 2 * m:2 * m + 2]
                             .rearrange("a b q v k -> (q v) (a b) k")).then_inc(S("sd_in"), 16)
            sp_pages(sp, l, ("sel_v",), (vdn,), "svpage_in")
            sp.wait_ge(S("pv_ready"), len(UNITS))
            window("k", wkd)
            window("v", wvd)

        def pe_decode(pe, T):
            pe.wait_ge(*stage("qz_ready"))
            for br in range(3):
                n = br - 1
                if br == 1:
                    pe_prompt_out(pe, T)
                    pe.wait_ge(S("om_ready"), 4)
                if br:
                    if br == 1:
                        pe.wait_ge(S("skpage_in"), DEC * NPAGE * 16)
                    else:
                        pe.wait_ge(S("wwin_in"), 64)
                    for x in range(4):
                        if x >= 2 or br == 2:
                            pe.wait_ge(S("kd_out"), 4 * n + x - 1)
                        for y in range(4):
                            ins = pe.transpose(ps[:, x % 2, y * P:(y + 1) * P], (kpage, wkd)[n][:, 4 * x + y, :], ident)
                        ins.then_inc(S("kd_t"), 1)
                    pe.wait_ge(S("kd_out"), 4 * (n + 1))
                    for b in range(DEC):
                        pe.matmul(ps[0:64, 2, 0:PAST], qz[1][:, b, :], kdT[:, b * PAST:(b + 1) * PAST],
                                  start=b == 0, stop=b == DEC - 1, skip_group_check=True)
                    for b in range(DEC):
                        ins = pe.matmul(ps[0:64, 2, PAST:PAST + DEC], qz[1][:, b, :], kT[n][:, SEQ:TOK],
                                        start=False, stop=b == DEC - 1, skip_group_check=True)
                else:
                    for b in range(DEC):
                        at = SEQ // CS + b * (PAST // CS)
                        ins = pe.matmul(ps[0:64, 2, 0:NCMP_D], qz[0][:, b, :], kcmp[:, at:at + NCMP_D],
                                        start=b == 0, stop=b == DEC - 1)
                ins.then_inc(S("ds_ready"), 1)
                pe_rw_decode(pe, T, 2 * br)
                pe.wait_ge(S("dp_ready"), br + 1)
                if br:
                    for m in range(2):
                        pe.transpose(ps[:, 3, m * 64:(m + 1) * 64], dP[:, m * P:(m + 1) * P], ident[0:64, 0:64])
                    ins = pe.transpose(ps[0:DEC, 3, 128:192], dP[:, PAST:PAST + DEC], ident[0:64, 0:64])
                else:
                    ins = pe.transpose(ps[0:NCMP_D, 3, 0:64], dP[:, 0:NCMP_D], ident[0:64, 0:64])
                ins.then_inc(S("dpt_ready"), 1)
                if br < 2:
                    pe_rw_decode(pe, T, 2 * br + 1)
                pe.wait_ge(S("dpt_out"), br + 1)
                if br == 1:
                    pe.wait_ge(S("svpage_in"), DEC * NPAGE * 16)
                for b in range(DEC):
                    c = slice(b * NQ, (b + 1) * NQ)
                    for m in range(2 if br else 1):
                        v, w = ((vdn, wvd)[n][:, 2 * b + m, :], P) if br else (vcd[0:NCMP_D, b, :], NCMP_D)
                        ins = pe.matmul(ps[:, 7, c], v, dPT[0:w, m, c], start=br == 0 and b == 0,
                                        stop=False, skip_group_check=True)
                if br:
                    at = 384 if br == 1 else 640
                    ins = pe.matmul(ps[:, 7, 0:64], rows[0:DEC, QT, at:at + P], dPT[0:DEC, 2, :],
                                    start=False, stop=br == 2, skip_group_check=True)
                ins.then_inc(S("do_ready"), 1)
            pe.wait_ge(S("osq_ready"), 1)
            for t in range(4):
                ins = pe.matmul(ps[:, 6, 0:DEC], ones, oD2[:, t, :], start=t == 0, stop=t == 3)
            ins.then_inc(S("oss_ready"), 1)

        def act_decode(act, T, link):
            for br in range(3):
                if br == 1:
                    act_prompt_root(act, T, link)
                if br:
                    for x in range(4):
                        act.wait_ge(S("kd_t"), 4 * (br - 1) + x + 1)
                        if x == 0 and br == 2:
                            act.wait_ge(S("ds_ready"), 2)
                        act.activation(kdT[:, x * 512:(x + 1) * 512], ps[:, x % 2, :], ACT.Copy)\
                            .then_inc(S("kd_out"), 1)
                act.wait_ge(S("dm_ready"), br + 1)
                nk = PAST + DEC if br else NCMP_D
                link(act.activation(dP[:, 0:nk], ps[0:64, 2, 0:nk], ACT.Exp, scale=SCALE, bias=dst_[:, 1:2],
                                    accum_out=dst_[:, 2:3]))
                act.sem_inc(S("de_ready"), 1)
            act.wait_ge(*stage("oD_ready"))
            act.activation(oD2, oD, ACT.Square).then_inc(S("osq_ready"), 1)
            act.wait_ge(S("oss_ready"), 1)
            act.activation(small[:, 0:DEC], ps[:, 6, 0:DEC], ACT.Sqrt, scale=1 / 512, bias=cst[:, C_EPS:C_EPS + 1])\
                .then_inc(S("odroot"), 1)

        def dve_decode(dve, T, link):
            dve_rw_spread(dve, T, link, 0)
            for br in range(3):
                nk = PAST + DEC if br else NCMP_D
                if br == 1:
                    dve_prompt_out(dve, T, link)
                dve.wait_ge(S("ds_ready"), br + 1)
                if br:
                    s = ps[0:64, 2, PAST:PAST + DEC]
                    link(dve.tensor_tensor(s, s, cst[0:64, C_DMASK:C_DMASK + DEC], ALU.add))
                link(dve.tensor_reduce(dst_[:, 0:1], ps[0:64, 2, 0:nk], X, ALU.max))
                link(dve.tensor_scalar(dst_[:, 1:2], dst_[:, 0:1], -SCALE, None, ALU.mult))
                dve.sem_inc(S("dm_ready"), 1)
                dve_rw_decode(dve, T, link, 2 * br)
                if br == 0:
                    dve.wait_ge(S("gD_in"), 16)
                dve.wait_ge(S("de_ready"), br + 1)
                link(dve.reciprocal(dst_[:, 3:4], dst_[:, 2:3]))
                link(dve.tensor_tensor(dst_[:, 3:4], dst_[:, 3:4], gD[:, br:br + 1], ALU.mult))
                link(dve.tensor_scalar(dP[:, 0:nk], dP[:, 0:nk], dst_[:, 3:4], None, ALU.mult))
                dve.sem_inc(S("dp_ready"), 1)
                dve.wait_ge(S("dpt_ready"), br + 1)
                if br:
                    dve.tensor_copy(dPT[:, 0:2, :], ps[:, 3, 0:128].rearrange("p (n m) -> p n m", n=2))
                    link(dve.tensor_copy(dPT[0:DEC, 2, :], ps[0:DEC, 3, 128:192]))
                else:
                    link(dve.tensor_copy(dPT[0:NCMP_D, 0, :], ps[0:NCMP_D, 3, 0:64]))
                dve.sem_inc(S("dpt_out"), 1)
                if br < 2:
                    dve_rw_decode(dve, T, link, 2 * br + 1)
            dve.wait_ge(S("do_ready"), 3)
            for g in range(2):
                h = slice(g * HD, (g + 1) * HD)
                ins = dve.tensor_copy(oD[h], ps[h, 7, 0:64].rearrange("p (b x) -> p x b", x=NQ)[:, 4 * g:4 * g + 4])
                link(ins)
            dve.sem_inc(reach("oD_ready"), 1)
            dve.wait_ge(S("odroot"), 1)
            link(dve.reciprocal(small[:, 0:DEC], small[:, 0:DEC]))
            for t in range(4):
                ins = dve.scalar_tensor_tensor(out=merged[:, t, SEQ:TOK], in0=oD[:, t, :],
                                               scalar=vec[:, V_GRP + t:V_GRP + t + 1], in1=small[:, 0:DEC],
                                               op0=ALU.mult, op1=ALU.mult)
                link(ins)
            dve.sem_inc(reach("attn_done"), 1)

        rw = proj[:, T_RW:NPROJ, :]
        xm = proj[:, 0:7, :]
        wdec, aa, gate, nkk, bb = (big[:, 6144 + 1040 * n:6144 + 1040 * (n + 1)].rearrange("p (m t) -> p m t", m=2)
                                   for n in range(5))
        tt = wks[:, 6656:7696].rearrange("p (m t) -> p m t", m=2)
        ar = wks[:, 0:2048].rearrange("p (m c s t) -> p m c s t", m=2, c=NCH, s=2)
        bt = wks[:, 2048:3072].rearrange("p (m c t) -> p m c t", m=2, c=NCH)
        kt = wks[:, 3072:4096].rearrange("p (m c t) -> p m c t", m=2, c=NCH)
        pp = aa
        bh = big[:, 0:1024].rearrange("p (m c t) -> p m c t", m=2, c=NCH)
        kh = big[:, 1024:2048].rearrange("p (m c t) -> p m c t", m=2, c=NCH)
        wu = big[:, 2048:3072].rearrange("p (c s n) -> p c s n", c=NCH, s=2)
        gT = big[:, 3072:3584].rearrange("p (c n) -> p c n", c=NCH)
        hh = big[:, 3584:4096].rearrange("p (c n) -> p c n", c=NCH)
        rwt = big[:, 4096:4608].rearrange("p (c n) -> p c n", c=NCH)
        st = big[:, 4608:5184].rearrange("p (c n) -> p c n", c=NCH + 1)
        swk = wks[0:64, 5184:5312]
        lora = wks[:, 7696:7952]
        tok = mix[:, 7 * TOK:7 * TOK + 4096]
        bst, kst, vst_ = (tok[:, 1024 * n:1024 * (n + 1)].rearrange("p (m c n) -> p m c n", m=2, c=NCH)
                          for n in range(3))
        ag = tok[:, 3072:4096].rearrange("p (c s n) -> p c s n", c=NCH, s=2)
        mats = fT[:, 0:4096].rearrange("p (k c n) -> p k c n", k=4, c=NCH)
        inv = proj[:, T_RW:NPROJ, :].rearrange("p c t -> p (c t)")
        xi, xT, yy = (inv[:, 1024 * n:1024 * (n + 1)].rearrange("p (c n) -> p c n", c=NCH) for n in range(3))
        oT = mid[:, 0:2 * TOK].rearrange("p (m t) -> p m t", m=2)
        sd = mid[:, 2 * TOK:2 * TOK + 1024].rearrange("p (x k) -> p x k", k=HD)
        zz = big[:, 2048:3072].rearrange("p (x k) -> p x k", k=HD)
        zt = big[:, 3072:4096].rearrange("p (x k) -> p x k", k=HD)
        shn = wks[0:DEC, 6656:6656 + RWC]
        shT = wks[:, 7952:8008].rearrange("p (c b) -> p c b", c=7)
        sk = wks[:, 8008:8024]
        pend = wks[:, 8024:8040].rearrange("p (m c) -> p m c", m=2)
        i2 = wks[:, 8040:8104]

        def levels(n):
            return cst[:, C_LVL + n * P:C_LVL + (n + 1) * P]

        def bc4(v, n):
            return v.unsqueeze(1).broadcast_to((P, n, v.shape[1]))

        def sp_rwkv(sp, T, l):
            L = bass.ds(l, 1)
            sp.wait_ge(S("rows_st"), 16 * 14)
            sp.wait_ge(S("state_st"), 16 * 5)
            sp.wait_ge(*stage("sd_new"))
            for m in range(2):
                sp.dma_start(o["s_wkv"][L, :, 2 * m:2 * m + 2].rearrange("a b q v k -> (q v) (a b) k"),
                             sd[:, m * DEC:(m + 1) * DEC, :]).then_inc(S("wkv_st"), 16)
            for m in range(2):
                sp.wait_ge(S("swk_ready"), m + 1)
                sp.dma_start(o["p_wkv"][L, :, 2 * m:2 * m + 2].rearrange("a b q v k -> v (a b q) k"),
                             swk.rearrange("p (q k) -> p q k", q=2)).then_inc(S("wkv_st"), 16)
                sp.wait_ge(S("wkv_st"), 32 + 16 * (m + 1))
                sp.sem_inc(S("swk_free"), 1)

        def pe_lora(pe, T, first, last):
            pe.wait_ge(S("lora_w_in"), 3 * 16)
            pe.wait_ge(*stage("lora_act"))
            pe.wait_ge(S("croot"), 2)
            pe.wait_ge(S("xc_d"), 2)
            for x in range(first, last):
                m, (r0, r1) = x // 3, ((0, 32), (32, 64), (64, 128))[x % 3]
                if x >= 2:
                    pe.wait_ge(S("lora_out"), x - 1)
                for h in range(2):
                    ins = pe.matmul(ps[:, 2 + 4 * (x % 2) + h, 0:HALF], lora[r0:r1, m * P:(m + 1) * P],
                                    xm[r0:r1, 6, h * HALF:(h + 1) * HALF], start=True, stop=True)
                ins.then_inc(S("lora_mm"), 1)

        def pe_kk_norm(pe, T):
            for m in range(2):
                pe.wait_ge(S("kksq"), m + 1)
                pe.wait_ge(S("lora_out"), 5 + m)
                mm_tokens(pe, 2 + 4 * m, bones, tt[:, m, :], True, True).then_inc(S("kkss"), 1)

        def act_lora_in(act, T, link):
            act.wait_ge(*stage("lora_in"))
            act.activation(xm[0:32, 6, :], xm[0:32, 6, :], ACT.Tanh)
            link(act.activation(xm[64:128, 6, :], xm[64:128, 6, :], ACT.Sigmoid))
            act.sem_inc(reach("lora_act"), 1)

        def act_lora(act, T, link):
            act.wait_ge(*stage("conv_done"))
            for x in range(6):
                m = x // 3
                act.wait_ge(S("lora_mm"), x + 1)
                dst = halves((wdec, aa, gate)[x % 3][:, m, :])
                src = pair(2 + 4 * (x % 2))
                if x % 3 == 2:
                    act.activation(dst, src, ACT.Copy).then_inc(S("lora_out"), 1)
                else:
                    bias = (V_W0, V_A0)[x % 3] + m
                    act.activation(dst, src, ACT.Sigmoid, bias=vec[:, bias:bias + 1]).then_inc(S("lora_out"), 1)
            act.wait_ge(*stage("kk_raw"))
            for m in range(2):
                act.activation(tt[:, m, :], nkk[:, m, :], ACT.Square).then_inc(S("kksq"), 1)
            for m in range(2):
                act.wait_ge(S("kkss"), m + 1)
                act.activation(halves(tt[:, m, :]), pair(2 + 4 * m), ACT.Sqrt).then_inc(S("kkroot"), 1)
            act.wait_ge(S("lora_out"), 6)
            link(act.activation(wdec, wdec, ACT.Exp, scale=-float(np.exp(-0.5))))
            act.sem_inc(reach("w_ready"), 1)

        def dve_shift(dve, T, link, tiles):
            t = slice(*tiles)
            dve.tensor_tensor(xm[:, t, 1:SEQ], rw[:, t, 0:SEQ - 1], rw[:, t, 1:SEQ], ALU.subtract)
            dve.tensor_scalar(xm[:, t, 0], rw[:, t, 0], -1.0, None, ALU.mult)
            link(dve.tensor_tensor(xm[:, t, SEQ:TOK], shT[:, t], rw[:, t, SEQ:TOK], ALU.subtract))
            for c in range(*tiles):
                ins = dve.scalar_tensor_tensor(out=xm[:, c, :], in0=xm[:, c, :], scalar=vec[:, V_MU + c:V_MU + c + 1],
                                               in1=rw[:, c, :], op0=ALU.mult, op1=ALU.add)
            link(ins)

        def dve_shift_state(dve, T, link):
            link(dve.tensor_tensor(i2, ident[:, 0:HD], ident[:, HD:P], ALU.add))
            dve.wait_ge(*stage("state_rows"))

        def dve_kk(dve, T, link):
            dve.wait_ge(S("state_st"), 5 * 16)
            for m in range(2):
                ins = dve.tensor_scalar(nkk[:, m, :], xm[:, 2 + m, :], vec[:, V_KK + m:V_KK + m + 1], -1.0,
                                        ALU.mult, ALU.mult)
            link(ins)
            dve.sem_inc(reach("kk_raw"), 1)

        RW_KEY_UNIT, RW_KEY_PARTS = 4, 14

        def dve_rw_keys(dve, T, link, part):
            if part == 0:
                dve.wait_ge(S("lora_out"), 6)
            if part < 2:
                m = part
                link(dve.tensor_scalar(bb[:, m, :], aa[:, m, :], -1.0, vec[:, V_KA + m:V_KA + m + 1], ALU.add,
                                       ALU.mult))
                link(dve.scalar_tensor_tensor(out=xm[:, 2 + m, :], in0=bb[:, m, :], scalar=1.0, in1=xm[:, 2 + m, :],
                                              op0=ALU.add, op1=ALU.mult))
            elif part < 6:
                if part == 2:
                    dve.wait_ge(S("kkroot"), 2)
                h = tt[:, (part - 2) // 2, part % 2 * HALF:(part % 2 + 1) * HALF]
                link(dve.tensor_scalar(h, h, 1e-12, None, ALU.max))
                link(dve.reciprocal(h, h))
            elif part == 6:
                link(dve.tensor_tensor(nkk, nkk, tt, ALU.mult))
            elif part == 7:
                link(dve.scalar_tensor_tensor(out=bb, in0=nkk, scalar=-1.0, in1=aa, op0=ALU.mult, op1=ALU.mult))
                dve.wait_ge(*stage("w_ready"))
            elif part < 10:
                m = part - 8
                for c in range(NCH):
                    s = slice(c * CH, (c + 1) * CH)
                    ins = dve.tensor_tensor_scan(pp[:, m, s], wdec[:, m, s], wdec[:, m, s], 1.0, ALU.mult, ALU.bypass)
                link(ins)
                dve.tensor_copy(pend[:, m], pp[:, m, 0:SEQ].rearrange("p (c t) -> p c t", t=CH)[:, :, CH - 1])
            else:
                m, h = (part - 10) // 2, slice(part % 2 * SEQ // 2, (part % 2 + 1) * SEQ // 2)
                link(dve.reciprocal(tt[:, m, h], pp[:, m, h]))

        def pe_rw_decode(pe, T, n):
            pe.wait_ge(S("z_ready"), n + 1)
            for h in range(2):
                ins = pe.matmul(ps[:, 4 + h, :], bones, zz[:, 8 * h:8 * h + 8, :].rearrange("p x k -> p (x k)"),
                                start=True, stop=True)
            ins.then_inc(S("zb_ready"), 1)

        def dve_rw_spread(dve, T, link, n):
            v = (nkk, wdec, bb, xm[:, 2:4, :], xm[:, 0:2, :])[n][:, :, SEQ:TOK]
            for m in range(2):
                ins = dve.tensor_tensor(zz[:, m * DEC:(m + 1) * DEC, :],
                                        v[:, m].unsqueeze(2).broadcast_to((P, DEC, HD)),
                                        i2.unsqueeze(1).broadcast_to((P, DEC, HD)), ALU.mult)
            link(ins)
            dve.sem_inc(S("z_ready"), 1)

        def dve_rw_decode(dve, T, link, n):
            dve.wait_ge(S("zb_ready"), n + 1)
            z = ps[:, 4:6, :].rearrange("p h (x k) -> p (h x) k", k=HD)
            if n == 0:
                dve.wait_ge(S("sd_in"), 32)
                link(dve.tensor_tensor(zt, sd, z, ALU.mult))
                link(dve.tensor_reduce(sk, zt, X, ALU.add))
                dve.wait_ge(*stage("w_ready"))
            elif n == 1:
                link(dve.tensor_tensor(sd, sd, z, ALU.mult))
            elif n == 2:
                link(dve.tensor_tensor(zt, z, sk.unsqueeze(2).broadcast_to((P, 2 * DEC, HD)), ALU.mult))
                link(dve.tensor_tensor(sd, sd, zt, ALU.add))
            elif n == 3:
                for m in range(2):
                    ins = dve.tensor_tensor(zt[:, m * DEC:(m + 1) * DEC], z[:, m * DEC:(m + 1) * DEC],
                                            xm[:, 4 + m, SEQ:TOK].unsqueeze(2).broadcast_to((P, DEC, HD)), ALU.mult)
                link(ins)
                link(dve.tensor_tensor(sd, sd, zt, ALU.add))
                dve.sem_inc(reach("sd_new"), 1)
            else:
                link(dve.tensor_tensor(zt, sd, z, ALU.mult))
                for m in range(2):
                    link(dve.tensor_reduce(oT[:, m, SEQ:TOK], zt[:, m * DEC:(m + 1) * DEC], X, ALU.add))
            if n < 4:
                dve_rw_spread(dve, T, link, n + 1)

        def dve_rw_decay(dve, T, link):
            pc = pp[:, :, 0:SEQ].rearrange("p m (c t) -> p m c t", t=CH)
            for m in range(2):
                def ch(v):
                    return v[:, m, 0:SEQ].rearrange("p (c t) -> p c t", t=CH)
                dve.tensor_tensor(ar[:, m, :, 1, :], ch(xm[:, 0:2, :]), pc[:, m], ALU.mult)
                dve.tensor_tensor(ar[:, m, :, 0, 1:CH], ch(nkk)[:, :, 1:CH], pc[:, m, :, 0:CH - 1], ALU.mult)
                dve.tensor_copy(ar[:, m, :, 0, 0], ch(nkk)[:, :, 0])
                link(dve.tensor_tensor(bt[:, m], ch(bb), ch(tt), ALU.mult))
                link(dve.tensor_tensor(kt[:, m], ch(xm[:, 2:4, :]), ch(tt), ALU.mult))
                e = pend[:, m].unsqueeze(2).broadcast_to((P, NCH, CH))
                link(dve.tensor_tensor(bh[:, m], bt[:, m], e, ALU.mult))
                link(dve.tensor_tensor(kh[:, m], kt[:, m], e, ALU.mult))
                dve.sem_inc(S("decayed"), 1)

        def pe_rw_chunks(pe, T):
            for m in range(2):
                pe.wait_ge(S("decayed"), m + 1)
                if m:
                    pe.wait_ge(S("o_out"), 1)
                    pe.wait_ge(S("swk_ready"), 1)
                srcs = (bh[:, m], kh[:, m], xm[:, 4 + m, 0:SEQ].rearrange("p (c t) -> p c t", t=CH), ar[:, m, :, 0, :])
                for n, v in enumerate(srcs):
                    for c in range(NCH):
                        for g in range(2):
                            h = slice(g * HD, (g + 1) * HD)
                            ins = pe.matmul(ps[h, n, c * CH:(c + 1) * CH], v[h, c, :], ident[h, h], start=True,
                                            stop=True)
                    ins.then_inc(S("stack_t"), 1)
                for n, v in enumerate((bt, kt)):
                    for c in range(NCH):
                        for g in range(2):
                            h = slice(g * HD, (g + 1) * HD)
                            ins = pe.matmul(ps[h, 4 + 2 * n + c // 4, c % 4 * P:(c % 4 + 1) * P], v[h, m, c, :],
                                            ar[h, m, c].rearrange("p s t -> p (s t)"), start=True, stop=True)
                    ins.then_inc(S("mat_mm"), 1)
                for n in range(6):
                    for q in range(2):
                        if n == 0:
                            pe.wait_ge(S("mats_ready"), m + 1)
                            pe.wait_ge(S("stack_out"), 4 * (m + 1))
                        else:
                            pe.wait_ge(S("x_ready"), 12 * m + 2 * (n - 1) + q + 1)
                        for c in range(4 * q, 4 * q + 4):
                            ins = pe.matmul(ps[:, q, c % 4 * P:(c % 4 + 1) * P], mats[:, 0, c, :],
                                            ident if n == 0 else xi[:, c, :], start=True, stop=True)
                        ins.then_inc(S("y_mm"), 1)
                    if n == 0:
                        continue
                    for q in range(2):
                        pe.wait_ge(S("y_masked"), 12 * m + 2 * n + q + 1)
                        for c in range(4 * q, 4 * q + 4):
                            s = slice(c % 4 * P, (c % 4 + 1) * P)
                            pe.matmul(ps[:, 2 + q, s], xT[:, c, :], yy[:, c, :], start=True, stop=True)
                        for c in range(4 * q, 4 * q + 4):
                            s = slice(c % 4 * P, (c % 4 + 1) * P)
                            ins = pe.matmul(ps[:, 4 + q, s], yy[:, c, :], xT[:, c, :], start=True, stop=True)
                        ins.then_inc(S("dx_mm"), 1)
                for c in range(NCH):
                    ins = pe.matmul(ps[:, 6, c * CH:(c + 1) * CH], mats[:, 2, c, :], vst_[:, m, c, :],
                                    start=True, stop=True)
                ins.then_inc(S("akv_mm"), 1)
                pe.wait_ge(S("akv_out"), m + 1)
                pe.wait_ge(S("x_ready"), 12 * (m + 1))
                for c in range(NCH):
                    ins = pe.matmul(ps[:, c // 4, c % 4 * P:(c % 4 + 1) * P], xT[:, c, :],
                                    ag[:, c].rearrange("p s n -> p (s n)"), start=True, stop=True)
                ins.then_inc(S("wu_mm"), 1)
                pe.wait_ge(S("wu_out"), m + 1)
                for c in range(NCH):
                    for g in range(2):
                        h = slice(g * HD, (g + 1) * HD)
                        s = slice(c * CH, (c + 1) * CH)
                        pe.matmul(ps[h, 2, s], wu[h, c, 0, :], bst[h, m, c, :], start=True, stop=True)
                        pe.matmul(ps[h, 3, s], bst[h, m, c, :], wu[h, c, 1, :], start=True, stop=False)
                        pe.matmul(ps[h, 3, s], kst[h, m, c, :], vst_[h, m, c, :], start=False, stop=True)
                        ins = pe.matmul(ps[h, 4, s], wu[h, c, 0, :], mats[h, 1, c, g * CH:(g + 1) * CH],
                                        start=True, stop=True)
                ins.then_inc(S("trans_mm"), 1)
                for c in range(NCH):
                    pe.wait_ge(S("st_ready"), (NCH + 1) * m + c + 1)
                    for g in range(2):
                        h = slice(g * HD, (g + 1) * HD)
                        ins = pe.matmul(ps[h, 5, c * CH:(c + 1) * CH], gT[h, c, :], st[h, c, :], start=True, stop=True)
                    ins.then_inc(S("st_mm"), 1)
                    for g in range(2):
                        h = slice(g * HD, (g + 1) * HD)
                        s = slice(c * CH, (c + 1) * CH)
                        pe.matmul(ps[h, 7, s], st[h, c, :], rwt[h, c, :], start=True, stop=False)
                        pe.matmul(ps[h, 7, s], wu[h, c, 1, :], mats[h, 1, c, g * CH:(g + 1) * CH], start=False,
                                  stop=False)
                        ins = pe.matmul(ps[h, 7, s], vst_[h, m, c, :], mats[h, 3, c, g * CH:(g + 1) * CH],
                                        start=False, stop=True)
                ins.then_inc(S("o_mm"), 1)
                pe.wait_ge(S("st_ready"), (NCH + 1) * (m + 1))
                pe.transpose(ps[0:64, 6, 0:P], st[:, NCH, :], ident).then_inc(S("swk_t"), 1)

        def act_rw_chunks(act, T, link):
            for m in range(2):
                for n, dst in enumerate((bst[:, m], kst[:, m], vst_[:, m], ag[:, :, 0, :])):
                    act.wait_ge(S("stack_t"), 4 * m + n + 1)
                    act.activation(dst, ps[:, n, :].rearrange("p (c n) -> p c n", c=NCH), ACT.Copy)\
                        .then_inc(S("stack_out"), 1)
                act.wait_ge(S("akv_mm"), m + 1)
                act.activation(ag[:, :, 1, :], ps[:, 6, :].rearrange("p (c n) -> p c n", c=NCH), ACT.Copy)\
                    .then_inc(S("akv_out"), 1)
                act.wait_ge(S("wu_mm"), m + 1)
                act.activation(big[:, 2048:3072].rearrange("p (x n) -> p x n", x=2), ps[:, 0:2, :], ACT.Copy)\
                    .then_inc(S("wu_out"), 1)
                act.wait_ge(S("trans_mm"), m + 1)
                act.activation(hh, ps[:, 3, :].rearrange("p (c n) -> p c n", c=NCH), ACT.Copy)\
                    .then_inc(S("hh_out"), 1)
                act.wait_ge(S("o_mm"), m + 1)
                act.activation(oT[:, m, 0:SEQ], ps[:, 7, :], ACT.Copy).then_inc(S("o_out"), 1)
                act.wait_ge(S("swk_t"), m + 1)
                if m:
                    act.wait_ge(S("swk_free"), m)
                act.activation(swk, ps[0:64, 6, 0:P], ACT.Copy).then_inc(S("swk_ready"), 1)

        def pool_rwkv(pool, T, link):
            pool.wait_ge(*stage("attn_done"))
            pool.wait_ge(S("rows_st"), 16 * 14)
            link(pool.memset(fT[:, 0:4096], 0.0))
            pool.sem_inc(reach("mats_zero"), 1)

        def dve_bonus_in(dve, T, link):
            link(dve.tensor_tensor(bb, xm[:, 0:2, :], xm[:, 2:4, :], ALU.mult))
            for n in range(2):
                ins = dve.tensor_scalar(bb[:, n, :], bb[:, n, :], vec[:, V_RK + n:V_RK + n + 1], None, ALU.mult)
            link(ins)
            dve.sem_inc(reach("bonus_in"), 1)

        def dve_rw_chunks(dve, T, link):
            dve.wait_ge(*stage("mats_zero"))
            masks = (cst[:, C_STR:C_STR + P], cst[:, C_INC:C_INC + P])
            for m in range(2):
                if m:
                    dve_bonus_in(dve, T, link)
                    dve.wait_ge(S("o_mm"), m)
                for n in range(2):
                    dve.wait_ge(S("mat_mm"), 2 * m + n + 1)
                    src = ps[:, 4 + 2 * n:6 + 2 * n, :].rearrange("p b (c s t) -> p (b c) s t", s=2, t=CH)
                    for s in range(2):
                        for g in range(2):
                            h = slice(g * HD, (g + 1) * HD)
                            mask = masks[s][h, g * CH:(g + 1) * CH].unsqueeze(1).broadcast_to((HD, NCH, CH))
                            ins = dve.tensor_tensor(mats[h, 2 * n + s, :, g * CH:(g + 1) * CH], src[h, :, s, :], mask,
                                                    ALU.mult)
                    link(ins)
                dve.sem_inc(S("mats_ready"), 1)
                for q in range(2):
                    c4 = slice(4 * q, 4 * q + 4)
                    link(dve.tensor_tensor(xT[:, c4], mats[:, 0, c4], bc4(cst[:, C_LT1:C_LT1 + P], 4), ALU.mult))
                    link(dve.tensor_tensor(xT[:, c4], xT[:, c4], bc4(ident, 4), ALU.add))
                for n in range(6):
                    for q in range(2):
                        c4 = slice(4 * q, 4 * q + 4)
                        y4 = ps[:, q, :].rearrange("p (c n) -> p c n", c=4)
                        dve.wait_ge(S("y_mm"), 12 * m + 2 * n + q + 1)
                        dve.tensor_tensor(yy[:, c4], y4, bc4(levels(n), 4), ALU.mult).then_inc(S("y_masked"), 1)
                        if n == 0:
                            dve.wait_ge(S("y_masked"), 12 * m + q + 1)
                            dve.tensor_tensor(xi[:, c4], yy[:, c4], bc4(ident, 4), ALU.add).then_inc(S("x_ready"), 1)
                    if n == 0:
                        continue
                    for q in range(2):
                        c4 = slice(4 * q, 4 * q + 4)
                        dve.wait_ge(S("dx_mm"), 10 * m + 2 * (n - 1) + q + 1)
                        dx = ps[:, 2 + q, :].rearrange("p (c n) -> p c n", c=4)
                        dxT = ps[:, 4 + q, :].rearrange("p (c n) -> p c n", c=4)
                        link(dve.tensor_tensor(xi[:, c4], xi[:, c4], dx, ALU.add))
                        dve.tensor_tensor(xT[:, c4], xT[:, c4], dxT, ALU.add).then_inc(S("x_ready"), 1)
                e = pend[:, m].unsqueeze(2).broadcast_to((P, NCH, HD))
                link(dve.tensor_tensor(gT, i2.unsqueeze(1).broadcast_to((P, NCH, HD)), e, ALU.mult))
                dve.wait_ge(S("trans_mm"), m + 1)
                link(dve.tensor_tensor(gT, gT, ps[:, 2, :].rearrange("p (c n) -> p c n", c=NCH), ALU.add))
                link(dve.tensor_tensor(rwt, ar[:, m, :, 1, :], ps[:, 4, :].rearrange("p (c n) -> p c n", c=NCH),
                                       ALU.add))
                dve.memset(st[:, 0, :], 0.0).then_inc(S("st_ready"), 1)
                dve.wait_ge(S("hh_out"), m + 1)
                for c in range(NCH):
                    dve.wait_ge(S("st_mm"), NCH * m + c + 1)
                    dve.tensor_tensor(st[:, c + 1, :], ps[:, 5, c * CH:(c + 1) * CH], hh[:, c, :], ALU.add)\
                        .then_inc(S("st_ready"), 1)
                dve.wait_ge(S("st_ready"), (NCH + 1) * (m + 1))

        def pe_rw_out(pe, T):
            pe.wait_ge(S("o_out"), 2)
            pe.wait_ge(S("swk_ready"), 2)
            for m in range(2):
                ins = mm_tokens(pe, 2 * m, bones, oT[:, m, :], True, True)
            ins.then_inc(S("gmean"), 1)
            pe.wait_ge(*stage("bonus_in"))
            for m in range(2):
                ins = mm_tokens(pe, 4 + 2 * m, bones, bb[:, m, :], True, True)
            ins.then_inc(S("bonus_mm"), 1)
            pe.wait_ge(S("gsq"), 1)
            for m in range(2):
                ins = mm_tokens(pe, 2 * m, bones, tt[:, m, :], True, True)
            ins.then_inc(S("gvar"), 1)
            pe.wait_ge(S("gsq"), 2)
            for m in range(2):
                ins = mm_tokens(pe, 4, ones, tt[:, m, :], m == 0, m == 1)
            ins.then_inc(S("gvar"), 1)

        def act_rw_out(act, T, link):
            act.wait_ge(*stage("g_centered"))
            link(act.activation(tt, oT, ACT.Square))
            act.sem_inc(S("gsq"), 1)
            act.wait_ge(S("gvar"), 1)
            for m in range(2):
                ins = act.activation(halves(nkk[:, m, :]), pair(2 * m), ACT.Sqrt, scale=1 / HD,
                                     bias=cst[:, C_EPS + 2:C_EPS + 3])
            link(ins)
            act.sem_inc(S("groot"), 1)
            act.wait_ge(*stage("oc_ready"))
            link(act.activation(tt, oT, ACT.Square))
            act.sem_inc(S("gsq"), 1)
            act.wait_ge(S("gvar"), 2)
            act.activation(halves(aa[:, 0, :]), pair(4), ACT.Sqrt, scale=1 / 256, bias=cst[:, C_EPS:C_EPS + 1])\
                .then_inc(S("groot"), 1)

        def dve_rw_out(dve, T, link):
            dve.wait_ge(S("gmean"), 1)
            for m in range(2):
                ins = dve.scalar_tensor_tensor(out=halves(oT[:, m, :]), in0=pair(2 * m), scalar=-1 / HD,
                                               in1=halves(oT[:, m, :]), op0=ALU.mult, op1=ALU.add)
            link(ins)
            dve.sem_inc(reach("g_centered"), 1)
            dve.wait_ge(S("bonus_mm"), 1)
            for m in range(2):
                ins = dve.tensor_tensor(halves(wdec[:, m, :]), pair(4 + 2 * m), halves(xm[:, 4 + m, :]), ALU.mult)
            link(ins)
            dve.wait_ge(S("groot"), 1)
            link(dve.reciprocal(nkk, nkk))
            link(dve.tensor_tensor(oT, oT, nkk, ALU.mult))
            for m in range(2):
                ins = dve.tensor_scalar(oT[:, m, :], oT[:, m, :], vec[:, V_LW + m:V_LW + m + 1],
                                        vec[:, V_LB + m:V_LB + m + 1], ALU.mult, ALU.add)
            link(ins)
            link(dve.tensor_tensor(oT, oT, wdec, ALU.add))
            link(dve.tensor_tensor(oT, oT, gate, ALU.mult))
            dve.sem_inc(reach("oc_ready"), 1)
            dve.wait_ge(S("groot"), 2)
            link(dve.reciprocal(aa[:, 0, :], aa[:, 0, :]))
            for m in range(2):
                link(dve.scalar_tensor_tensor(out=merged[:, 6 + m, :], in0=oT[:, m, :],
                                              scalar=vec[:, V_GRP + 6 + m:V_GRP + 7 + m], in1=aa[:, 0, :],
                                              op0=ALU.mult, op1=ALU.mult))
            dve.sem_inc(reach("merged_ready"), 1)

        OUT_UNITS = list(range(U_OUT, U_OUT + KC))

        def sp_wout(sp, T, l):
            sp.wait_ge(S("o_mm"), 2)
            w = a["w_out"][bass.ds(l, 1)]
            for m, u in enumerate(OUT_UNITS):
                sp.wait_ge(S("lo_ready"), u - 3)
                for g in range(2):
                    sp.dma_start(nat[g * HD:(g + 1) * HD, u % 4, 0:4, :],
                                 w[:, g * 256:(g + 1) * 256, m * P:(m + 1) * P]
                                 .rearrange("a (t d) n -> d (a t) n", d=HD)).then_inc(S(f"nat_full{u % 4}"), 16)
                sp.dma_start(nat[:, u % 4, 4:8, :], w[:, 512:1024, m * P:(m + 1) * P]
                             .rearrange("a (k p) n -> p (a k) n", p=P)).then_inc(S(f"nat_full{u % 4}"), 16)

        def act_merged_split(act, T):
            act.wait_ge(S("wkv_st"), 64)
            for u in OUT_UNITS[0:2]:
                act_unit(act, u)
            act.wait_ge(*stage("merged_ready"))
            for c in range(KC):
                act.activation(mH[:, c, :], merged[:, c, :], ACT.Copy).then_inc(S("mh_ready"), 1)

        def dve_merged_split(dve, T):
            for u in OUT_UNITS[0:2]:
                dve_unit(dve, u)
            for c in range(KC):
                dve.wait_ge(S("mh_ready"), c + 1)
                dve.tensor_tensor(mL[:, c, :], merged[:, c, :], mH[:, c, :].bitcast(F32), ALU.subtract)\
                    .then_inc(S("ml_ready"), 1)

        def pe_wout(pe, T):
            for m, u in enumerate(OUT_UNITS):
                pe.wait_ge(S("f_used"), T.up("f_used"))
                pe_unit(pe, u, 2 * (m % 2), mH, mL, wait_x=("ml_ready", 0) if m == 0 else None)
            pe_sumsq_out(pe, T)

        def sp_mixer(sp, T, l):
            sp_project(sp, T, l)
            sp_rows_out(sp, T, l)
            sp_compress_w(sp, T, l, 1)
            sp_state_out(sp, T, l)
            sp_decode_in(sp, T, l)
            sp_rwkv(sp, T, l)
            sp_wout(sp, T, l)

        def pe_mixer(pe, T):
            pe_project(pe, T)
            pe_conv_state(pe, T)
            pe_compress_t(pe, T, 0)
            pe_compress(pe, T, 0)
            pe_conv_sum(pe, T)
            pe_compress_t(pe, T, 1)
            pe_lora(pe, T, 0, 2)
            pe_compress(pe, T, 1)
            pe_lora(pe, T, 2, 6)
            pe_cmp_rows(pe, T)
            pe_kk_norm(pe, T)
            pe_prompt(pe, T)
            pe_decode(pe, T)
            pe_rw_chunks(pe, T)
            pe_rw_out(pe, T)
            pe_wout(pe, T)

        def act_mixer(act, T, link):
            act_project(act, T, link)
            act_conv_state(act, T, link)
            act_compress(act, T, link, 0)
            act_conv_sum(act, T, link)
            act_lora_in(act, T, link)
            act_compress(act, T, link, 1)
            act_gates(act, T, link)
            act_lora(act, T, link)
            act_prompt(act, T, link)
            act_decode(act, T, link)
            act_rw_chunks(act, T, link)
            act_rw_out(act, T, link)
            act_merged_split(act, T)
            act_out(act, T, OUT_UNITS, 1)

        def dve_mixer(dve, T, link):
            dve_conv(dve, T, link)
            dve_project(dve, T, link)
            dve_shift_state(dve, T, link)
            dve_compress_in(dve, T, 0)
            dve_shift(dve, T, link, (6, 7))
            dve.sem_inc(reach("lora_in"), 1)
            dve_shift(dve, T, link, (0, 4))
            dve_compress(dve, T, link, 0)
            dve_conv_merge(dve, T, link)
            dve_compress_in(dve, T, 1)
            dve_kk(dve, T, link)
            dve.wait_ge(S("xc_p"), 4)
            dve_shift(dve, T, link, (4, 6))
            dve_compress(dve, T, link, 1)
            dve_cmp_rows(dve, T, link)
            dve_prompt(dve, T, link)
            dve_decode(dve, T, link)
            dve_rw_decay(dve, T, link)
            dve_rw_chunks(dve, T, link)
            dve_rw_out(dve, T, link)
            dve_merged_split(dve, T)
            dve_out(dve, T, OUT_UNITS)

        def pool_mixer(pool, T, link):
            pool_compress_zero(pool, T, link)
            pool_rope(pool, T, link)
            pool_compress(pool, T, link)
            pool_qz(pool, T, link)
            pool_rwkv(pool, T, link)

        @block.sync
        def _(sp):
            T = Tally()
            sp_first(sp, T)
            with sp.Fori(0, DEPTH) as l:
                boundary(sp, l, T)
                sp_ffn(sp, T, l, 0)
                sp_mixer(sp, T, l)
                sp_ffn(sp, T, l, 1)
            sp_last(sp, T)

        @block.tensor
        def _(pe):
            T = Tally()
            pe_first(pe, T)
            with pe.Fori(0, DEPTH) as l:
                boundary(pe, l, T)
                pe_prenorm(pe, T)
                pe_vectors(pe, T)
                pe_ffn(pe, T, 0)
                pe_down(pe, T, 0)
                pe_prenorm(pe, T)
                pe_mixer(pe, T)
                pe_prenorm(pe, T)
                pe_ffn(pe, T, 1)
                pe_down(pe, T, 1)
                pe.wait_ge(S("h_ready"), 3 * KC // 2)
                pe.wait_ge(S("hd_ready"), 3 * KC // 2)
            pe_last(pe, T)

        @block.scalar
        def _(act):
            T = Tally()
            act_first(act, T)
            with act.Fori(0, DEPTH) as l:
                boundary(act, l, T)
                link = chain(act, "act_step", T)
                act.sem_inc(S("f_used"), 2)
                act.sem_inc(S("p_used"), 2)
                act_prenorm(act, T, 0)
                for u in range(2):
                    act_unit(act, u)
                act_xn_split(act, T)
                act_ffn(act, T, 0)
                act_out(act, T, [u for u, *_ in dn_units(0)], 3)
                act_prenorm(act, T, 1)
                act_xn_split(act, T)
                act_mixer(act, T, link)
                act_prenorm(act, T, 2)
                act_xn_split(act, T)
                act_ffn(act, T, 1)
                act_out(act, T, [u for u, *_ in dn_units(1)], 3)
            act_last(act, T)

        @block.vector
        def _(dve):
            T = Tally()
            dve_first(dve, T)
            with dve.Fori(0, DEPTH) as l:
                boundary(dve, l, T)
                link = chain(dve, "dve_step", T)
                dve.sem_inc(S("gu_used"), 2)
                for u in range(2):
                    dve_unit(dve, u)
                dve_prenorm(dve, T, 0, link)
                dve_ffn(dve, T, 0)
                dve_out(dve, T, [u for u, *_ in dn_units(0)])
                dve_postnorm(dve, T, 1)
                dve_prenorm(dve, T, 2)
                dve_mixer(dve, T, link)
                dve_postnorm(dve, T, 3)
                dve_prenorm(dve, T, 4)
                dve_ffn(dve, T, 1)
                dve_out(dve, T, [u for u, *_ in dn_units(1)])
                dve_postnorm(dve, T, 5)

        @block.gpsimd
        def _(pool):
            T = Tally()
            with pool.Fori(0, DEPTH) as l:
                boundary(pool, l, T)
                link = chain(pool, "pool_step", T)
                pool_sumsq(pool, T)
                pool_residual(pool, T)
                pool_mixer(pool, T, link)
                for _ in range(2):
                    pool_sumsq(pool, T)
                    pool_residual(pool, T)


_OUTS = [
    ("y_prompt", (1, SEQ, D)), ("y_sample", (DEC, 1, D)),
    *[(f"p_{n}", (DEPTH, 1, SEQ, NKV, HD)) for n in ("cmp_k", "cmp_v", "sel_k", "sel_v", "win_k", "win_v")],
    ("p_conv", (DEPTH, 1, CW - 1, 256)), ("p_shift", (DEPTH, 1, RWC)), ("p_wkv", (DEPTH, 1, 4, HD, HD)),
    *[(f"s_{n}", (DEPTH, DEC, 1, NKV, HD)) for n in ("cmp_k", "cmp_v", "sel_k", "sel_v")],
    *[(f"s_{n}", (DEPTH, DEC, PAST, NKV, HD)) for n in ("win_k", "win_v")],
    ("s_conv", (DEPTH, DEC, CW - 1, 256)), ("s_shift", (DEPTH, DEC, RWC)), ("s_wkv", (DEPTH, DEC, 4, HD, HD)),
]
def kernel(**inputs):
    import concourse.bacc as bacc
    from concourse.bass_utils import run_bass_kernel_spmd

    nc = bacc.Bacc("TRN2", target_bir_lowering=False, num_devices=1)
    const, rope = constants()
    arrays, a, o = {}, {}, {}
    for name, v in {**inputs, "const": const, "rope": rope}.items():
        v = np.ascontiguousarray(v)
        arrays[f"in_{name}"] = v
        a[name] = nc.dram_tensor(f"in_{name}", v.shape, mybir.dt.from_np(v.dtype), kind="ExternalInput").ap()
    for name, shape in _OUTS:
        o[name] = nc.dram_tensor(f"out_{name}", shape, F32, kind="ExternalOutput").ap()
    trunk(nc, a, o)
    r = run_bass_kernel_spmd(nc, [arrays], core_ids=[0])
    return tuple(r.results[0][f"out_{name}"] for name, _ in _OUTS)
```
